# Optimizing a Trainium2 kernel written in Bass

```python
import jax, jax.numpy as jnp
from jax import lax
import numpy as np

D_MODEL = 2048
BATCH = 1
SEQ = 512
DEPTH = 2

GRID_W = 64
CTX_LEN = 256
HEAD_DIM = 128
HALF_DIM = HEAD_DIM // 2
AXIS_FREQS = HEAD_DIM // 4
ROPE_THETA = 10000.0
N_HEADS_A = 8
N_KV_A = 2
N_HEADS_B = 8
N_KV_B = 2
G_A = N_HEADS_A // N_KV_A
G_B = N_HEADS_B // N_KV_B
Q_BLOCK = 128
WINDOW = 128
BAND = Q_BLOCK + 2 * WINDOW
ATTN_SCALE = HEAD_DIM ** -0.5
NEG_INF = -1e30
Q_W = (N_HEADS_A + N_HEADS_B) * HEAD_DIM
KV_A_W = N_KV_A * HEAD_DIM
KV_B_W = N_KV_B * HEAD_DIM
KV_W = 2 * KV_A_W + 2 * KV_B_W
ATTN_WIDTH = Q_W
EVEN_IN = Q_W + KV_W + ATTN_WIDTH
POOL_WIDTH = D_MODEL
POOL_SIZES = (2, 4, 8, 16)
N_POOL_GROUPS = len(POOL_SIZES)
POOL_GROUP = POOL_WIDTH // N_POOL_GROUPS
ODD_IN = 2 * POOL_WIDTH
EPS = 1e-6
N_EVEN = (DEPTH + 1) // 2
N_ODD = DEPTH // 2


def _rmsnorm(x, g):
    xf = x.astype(jnp.float32)
    y = xf * lax.rsqrt(jnp.mean(xf * xf, axis=-1, keepdims=True) + EPS)
    return (y * g.astype(jnp.float32)).astype(x.dtype)

def _modulation(cvec, w, b):
    m = jax.nn.silu(cvec) @ w + b
    m = m[..., None, :]
    return m[..., :D_MODEL], m[..., D_MODEL:2 * D_MODEL], m[..., 2 * D_MODEL:]

def _axial_rope(rows):
    row = jnp.broadcast_to(jnp.arange(rows)[:, None], (rows, GRID_W)).reshape(-1).astype(jnp.float32)
    col = jnp.broadcast_to(jnp.arange(GRID_W)[None, :], (rows, GRID_W)).reshape(-1).astype(jnp.float32)
    inv = ROPE_THETA ** (-jnp.arange(AXIS_FREQS, dtype=jnp.float32) / AXIS_FREQS)
    ang = jnp.concatenate([row[:, None] * inv, col[:, None] * inv], axis=-1)
    return jnp.cos(ang), jnp.sin(ang)

def _rope(x, cos, sin):
    shape = (cos.shape[0],) + (1,) * (x.ndim - 3) + (cos.shape[1],)
    cos = cos.reshape(shape)
    sin = sin.reshape(shape)
    xf = x.astype(jnp.float32)
    x1, x2 = xf[..., :HALF_DIM], xf[..., HALF_DIM:]
    return jnp.concatenate([x1 * cos - x2 * sin, x2 * cos + x1 * sin], axis=-1).astype(x.dtype)

def _split_kv(kv):
    B, L = kv.shape[:2]
    kA = kv[..., :KV_A_W].reshape(B, L, N_KV_A, HEAD_DIM)
    vA = kv[..., KV_A_W:2 * KV_A_W].reshape(B, L, N_KV_A, HEAD_DIM)
    kB = kv[..., 2 * KV_A_W:2 * KV_A_W + KV_B_W].reshape(B, L, N_KV_B, HEAD_DIM)
    vB = kv[..., 2 * KV_A_W + KV_B_W:].reshape(B, L, N_KV_B, HEAD_DIM)
    return kA, vA, kB, vB

def _split_q(q):
    B, L = q.shape[:2]
    q = q.reshape(B, L, N_HEADS_A + N_HEADS_B, HEAD_DIM)
    qA = q[:, :, :N_HEADS_A].reshape(B, L, N_KV_A, G_A, HEAD_DIM)
    qB = q[:, :, N_HEADS_A:].reshape(B, L, N_KV_B, G_B, HEAD_DIM)
    return qA, qB

def _dense_attention(q, k, v):
    B, L = q.shape[:2]
    nb = L // Q_BLOCK

    def block(n):
        qb = lax.dynamic_slice_in_dim(q, n * Q_BLOCK, Q_BLOCK, axis=1)
        s = jnp.einsum('bqkgd,bskd->bkgqs', qb, k).astype(jnp.float32) * ATTN_SCALE
        p = jax.nn.softmax(s, axis=-1).astype(v.dtype)
        return jnp.einsum('bkgqs,bskd->bqkgd', p, v)

    o = lax.map(block, jnp.arange(nb))
    return jnp.moveaxis(o, 0, 1).reshape(B, L, -1)

def _window_attention(q, k, v, kc, vc, sink):
    B, L, KV, G, _ = q.shape
    C = kc.shape[1]
    nb = L // Q_BLOCK
    pad = ((0, 0), (WINDOW, WINDOW), (0, 0), (0, 0))
    kp = jnp.pad(k, pad)
    vp = jnp.pad(v, pad)
    sink_l = sink.astype(jnp.float32).reshape(1, KV, G, 1, 1)

    def block(n):
        start = n * Q_BLOCK
        qb = lax.dynamic_slice_in_dim(q, start, Q_BLOCK, axis=1)
        kb = lax.dynamic_slice_in_dim(kp, start, BAND, axis=1)
        vb = lax.dynamic_slice_in_dim(vp, start, BAND, axis=1)
        qpos = start + jnp.arange(Q_BLOCK)
        kpos = start - WINDOW + jnp.arange(BAND)
        valid = (jnp.abs(kpos[None, :] - qpos[:, None]) <= WINDOW) & (kpos >= 0)[None, :] & (kpos < L)[None, :]
        s_band = jnp.einsum('bqkgd,bjkd->bkgqj', qb, kb).astype(jnp.float32) * ATTN_SCALE
        s_band = jnp.where(valid, s_band, NEG_INF)
        s_ctx = jnp.einsum('bqkgd,bckd->bkgqc', qb, kc).astype(jnp.float32) * ATTN_SCALE
        s_sink = jnp.broadcast_to(sink_l, s_ctx.shape[:-1] + (1,))
        p = jax.nn.softmax(jnp.concatenate([s_band, s_ctx, s_sink], axis=-1), axis=-1).astype(v.dtype)
        return (jnp.einsum('bkgqj,bjkd->bqkgd', p[..., :BAND], vb)
                + jnp.einsum('bkgqc,bckd->bqkgd', p[..., BAND:BAND + C], vc))

    o = lax.map(block, jnp.arange(nb))
    return jnp.moveaxis(o, 0, 1).reshape(B, L, -1)

def _ctx_attention(q, k, v, sink=None):
    B, C = q.shape[:2]
    s = jnp.einsum('bqkgd,bckd->bkgqc', q, k).astype(jnp.float32) * ATTN_SCALE
    if sink is not None:
        KV, G = q.shape[2], q.shape[3]
        s_sink = jnp.broadcast_to(sink.astype(jnp.float32).reshape(1, KV, G, 1, 1), s.shape[:-1] + (1,))
        p = jax.nn.softmax(jnp.concatenate([s, s_sink], axis=-1), axis=-1)[..., :C]
    else:
        p = jax.nn.softmax(s, axis=-1)
    return jnp.einsum('bkgqc,bckd->bqkgd', p.astype(v.dtype), v).reshape(B, C, -1)

def _attention_layer(x, ctx, cos, sin, c, c_ctx, mod_w, mod_b, pre_g, post_g, w_in, q_norm, k_norm, sink, w_out, need_ctx_out):
    shift, scale, gate = _modulation(c, mod_w, mod_b)
    shift_c, scale_c, gate_c = _modulation(c_ctx, mod_w, mod_b)
    h = _rmsnorm(x, pre_g) * (1 + scale) + shift
    hc = _rmsnorm(ctx, pre_g) * (1 + scale_c) + shift_c

    proj = h @ w_in
    qA, qB = _split_q(proj[..., :Q_W])
    kA, vA, kB, vB = _split_kv(proj[..., Q_W:Q_W + KV_W])
    z = proj[..., Q_W + KV_W:]

    kA_c, vA_c, kB_c, vB_c = _split_kv(hc @ w_in[:, Q_W:Q_W + KV_W])
    kA_c = _rmsnorm(kA_c, k_norm)

    qA = _rope(_rmsnorm(qA, q_norm), cos, sin)
    kA = _rope(_rmsnorm(kA, k_norm), cos, sin)
    outA = _dense_attention(qA, jnp.concatenate([kA, kA_c], axis=1), jnp.concatenate([vA, vA_c], axis=1))

    outB = _window_attention(_rope(qB, cos, sin), _rope(kB, cos, sin), vB, kB_c, vB_c, sink)

    y = jnp.concatenate([outA, outB], axis=-1) * jax.nn.silu(z)
    x = x + gate * _rmsnorm(y @ w_out, post_g)

    if need_ctx_out:
        qA_c, qB_c = _split_q(hc @ w_in[:, :Q_W])
        z_c = hc @ w_in[:, Q_W + KV_W:]
        oA_c = _ctx_attention(_rmsnorm(qA_c, q_norm), kA_c, vA_c)
        oB_c = _ctx_attention(qB_c, kB_c, vB_c, sink)
        yc = jnp.concatenate([oA_c, oB_c], axis=-1) * jax.nn.silu(z_c)
        ctx = ctx + gate_c * _rmsnorm(yc @ w_out, post_g)
    return x, ctx

def _multiscale_pool(u, pool_w, pool_scale):
    B, L, _ = u.shape
    uf = u.astype(jnp.float32)
    cs = jnp.concatenate([jnp.zeros_like(uf[:, :1]), lax.cumsum(uf, axis=1)], axis=1)
    t = jnp.arange(L)
    outs = []
    for g, w in enumerate(POOL_SIZES):
        lo = jnp.clip(t - w // 2, 0, L)
        hi = jnp.clip(t + w // 2, 0, L)
        csg = cs[..., g * POOL_GROUP:(g + 1) * POOL_GROUP]
        mean = (jnp.take(csg, hi, axis=1) - jnp.take(csg, lo, axis=1)) / (hi - lo).astype(jnp.float32)[:, None]
        outs.append(mean - uf[..., g * POOL_GROUP:(g + 1) * POOL_GROUP])
    pooled = jnp.stack(outs, axis=2).astype(u.dtype)
    mixed = jnp.einsum('blgc,gcd->blgd', pooled, pool_w).reshape(B, L, POOL_WIDTH)
    return mixed * pool_scale

def _pool_layer(x, ctx, c, c_ctx, mod_w, mod_b, pre_g, post_g, w_in, pool_w, pool_scale, w_out, need_ctx_out):
    shift, scale, gate = _modulation(c, mod_w, mod_b)
    h = _rmsnorm(x, pre_g) * (1 + scale) + shift
    proj = h @ w_in
    y = _multiscale_pool(proj[..., :POOL_WIDTH], pool_w, pool_scale) * jax.nn.silu(proj[..., POOL_WIDTH:])
    x = x + gate * _rmsnorm(y @ w_out, post_g)
    if need_ctx_out:
        shift_c, scale_c, gate_c = _modulation(c_ctx, mod_w, mod_b)
        hc = _rmsnorm(ctx, pre_g) * (1 + scale_c) + shift_c
        pc = hc @ w_in
        yc = _multiscale_pool(pc[..., :POOL_WIDTH], pool_w, pool_scale) * jax.nn.silu(pc[..., POOL_WIDTH:])
        ctx = ctx + gate_c * _rmsnorm(yc @ w_out, post_g)
    return x, ctx

def first_inputs(seed: int = 0) -> dict:
    key = jax.random.key(seed)
    ks = jax.random.split(key, 24)
    f32 = jnp.float32

    def nrm(k, shape, s):
        return jax.random.normal(k, shape, f32) * s

    return {
        'x': nrm(ks[0], (BATCH, SEQ, D_MODEL), 1.0),
        'c': nrm(ks[1], (BATCH, D_MODEL), 1.0),
        'ctx': nrm(ks[2], (BATCH, CTX_LEN, D_MODEL), 1.0),
        'c_ctx': nrm(ks[3], (D_MODEL,), 1.0),
        'ev_mod_w': nrm(ks[4], (N_EVEN, D_MODEL, 3 * D_MODEL), 0.5 * D_MODEL ** -0.5),
        'ev_mod_b': nrm(ks[5], (N_EVEN, 3 * D_MODEL), 0.02),
        'ev_pre_g': 1.0 + nrm(ks[6], (N_EVEN, D_MODEL), 0.05),
        'ev_post_g': 1.0 + nrm(ks[7], (N_EVEN, D_MODEL), 0.05),
        'ev_w_in': nrm(ks[8], (N_EVEN, D_MODEL, EVEN_IN), D_MODEL ** -0.5),
        'ev_q_norm': 1.0 + nrm(ks[9], (N_EVEN, HEAD_DIM), 0.05),
        'ev_k_norm': 1.0 + nrm(ks[10], (N_EVEN, HEAD_DIM), 0.05),
        'ev_sink': nrm(ks[11], (N_EVEN, N_HEADS_B), 0.5),
        'ev_w_out': nrm(ks[12], (N_EVEN, ATTN_WIDTH, D_MODEL), ATTN_WIDTH ** -0.5),
        'od_mod_w': nrm(ks[13], (N_ODD, D_MODEL, 3 * D_MODEL), 0.5 * D_MODEL ** -0.5),
        'od_mod_b': nrm(ks[14], (N_ODD, 3 * D_MODEL), 0.02),
        'od_pre_g': 1.0 + nrm(ks[15], (N_ODD, D_MODEL), 0.05),
        'od_post_g': 1.0 + nrm(ks[16], (N_ODD, D_MODEL), 0.05),
        'od_w_in': nrm(ks[17], (N_ODD, D_MODEL, ODD_IN), D_MODEL ** -0.5),
        'od_pool_w': nrm(ks[18], (N_ODD, N_POOL_GROUPS, POOL_GROUP, POOL_GROUP), POOL_GROUP ** -0.5),
        'od_pool_scale': 1.0 + nrm(ks[19], (N_ODD, POOL_WIDTH), 0.1),
        'od_w_out': nrm(ks[20], (N_ODD, POOL_WIDTH, D_MODEL), POOL_WIDTH ** -0.5),
    }

def first_block(x, c, ctx, c_ctx, ev_mod_w, ev_mod_b, ev_pre_g, ev_post_g, ev_w_in, ev_q_norm, ev_k_norm, ev_sink, ev_w_out,
              od_mod_w, od_mod_b, od_pre_g, od_post_g, od_w_in, od_pool_w, od_pool_scale, od_w_out):
    ROWS = x.shape[1] // GRID_W
    cos, sin = _axial_rope(ROWS)
    for i in range(DEPTH):
        need_ctx_out = any(j % 2 == 0 for j in range(i + 1, DEPTH))
        if i % 2 == 0:
            e = i // 2
            x, ctx = _attention_layer(x, ctx, cos, sin, c, c_ctx, ev_mod_w[e], ev_mod_b[e], ev_pre_g[e], ev_post_g[e],
                                      ev_w_in[e], ev_q_norm[e], ev_k_norm[e], ev_sink[e], ev_w_out[e], need_ctx_out)
        else:
            o = i // 2
            x, ctx = _pool_layer(x, ctx, c, c_ctx, od_mod_w[o], od_mod_b[o], od_pre_g[o], od_post_g[o],
                                 od_w_in[o], od_pool_w[o], od_pool_scale[o], od_w_out[o], need_ctx_out)
    return x


DEPTH_2 = 1

SB_HEADS = D_MODEL // (2 * HEAD_DIM)
RET_HEADS = D_MODEL // (2 * HEAD_DIM)
SB_WIDTH = SB_HEADS * HEAD_DIM
RET_WIDTH = RET_HEADS * HEAD_DIM
MIX_WIDTH = SB_WIDTH + RET_WIDTH
IN_WIDTH = 4 * SB_WIDTH + 4 * RET_WIDTH
RET_CHUNK = 128
ROPE_BASE = 10000.0


def rms_norm(x, gain):
    xf = x.astype(jnp.float32)
    y = xf * lax.rsqrt(jnp.mean(xf * xf, axis=-1, keepdims=True) + EPS)
    return (y * gain.astype(jnp.float32)).astype(x.dtype)

def split_heads(t, n_heads):
    b, s, _ = t.shape
    return t.reshape(b, s, n_heads, HEAD_DIM).transpose(0, 2, 1, 3)

def merge_heads(t):
    b, h, s, d = t.shape
    return t.transpose(0, 2, 1, 3).reshape(b, s, h * d)

def rotary(t):
    s, d = t.shape[2], t.shape[3]
    half = d // 2
    inv_freq = ROPE_BASE ** (-jnp.arange(half, dtype=jnp.float32) / half)
    ang = jnp.arange(s, dtype=jnp.float32)[:, None] * inv_freq[None, :]
    cos, sin = jnp.cos(ang), jnp.sin(ang)
    tf = t.astype(jnp.float32)
    t1, t2 = tf[..., :half], tf[..., half:]
    return jnp.concatenate([t1 * cos - t2 * sin, t1 * sin + t2 * cos], axis=-1)

def stick_breaking_attention(q, k, v):
    b, h, s, d = q.shape
    nb = s // Q_BLOCK
    qb = q.astype(jnp.float32).reshape(b, h, nb, Q_BLOCK, d).transpose(2, 0, 1, 3, 4)
    kf = k.astype(jnp.float32)
    vf = v.astype(jnp.float32)
    key_pos = jnp.arange(s)
    inv_sqrt_d = float(1.0 / np.sqrt(d))

    def one_block(args):
        q_blk, blk = args
        q_pos = blk * Q_BLOCK + jnp.arange(Q_BLOCK)
        z = jnp.einsum('bhqd,bhsd->bhqs', q_blk, kf) * inv_sqrt_d
        past = key_pos[None, :] < q_pos[:, None]
        log_not = jnp.where(past, jax.nn.log_sigmoid(-z), 0.0)
        later = lax.cumsum(log_not, axis=3, reverse=True) - log_not
        w = jnp.where(past, jnp.exp(jax.nn.log_sigmoid(z) + later), 0.0)
        return jnp.einsum('bhqs,bhsd->bhqd', w, vf)

    out = lax.map(one_block, (qb, jnp.arange(nb)))
    return out.transpose(1, 2, 0, 3, 4).reshape(b, h, s, d)

def chunkwise_retention(q, k, v):
    b, h, s, d = q.shape
    c = RET_CHUNK
    n = s // c
    log_gamma = jnp.log1p(-jnp.exp2(-5.0 - jnp.arange(h, dtype=jnp.float32)))
    idx = jnp.arange(c, dtype=jnp.float32)
    rel = idx[:, None] - idx[None, :]
    decay_in = jnp.where(rel[None] >= 0, jnp.exp(jnp.maximum(rel, 0.0)[None] * log_gamma[:, None, None]), 0.0)
    q_decay = jnp.exp((idx[None, :] + 1.0) * log_gamma[:, None])[..., None]
    k_decay = jnp.exp((c - 1.0 - idx[None, :]) * log_gamma[:, None])[..., None]
    chunk_decay = jnp.exp(c * log_gamma)[:, None, None]

    def chunks(t):
        return t.reshape(b, h, n, c, d).transpose(2, 0, 1, 3, 4)

    def step(state, inp):
        qc, kc, vc = inp
        inner = jnp.einsum('bhij,bhjd->bhid', jnp.einsum('bhid,bhjd->bhij', qc, kc) * decay_in, vc)
        cross = jnp.einsum('bhid,bhde->bhie', qc * q_decay, state)
        new_state = state * chunk_decay + jnp.einsum('bhjd,bhje->bhde', kc * k_decay, vc)
        return new_state, inner + cross

    state0 = jnp.zeros((b, h, d, d), jnp.float32)
    _, out = lax.scan(step, state0, (chunks(q), chunks(k), chunks(v)))
    return out.transpose(1, 2, 0, 3, 4).reshape(b, h, s, d)

def head_group_norm(o, gain):
    mu = jnp.mean(o, axis=-1, keepdims=True)
    var = jnp.mean(jnp.square(o - mu), axis=-1, keepdims=True)
    return merge_heads((o - mu) * lax.rsqrt(var + EPS)) * gain.astype(jnp.float32)

def second_inputs(seed: int = 0) -> dict:
    key = jax.random.key(seed)
    ks = jax.random.split(key, 10)
    f32 = jnp.float32
    x = jax.random.normal(ks[0], (BATCH, SEQ, D_MODEL), f32)
    c = jax.random.normal(ks[1], (BATCH, D_MODEL), f32)
    w_ada = jax.random.normal(ks[2], (DEPTH_2, D_MODEL, 3 * D_MODEL), f32) * D_MODEL ** -0.5
    b_ada = 0.02 * jax.random.normal(ks[3], (DEPTH_2, 3 * D_MODEL), f32)
    norm_gain = 1.0 + 0.02 * jax.random.normal(ks[4], (DEPTH_2, D_MODEL), f32)
    w_in = jax.random.normal(ks[5], (DEPTH_2, D_MODEL, IN_WIDTH), f32) * D_MODEL ** -0.5
    sb_q_gain = 1.0 + 0.02 * jax.random.normal(ks[6], (DEPTH_2, HEAD_DIM), f32)
    sb_k_gain = 1.0 + 0.02 * jax.random.normal(ks[7], (DEPTH_2, HEAD_DIM), f32)
    ret_norm_gain = 1.0 + 0.02 * jax.random.normal(ks[8], (DEPTH_2, RET_WIDTH), f32)
    w_out = jax.random.normal(ks[9], (DEPTH_2, MIX_WIDTH, D_MODEL), f32) * MIX_WIDTH ** -0.5
    return {"x": x, "c": c, "w_ada": w_ada, "b_ada": b_ada, "norm_gain": norm_gain,
            "w_in": w_in, "sb_q_gain": sb_q_gain, "sb_k_gain": sb_k_gain,
            "ret_norm_gain": ret_norm_gain, "w_out": w_out}

def second_block(x, c, w_ada, b_ada, norm_gain, w_in, sb_q_gain, sb_k_gain, ret_norm_gain, w_out):
    split_at = [SB_WIDTH * i for i in range(1, 5)] + [4 * SB_WIDTH + RET_WIDTH * i for i in range(1, 4)]
    for layer in range(DEPTH_2):
        mod = jax.nn.silu(c) @ w_ada[layer] + b_ada[layer]
        shift, scale, gate = jnp.split(mod, 3, axis=-1)
        h = rms_norm(x, norm_gain[layer]) * (1.0 + scale[:, None, :]) + shift[:, None, :]

        proj = h @ w_in[layer]
        q_sb, k_sb, v_sb, z_sb, q_r, k_r, v_r, z_r = jnp.split(proj, split_at, axis=-1)

        qa = rms_norm(split_heads(q_sb, SB_HEADS), sb_q_gain[layer])
        ka = rms_norm(split_heads(k_sb, SB_HEADS), sb_k_gain[layer])
        oa = merge_heads(stick_breaking_attention(qa, ka, split_heads(v_sb, SB_HEADS)))
        oa = oa * jax.nn.silu(z_sb.astype(jnp.float32))

        qr = rotary(split_heads(q_r, RET_HEADS))
        kr = rotary(split_heads(k_r, RET_HEADS)) * (HEAD_DIM ** -0.5)
        vr = split_heads(v_r, RET_HEADS).astype(jnp.float32)
        ob = head_group_norm(chunkwise_retention(qr, kr, vr), ret_norm_gain[layer])
        ob = ob * jax.nn.silu(z_r.astype(jnp.float32))

        y = jnp.concatenate([oa, ob], axis=-1).astype(x.dtype) @ w_out[layer]
        x = x + (gate[:, None, :] * y).astype(x.dtype)
    return x


def setup_inputs(seed=0):
    out = dict(first_inputs(seed))
    for name, value in second_inputs(seed + 1).items():
        if name != "x":
            out[name + "_2"] = value
    return out


def reference(
    x, c, ctx, c_ctx, ev_mod_w, ev_mod_b, ev_pre_g, ev_post_g, ev_w_in, ev_q_norm, ev_k_norm,
    ev_sink, ev_w_out, od_mod_w, od_mod_b, od_pre_g, od_post_g, od_w_in, od_pool_w,
    od_pool_scale, od_w_out, c_2, w_ada_2, b_ada_2, norm_gain_2, w_in_2, sb_q_gain_2,
    sb_k_gain_2, ret_norm_gain_2, w_out_2,
):
    x = first_block(
        x, c, ctx, c_ctx, ev_mod_w, ev_mod_b, ev_pre_g, ev_post_g, ev_w_in, ev_q_norm,
        ev_k_norm, ev_sink, ev_w_out, od_mod_w, od_mod_b, od_pre_g, od_post_g, od_w_in,
        od_pool_w, od_pool_scale, od_w_out,
    )
    return second_block(
        x, c_2, w_ada_2, b_ada_2, norm_gain_2, w_in_2, sb_q_gain_2, sb_k_gain_2,
        ret_norm_gain_2, w_out_2,
    )


_drawn_inputs = setup_inputs


def setup_inputs(seed=0):
    import zlib

    import numpy as np

    out = dict(_drawn_inputs(seed))
    spreads = {}
    factors = {'ev_pre_g': 2.772,
     'ev_post_g': 3.002,
     'ev_q_norm': 8.0,
     'ev_k_norm': 8.0,
     'ev_sink': 8.0,
     'od_post_g': 3.659,
     'norm_gain_2': 4.48,
     'sb_q_gain_2': 8.0,
     'sb_k_gain_2': 8.0,
     'ret_norm_gain_2': 8.0}
    for name, (base, spread) in spreads.items():
        noise = np.random.default_rng([zlib.crc32(name.encode()), seed]).standard_normal(out[name].shape)
        drawn = base * np.exp(spread * noise) if base else spread * noise
        out[name] = __import__('jax').numpy.asarray(drawn.astype(out[name].dtype))
    for name, factor in factors.items():
        out[name] = (out[name] * factor).astype(out[name].dtype)
    return out
```

```python
from contextlib import ExitStack

import concourse.bass as bass
from concourse import mybir

F32 = mybir.dt.float32
F32R = mybir.dt.float32r
ALU = mybir.AluOpType
ACT = mybir.ActivationFunctionType
AX_X = mybir.AxisListType.X

P = 128
D = 2048
KT = 16
SEQ = 512
CTX = 256
EPS = 1e-6
SCALE = 128.0 ** -0.5
NAT_LOG_EXP = 6

INPUTS = [
    "x", "c", "ctx", "c_ctx", "ev_mod_w", "ev_mod_b", "ev_pre_g", "ev_post_g", "ev_w_in", "ev_q_norm",
    "ev_k_norm", "ev_sink", "ev_w_out", "od_mod_w", "od_mod_b", "od_pre_g", "od_post_g", "od_w_in",
    "od_pool_w", "od_pool_scale", "od_w_out", "c_2", "w_ada_2", "b_ada_2", "norm_gain_2", "w_in_2",
    "sb_q_gain_2", "sb_k_gain_2", "ret_norm_gain_2", "w_out_2",
]
TABLES = ["t_sq", "t_mask", "t_sb", "t_rope_a", "t_rope_b", "t_rcnt", "t_decay"]


class Line:

    def __init__(self, sem):
        self.sem, self.n, self.ops = sem, 0, []

    def do(self, fn, after=(), sig=True):
        if sig:
            self.n += 1
        self.ops.append((fn, [m for m in after if m is not None], self.sem if sig else None, 1))
        return (self.sem, self.n) if sig else None

    def dma(self, out, in_, slot, after=()):
        slot.n += 16
        self.ops.append((lambda e: e.dma_start(out, in_), [m for m in after if m is not None], slot.sem, 16))
        return (slot.sem, slot.n)

    def emit(self, eng):
        seen = {}
        for fn, after, sem, by in self.ops:
            for s, v in after:
                if seen.get(s.name, 0) < v:
                    eng.wait_ge(s, v)
                    seen[s.name] = v
            ins = fn(eng)
            if sem is not None:
                ins.then_inc(sem, by)


class Slot:

    def __init__(self, sem):
        self.sem, self.n = sem, 0


def program(nc, T, out):
    with ExitStack() as ctx:
        build(nc, ctx, T, out)


def build(nc, ctx, T, out):
    base = nc.sbuf_base
    end = nc.sbuf_usable_end
    arena = ctx.enter_context(nc.sbuf_tensor("arena", [P, (end - base) // 4 - 64], F32))
    del arena
    top = [(base + 63) // 64 * 64]

    def place(name, shape, dt, at=None):
        size = 4
        for s in shape[1:]:
            size *= s
        if at is None:
            at = top[0]
            top[0] += (size + 31) // 32 * 32
            assert top[0] <= end - 32, (name, top[0], end)
        return nc.alloc_sbuf_tensor_at(name, list(shape), dt, offset=at), at

    def sem(name):
        return ctx.enter_context(nc.semaphore(name))

    def slot(name):
        return Slot(sem(name))

    HHI, _ = place("HHI", [P, KT, SEQ], F32R)
    HLO, _ = place("HLO", [P, KT, SEQ], F32R)
    Y, y0 = place("Y", [P, KT, SEQ], F32)
    CHI, _ = place("CHI", [P, KT, CTX], F32R, y0)
    CLO, _ = place("CLO", [P, KT, CTX], F32R, y0 + 16384)
    NR, NS = 3, 3
    RAW = [place(f"RAW{i}", [P, 4, 256], F32)[0] for i in range(NR)]
    WHI = [place(f"WHI{i}", [P, 4, 256], F32R)[0] for i in range(NS)]
    WLO = [place(f"WLO{i}", [P, 4, 256], F32R)[0] for i in range(NS)]
    MRAW = [place(f"MRAW{i}", [P, 4, 256], F32)[0] for i in range(2)]
    MACC, _ = place("MACC", [P, 256], F32)
    SQ2 = [place(f"SQ{i}", [P, SEQ], F32)[0] for i in range(2)]
    TM, _ = place("TM", [P, SEQ], F32)
    TY, _ = place("TY", [P, SEQ], F32)
    TT_, _ = place("TT", [P, SEQ], F32)
    IDN, _ = place("IDN", [P, P], F32)
    ONE, _ = place("ONE", [P, P], F32)
    CS, _ = place("CS", [P, SEQ], F32)
    SN, _ = place("SN", [P, SEQ], F32)
    MK, _ = place("MK", [P, 3, P], F32)
    COL, _ = place("COL", [P, 304], F32)
    MOD, _ = place("MOD", [P, 3, 48], F32)
    MODX, _ = place("MODX", [P, 32], F32)
    SC, _ = place("SC", [P, 48], F32)
    SM, _ = place("SM", [P, 64], F32)
    s0 = top[0]
    room = end - 32 - s0

    def scratch(name, shape, dt, off):
        size = 4
        for s in shape[1:]:
            size *= s
        assert off + size <= room, (name, off, size, room)
        return place(name, shape, dt, s0 + off)[0]

    K1 = 1024
    PR = [scratch(f"PR{i}", [P, P], F32, 46 * K1 - 1536 + i * 512) for i in range(3)]
    XN = [scratch(f"XN{i}", [P, D], F32, 16 * K1 + i * 8 * K1) for i in range(3)]
    CT = scratch("CT", [P, KT, CTX], F32, 0)
    KTA = scratch("KTA", [P, 4, 768], F32, 0)
    VV = scratch("VV", [P, 6, 512], F32, 12 * K1)
    PB = [scratch(f"PB{i}", [P, 768], F32, 24 * K1 + i * 3 * K1) for i in range(2)]
    PT = scratch("PT", [P, 6, SEQ], F32, 30 * K1)
    QT = scratch("QT", [P, SEQ], F32, 42 * K1)
    XR = scratch("XR", [P, KT, SEQ], F32, 0)
    UP = [scratch(f"UP{i}", [P, 4, 544], F32, i * 8704) for i in range(3)]
    PHI = scratch("PHI", [P, 4, SEQ], F32R, 26112)
    PLO = scratch("PLO", [P, 4, SEQ], F32R, 26112 + 8192)
    RC = scratch("RC", [P, SEQ], F32, 26112 + 16384)
    Q2 = [scratch(f"Q2{i}", [P, 2, SEQ], F32, i * 4 * K1) for i in range(2)]
    K2 = [scratch(f"K2{i}", [P, 2, SEQ], F32, 8 * K1 + i * 4 * K1) for i in range(2)]
    V2 = [scratch(f"V2{i}", [P, 4, 256], F32, 16 * K1 + i * 4 * K1) for i in range(2)]
    SP = scratch("SP", [P, 4, SEQ], F32, 24 * K1)
    LS = scratch("LS", [P, SEQ], F32, 32 * K1)
    WB = [scratch(f"WB{i}", [P, SEQ], F32, 34 * K1 + i * 2 * K1) for i in range(2)]
    DK = scratch("DK", [P, SEQ], F32, 38 * K1)
    TA = [scratch(f"TA{i}", [P, SEQ], F32, 40 * K1 + i * 2 * K1) for i in range(2)]
    LSB = scratch("LSB", [P, SEQ], F32, 44 * K1)

    def bank(name, n=512):
        return ctx.enter_context(nc.psum_tensor(name, [P, n], F32))

    G = [[bank("G0"), bank("G1")], [bank("G2"), bank("G3")]]
    S = bank("S", 1024)
    TB = bank("TB")
    OB = bank("OB")

    pe, act, dve, pool, sp = (Line(sem(n)) for n in ("s_pe", "s_act", "s_dve", "s_pool", "s_sp"))
    s_raw = [slot(f"s_raw{i}") for i in range(NR)]
    s_mraw = [slot(f"s_mraw{i}") for i in range(2)]
    s_par = slot("s_par")
    s_cst = slot("s_cst")
    s_xn = [slot(f"s_xn{i}") for i in range(3)]
    s_rope = slot("s_rope")
    s_tri = slot("s_tri")
    s_spill = slot("s_spill")
    s_back = slot("s_back")
    s_rc = slot("s_rc")
    s_dk = slot("s_dk")
    s_out = [slot(f"s_out{i}") for i in range(2)]
    XS = nc.dram_tensor("x_spill", [KT, P, SEQ], F32)

    def write_out():
        OUT = [HHI, HLO]
        XO, _ = place("XO", [P, 2, D], F32, s0)
        ofree = [None, None]
        tb2 = [TB, OB]
        tf = [tmp["tb"], tmp["ob"]]
        cnt = 0
        for i in range(4):
            r = i % 2
            for q in range(4):
                b = cnt % 2
                cnt += 1
                for j in range(4):
                    k = 4 * q + j
                    m = tr(tb2[b][:, j * P:(j + 1) * P], Y[:, k, i * P:(i + 1) * P], [y_marks[k], tf[b]], sig=j == 3)
                dst = XO[:, r, 512 * q:512 * q + 512]
                if b:
                    tf[b] = vcopy(dst, tb2[b][:, :], [m, ofree[r], y_marks[KT - 1]])
                else:
                    tf[b] = acopy(dst, tb2[b][:, :], [m, ofree[r], y_marks[KT - 1]])
            ofree[r] = pool.dma(out[0, i * P:(i + 1) * P, :], XO[:, r, :], s_out[r], [tf[0], tf[1]])
        last_out = ofree[1]

        with nc.Block() as block:
            @block.sync
            def _(eng):
                sp.emit(eng)

            @block.gpsimd
            def _(eng):
                pool.emit(eng)
                for s in s_out + s_raw + s_mraw:
                    eng.wait_ge(s.sem, s.n)
                eng.wait_ge(s_spill.sem, s_spill.n)

            @block.scalar
            def _(eng):
                act.emit(eng)

            @block.vector
            def _(eng):
                dve.emit(eng)

            @block.tensor
            def _(eng):
                pe.emit(eng)

    def mm(o, l, r, start, stop, after=(), sig=False):
        return pe.do(lambda e: e.matmul(o, l, r, start=start, stop=stop, skip_group_check=True), after, sig)

    def tr(o, i, after=(), sig=False):
        return pe.do(lambda e: e.transpose(o, i, IDN[:, :]), after, sig)

    def af(o, i, f, after=(), bias=0.0, scale=1.0, acc=None):
        if acc is None:
            return act.do(lambda e: e.activation(o, i, f, bias=bias, scale=scale), after)
        return act.do(lambda e: e.activation(o, i, f, bias=bias, scale=scale, accum_out=acc), after)

    def acopy(o, i, after=(), scale=1.0):
        return act.do(lambda e: e.activation(o, i, ACT.Copy, scale=scale), after)

    def tt(o, a, b, op, after=()):
        return dve.do(lambda e: e.tensor_tensor(o, a, b, op), after)

    def ts(o, a, s1, s2, op0, op1, after=()):
        if op1 is None:
            return dve.do(lambda e: e.tensor_scalar(o, a, s1, None, op0), after)
        return dve.do(lambda e: e.tensor_scalar(o, a, s1, s2, op0, op1), after)

    def stt(o, a, s, b, op0, op1, after=()):
        return dve.do(lambda e: e.scalar_tensor_tensor(out=o, in0=a, scalar=s, in1=b, op0=op0, op1=op1), after)

    def vcopy(o, i, after=()):
        return dve.do(lambda e: e.tensor_copy(o, i), after)

    def vset(o, v, after=()):
        return dve.do(lambda e: e.memset(o, v), after)

    def f(t):
        return t.bitcast(F32)

    MUL, ADD, SUB, MAX, MIN = ALU.mult, ALU.add, ALU.subtract, ALU.max, ALU.min

    def weight(w, n0, nk=KT, k0=0):
        return [w[(k0 + c) * P:(k0 + c + 4) * P, n0:n0 + 256].rearrange("(t p) n -> p t n", p=P)
                for c in range(0, nk, 4)]

    ev_w = T["ev_w_in"][0]
    od_w = T["od_w_in"][0]
    w2 = T["w_in_2"][0]
    units = []
    units += [weight(ev_w, 2048 + 256 * i) for i in range(4)]
    for p in range(8):
        units += [weight(ev_w, 3072 + 256 * p), weight(ev_w, 256 * p)]
    units += [weight(T["ev_w_out"][0], 256 * i) for i in range(8)]
    for g in range(4):
        units += [weight(od_w, 512 * g), weight(od_w, 512 * g + 256)]
        units += [weight(od_w, 2048 + 512 * g), weight(od_w, 2048 + 512 * g + 256)]
        units += [weight(T["od_pool_w"][0, g], 0, 4), weight(T["od_pool_w"][0, g], 256, 4)]
    units += [weight(T["od_w_out"][0], 256 * i) for i in range(8)]
    for p in range(4):
        units += [weight(w2, 1024 * i + 256 * p) for i in range(4)]
    for p in range(4):
        units += [weight(w2, 4096 + 1024 * i + 256 * p) for i in range(4)]
    units += [weight(T["w_out_2"][0], 256 * i) for i in range(8)]
    chunks = [c for u in units for c in u]
    raw_free = [None] * NR
    split_free = [None] * NS
    loaded = {}
    split = {}
    at = {"load": 0, "split": 0, "use": 0, "unit": 0}

    def load_next():
        i = at["load"]
        if i < len(chunks):
            loaded[i] = sp.dma(RAW[i % NR][:, :, :], chunks[i], s_raw[i % NR], [raw_free[i % NR]])
            at["load"] += 1

    def split_next():
        i = at["split"]
        if i < len(chunks):
            r, s = i % NR, i % NS
            a = acopy(WHI[s][:, :, :], RAW[r][:, :, :], [loaded[i], split_free[s]])
            b = tt(WLO[s][:, :, :], RAW[r][:, :, :], f(WHI[s][:, :, :]), SUB, [a])
            raw_free[r] = b
            split[i] = (a, b)
            at["split"] += 1
            load_next()

    background = []

    def step(gens):
        for g in list(gens):
            try:
                next(g)
            except StopIteration:
                if g in background:
                    background.remove(g)

    def finish(g):
        if g in background:
            for _ in g:
                pass
            background.remove(g)

    bank_free = [[None, None], [None, None]]

    def unit(work):
        u = at["unit"]
        at["unit"] += 1
        nch = len(units[u])
        done = None
        for c in range(nch):
            i = at["use"]
            at["use"] += 1
            while at["split"] < min(i + NS, len(chunks)) and at["split"] <= i:
                split_next()
            s = i % NS
            after = list(split[i])
            done = work(4 * c, WHI[s], WLO[s], c == 0, c == nch - 1, after)
            split_free[s] = done
            while at["split"] < min(i + NS, len(chunks)):
                split_next()
            step([mods])
        return done

    def gemm(hi, lo, ready, extra=None):
        pair = at["unit"] % 2
        banks, free = G[pair], bank_free[pair]

        def work(k0, wh, wl, first, last, after):
            done = None
            for nt in range(2):
                cols = slice(nt * P, nt * P + P)
                for j in range(4):
                    k = k0 + j
                    w = after + [m for m in ready[k]]
                    if first and j == 0:
                        w = w + [free[nt]]
                    o = banks[nt][:, :]
                    a, b = wh[:, j, cols], wl[:, j, cols]
                    end = last and j == 3
                    fin = nt == 1 and j == 3
                    mm(o, a, hi[:, k, :], first and j == 0, False, w)
                    mm(o, a, lo[:, k, :], False, False)
                    done = mm(o, b, hi[:, k, :], False, end, sig=(fin or end) and extra is None)
                    if extra is not None:
                        eo, ehi, elo, eready, efree = extra
                        w = [m for m in eready[k]]
                        if first and j == 0 and nt == 0:
                            w = w + [efree]
                        mm(eo(nt), a, ehi[:, k, :], first and j == 0 and nt == 0, False, w)
                        mm(eo(nt), a, elo[:, k, :], False, False)
                        done = mm(eo(nt), b, ehi[:, k, :], False, end, sig=fin or end)
                    if end and nt == 0:
                        half.append(done)
                    if j % 2:
                        step(background)
            return done

        half = []
        done = unit(work)
        return pair, banks, [half[0], done]

    def gemm_tok(tiles, outs, frees):
        def work(k0, wh, wl, first, last, after):
            done = None
            for i, (hi, lo, ready) in enumerate(tiles):
                for j in range(4):
                    k = k0 + j
                    w = after + [m for m in ready[k]]
                    begin = first and j == 0 and i % 2 == 0
                    if begin:
                        w = w + [frees[i // 2]]
                    mm(outs(i), hi(k), wh[:, j, :], begin, False, w)
                    mm(outs(i), lo(k), wh[:, j, :], False, False)
                    done = mm(outs(i), hi(k), wl[:, j, :], False, last and j == 3,
                              sig=i == len(tiles) - 1 and j == 3)
                step(background)
            return done

        return unit(work)

    pool.dma(IDN[:, :], T["t_sq"][0], s_cst)
    m_cst = pool.dma(ONE[:, :], T["t_sq"][1], s_cst)
    z0 = vset(PR[1][:, :], 0.0)
    z1 = vset(PR[2][:, :], 0.0)

    def params(pr, r, src, n, after=()):
        return pool.dma(PR[pr][r:r + n, :], src.rearrange("(t p) -> t p", p=P), s_par, after)

    params(0, 0, T["c"][0], 16)
    params(0, 16, T["c_ctx"], 16)
    params(0, 32, T["c_2"][0], 16)
    params(0, 48, T["ev_pre_g"][0], 16)
    params(0, 64, T["ev_post_g"][0], 16)
    params(0, 80, T["od_pre_g"][0], 16)
    params(0, 96, T["od_post_g"][0], 16)
    params(0, 112, T["norm_gain_2"][0], 16)
    params(1, 0, T["od_pool_scale"][0], 16, [z0, z1])
    params(1, 16, T["ret_norm_gain_2"][0], 8)
    params(1, 24, T["ev_q_norm"][0], 1)
    params(1, 25, T["ev_k_norm"][0], 1)
    params(1, 26, T["sb_q_gain_2"][0], 1)
    params(1, 27, T["sb_k_gain_2"][0], 1)
    params(1, 32, T["ev_mod_b"][0], 48)
    params(1, 80, T["od_mod_b"][0], 48)
    params(2, 0, T["b_ada_2"][0], 48)
    m_par = pool.dma(SM[0:1, 0:8], T["ev_sink"], s_par)
    m_xn = [pool.dma(XN[i][:, :], T["ctx"][0, i * P:(i + 1) * P, :], s_xn[i]) for i in range(2)]
    m_xn.append(pool.dma(XN[2][:, :], T["x"][0, 0:P, :], s_xn[2]))
    m_rope = pool.dma(CS[:, :], T["t_rope_a"][0], s_rope)
    m_rope = pool.dma(SN[:, :], T["t_rope_a"][1], s_rope)
    m_mk = pool.dma(MK[:, 0:2, :], T["t_mask"].rearrange("a p n -> p a n"), s_tri)

    act.do(lambda e: e.add_instruction(mybir.InstLoadActFuncSet(
        act_func_set_id=NAT_LOG_EXP, name=nc.get_next_instruction_name(),
        engine=mybir.EngineType.Activation, ins=[], outs=[])), (), False)

    tr(TB[:, 0:P], PR[0][:, :], [m_cst, m_par])
    tr(TB[:, P:2 * P], PR[1][:, :])
    tr(TB[:, 2 * P:3 * P], PR[2][:, :])
    m_t = mm(TB[:, 384:392], ONE[0:1, :], SM[0:1, 0:8], True, True, sig=True)
    m_col = vcopy(COL[:, :], TB[:, 0:304], [m_t])
    m_snk = ts(SM[:, 8:16], TB[:, 384:392], -1.0, None, MUL, None, [m_t])
    m_snk = ts(SM[:, 16:24], TB[:, 384:392], 1.0, None, MUL, None, [m_snk])

    a1 = af(SC[:, :], COL[:, 0:48], ACT.Abs, [m_col])
    a1 = af(SC[:, :], SC[:, :], ACT.Exp, [a1], scale=-1.0)
    a1 = af(SC[:, :], SC[:, :], ACT.Ln, [a1], bias=1.0)
    d1 = stt(SC[:, :], COL[:, 0:48], 0.0, SC[:, :], MIN, SUB, [a1])
    a1 = af(SC[:, :], SC[:, :], ACT.Exp, [d1])
    m_sc = tt(SC[:, :], COL[:, 0:48], SC[:, :], MUL, [a1])
    scv = SC[:, :].rearrange("p (v k) -> p k v", k=KT)

    ring_free = [None] * 3
    x_done = [None] * KT
    c_done = [None] * KT
    nat = [("c", 0), ("c", 1)] + [("x", i) for i in range(4)]
    tb = [TB, OB]
    tfree = [m_snk, None]
    cnt = 0
    for n, (what, i) in enumerate(nat):
        r = n % 3
        if n >= 3:
            m_xn.append(pool.dma(XN[r][:, :], T["x"][0, i * P:(i + 1) * P, :], s_xn[r], [ring_free[r]]))
        for q in range(4):
            b = cnt % 2
            for j in range(4):
                k = 4 * q + j
                m = tr(tb[b][:, j * P:(j + 1) * P], XN[r][:, k * P:(k + 1) * P],
                       [m_xn[n], tfree[b], m_cst], sig=j == 3)
            dst = (CT if what == "c" else Y)[:, 4 * q:4 * q + 4, i * P:(i + 1) * P]
            src = tb[b][:, :].rearrange("p (j n) -> p j n", j=4)
            if cnt % 2:
                tfree[b] = vcopy(dst, src, [m])
            else:
                tfree[b] = act.do(lambda e, dst=dst, src=src: e.activation(dst, src, ACT.Copy), [m])
            for j in range(4):
                if what == "c":
                    c_done[4 * q + j] = tfree[b]
                else:
                    x_done[4 * q + j] = tfree[b]
            cnt += 1
        ring_free[r] = m
    both = [tfree[0], tfree[1]]
    spill = [pool.dma(XS.ap()[k], Y[:, k, :], s_spill, both) for k in range(KT)]
    m_spill = spill[-1]

    tmp = {"sq": [None, None], "chain": None, "tb": None, "ob": None, "s": None}
    tmp["tb"] = tfree[0]
    tmp["ob"] = tfree[1]

    def rstd(n, bank_ap, m_stat, count, extra=()):
        m = ts(TM[:, 0:n], bank_ap, 1.0 / count, EPS, MUL, ADD, [m_stat, tmp["chain"]] + list(extra))
        a = af(TY[:, 0:n], TM[:, 0:n], ACT.Ln, [m])
        a = af(TY[:, 0:n], TY[:, 0:n], ACT.Exp, [a], scale=-0.5)
        b = tt(TT_[:, 0:n], TY[:, 0:n], TY[:, 0:n], MUL, [a])
        b = stt(TT_[:, 0:n], TT_[:, 0:n], -0.5, TM[:, 0:n], MUL, MUL, [b])
        b = stt(TY[:, 0:n], TT_[:, 0:n], 1.5, TY[:, 0:n], ADD, MUL, [b])
        return m, b

    def column_stats(tiles, n, ready, bank, free):
        m = None
        for k in range(KT):
            s = k % 2
            a = af(SQ2[s][:, 0:n], tiles[:, k, 0:n], ACT.Square, list(ready[k]) + [tmp["sq"][s]])
            m = mm(bank[:, 0:n], ONE[:, :], SQ2[s][:, 0:n], k == 0, k == KT - 1, [a, free], sig=True)
            tmp["sq"][s] = m
        return m

    def modulated(tiles, n, m_y, gain, shift, hi, lo, free, ready_in=()):
        ready = []
        last = None
        tfree_ = [None, None]
        for k in range(KT):
            s = k % 2
            d = tt(SQ2[s][:, 0:n], tiles[:, k, 0:n], TY[:, 0:n], MUL, [m_y, tmp["sq"][s]] + list(ready_in))
            d2 = ts(SQ2[s][:, 0:n], SQ2[s][:, 0:n], gain(k), shift(k), MUL, ADD, [d])
            a = acopy(hi[:, k, 0:n], SQ2[s][:, 0:n], [d2] + list(free))
            last = tt(lo[:, k, 0:n], SQ2[s][:, 0:n], f(hi[:, k, 0:n]), SUB, [a])
            tmp["sq"][s] = last
            ready.append([last])
        tmp["chain"] = last
        return ready, last

    m_sx = column_stats(Y, SEQ, [both] * KT, TB, tmp["tb"])
    m_m, m_yx = rstd(SEQ, TB[:, :], m_sx, D)
    tmp["tb"] = m_m

    ev_mw = T["ev_mod_w"][0]
    mod_bank = [G[0][0], G[0][1]]
    mfree = [None, None]
    rings = RAW + MRAW
    rsem = s_raw + s_mraw
    rfree = [None] * 5
    n_m = 0
    for nb in range(16):
        b = nb % 2
        for c in range(4):
            r = n_m % 5
            n_m += 1
            m_l = sp.dma(rings[r][:, :, :], weight(ev_mw, 256 * nb)[c], rsem[r], [rfree[r]])
            m = None
            for nt in range(2):
                for j in range(4):
                    m = mm(mod_bank[b][:, 2 * nt:2 * nt + 2], rings[r][:, j, nt * P:(nt + 1) * P],
                           scv[:, 4 * c + j, 0:2], c == 0 and nt == 0 and j == 0, c == 3 and j == 3,
                           [m_l, m_sc, mfree[b]], sig=nt == 1 and j == 3)
            rfree[r] = m
        v = mod_bank[b][:, 0:4].rearrange("p (n v) -> p v n", v=2)
        d = tt(MOD[:, 0, 2 * nb:2 * nb + 2], v[:, 0, :], COL[:, 160 + 2 * nb:162 + 2 * nb], ADD, [m, m_col])
        mfree[b] = tt(MODX[:, 2 * nb:2 * nb + 2], v[:, 1, :], COL[:, 160 + 2 * nb:162 + 2 * nb], ADD, [m])
    for r in range(NR):
        raw_free[r] = rfree[r]
    mraw_free = [rfree[3], rfree[4]]
    m_mod0 = mfree[1]
    for p_ in range(2):
        bank_free[p_] = [mfree[1], mfree[1]] if p_ == 0 else [None, None]

    def gain_cols(dst, scale, g, after):
        return stt(dst, scale, 1.0, g, ADD, MUL, after)

    m_g = gain_cols(MOD[:, 0, 16:32], MOD[:, 0, 16:32], COL[:, 48:64], [m_mod0])
    m_gx = gain_cols(MODX[:, 16:32], MODX[:, 16:32], COL[:, 48:64], [m_mod0])

    mod_jobs = [("ev", T["ev_mod_w"][0], 0, 0, 16, 24, 160), ("od", T["od_mod_w"][0], 1, 0, 0, 24, 208),
                ("w2", T["w_ada_2"][0], 2, 32, 0, 24, 256)]
    mod_done = {}

    def mod_stream():
        n = 0
        acc_free = None
        for name, w, layer, c0, nb0, nb1, bias in mod_jobs:
            for nb in range(nb0, nb1):
                d = None
                for c in range(4):
                    r = n % 2
                    n += 1
                    m_l = sp.dma(MRAW[r][:, :, :], weight(w, 256 * nb)[c], s_mraw[r], [mraw_free[r]])
                    yield
                    for j in range(4):
                        col = SC[:, c0 + 4 * c + j:c0 + 4 * c + j + 1]
                        if c == 0 and j == 0:
                            d = ts(MACC[:, :], MRAW[r][:, j, :], col, None, MUL, None, [m_l, m_sc, acc_free])
                        else:
                            d = stt(MACC[:, :], MRAW[r][:, j, :], col, MACC[:, :], MUL, ADD, [m_l, d])
                    mraw_free[r] = d
                yield
                b = G_mod()
                mm(b[:, 0:1], MACC[:, 0:P], ONE[:, 0:1], True, True, [d, tmp["tb"]])
                m = mm(b[:, 1:2], MACC[:, P:2 * P], ONE[:, 0:1], True, True, sig=True)
                acc_free = m
                v = tt(MOD[:, layer, 2 * nb:2 * nb + 2], b[:, 0:2], COL[:, bias + 2 * nb:bias + 2 * nb + 2],
                       ADD, [m])
                tmp["tb"] = v
                mod_done[(name, nb)] = v
            yield

    def G_mod():
        return TB

    h_ready, m_h = modulated(Y, SEQ, m_yx, lambda k: MOD[:, 0, 16 + k:17 + k], lambda k: MOD[:, 0, k:k + 1],
                             HHI, HLO, [], [m_g])
    m_sc_ = column_stats(CT, CTX, [both] * KT, OB, tmp["ob"])
    m_m, m_yc = rstd(CTX, OB[:, 0:CTX], m_sc_, D)
    tmp["ob"] = m_m
    hc_ready, m_hc = modulated(CT, CTX, m_yc, lambda k: MODX[:, 16 + k:17 + k], lambda k: MODX[:, k:k + 1],
                               CHI, CLO, [m_spill, m_h], [m_gx])

    load_next()
    load_next()
    load_next()
    mods = mod_stream()

    def norm_rope(src, dst, n, gcol, rope, after, fin):
        a = af(SQ2[1][:, 0:n], src, ACT.Square, list(after) + [tmp["sq"][1]])
        yield
        if gcol is not None:
            m = mm(TB[:, 0:n], ONE[:, :], SQ2[1][:, 0:n], True, True, [a, tmp["tb"]], sig=True)
            tmp["sq"][1] = m
            mm_, y = rstd(n, TB[:, 0:n], m, 128)
            tmp["tb"] = mm_
            yield
            d = stt(TM[:, 0:n], src, gcol, TY[:, 0:n], MUL, MUL, [y])
            cur = TM[:, 0:n]
            tmp["chain"] = d
        else:
            tmp["sq"][1] = a
            cur, d = src, a
        if rope:
            h = 64
            cl = cur
            d1 = tt(TT_[h:P, 0:n], cl[0:h, :], SN[0:h, 0:n], MUL, [d, m_rp[0], tmp["chain"]] + list(after))
            d2 = tt(TT_[0:h, 0:n], cl[h:P, :], SN[h:P, 0:n], MUL, [d1])
            d3 = tt(dst, cur, CS[:, 0:n], MUL, [d2])
            d4 = tt(dst, dst, TT_[:, 0:n], ADD, [d3])
        else:
            d4 = vcopy(dst, cur, [d])
        tmp["chain"] = d4
        fin.append(d4)
        yield

    def run(g):
        for _ in g:
            pass

    m_rp = [m_rope]

    ctx_place = lambda nt: OB[:, nt * CTX:(nt + 1) * CTX]
    kv_marks = []
    scr_free = [m_hc]
    x_tiles = [(lambda k, i=i: HHI[:, k, i * P:(i + 1) * P], lambda k, i=i: HLO[:, k, i * P:(i + 1) * P], h_ready)
               for i in range(4)]
    c_tiles = [(lambda k, i=i: CHI[:, k, i * P:(i + 1) * P], lambda k, i=i: CLO[:, k, i * P:(i + 1) * P], hc_ready)
               for i in range(2)]
    for side in range(2):
        pair, banks, done = gemm(HHI, HLO, h_ready, (ctx_place, CHI, CLO, hc_ready, tmp["ob"]))
        ev = []
        for nt in range(2):
            kh = 2 * side + nt
            a = acopy(KTA[:, kh, 0:SEQ], banks[nt][:, :], [done[1]] + scr_free)
            bank_free[pair][nt] = a
            a2 = acopy(KTA[:, kh, SEQ:768], ctx_place(nt), [done[1]])
            tmp["ob"] = a2
            ev.append((kh, a, a2))
        parts = []
        for kh, a, a2 in ev:
            if side == 0:
                parts.append(chain([
                    norm_rope(KTA[:, kh, 0:SEQ], KTA[:, kh, 0:SEQ], SEQ, COL[:, 153:154], True, [a], kv_marks),
                    norm_rope(KTA[:, kh, SEQ:768], KTA[:, kh, SEQ:768], CTX, COL[:, 153:154], False, [a2],
                              kv_marks)]))
            else:
                parts.append(norm_rope_copy(norm_rope, KTA, kh, SQ2, tmp, a, kv_marks, vcopy))
        task = chain(parts)
        background.append(task)
        pair = at["unit"] % 2
        outs = [G[pair][0][:, 0:256], G[pair][0][:, 256:512], G[pair][1][:, 0:256], G[pair][1][:, 256:512],
                OB[:, 0:256], OB[:, 256:512]]
        done = gemm_tok(x_tiles + c_tiles, lambda i: outs[i],
                        [bank_free[pair][0], bank_free[pair][1], tmp["ob"]])
        for i, b in enumerate([G[pair][0], G[pair][1], OB]):
            a = acopy(VV[:, 2 * i:2 * i + 2, side * 256:side * 256 + 256],
                      b[:, :].rearrange("p (t n) -> p t n", t=2), [done] + scr_free)
            if i < 2:
                bank_free[pair][i] = a
            else:
                tmp["ob"] = a
            kv_marks.append(a)
        finish(task)
    m_ctx_read = done

    buf = {"qt": None, "pb": [None, None], "pt": None, "s": None, "nm": 0}

    def softmax_head(h, y_mark, y_ready):
        band = h >= 8
        kv = (h // 4) if not band else 2 + (h - 8) // 4
        vcol = slice(kv * P, kv * P + P)
        kt_ = KTA[:, kv, :]
        pend = []

        def spread(qt, b, jobs, m_p):
            mt = None
            for g0 in range(0, len(jobs), 4):
                part = jobs[g0:g0 + 4]
                for x_, (j, c0) in enumerate(part):
                    mt = tr(TB[:, x_ * P:(x_ + 1) * P], PB[b][:, c0:c0 + P], [m_p, tmp["tb"]],
                            sig=x_ == len(part) - 1)
                x_ = 0
                runs = []
                for x2, (j, c0) in enumerate(part):
                    if runs and runs[-1][1] + runs[-1][2] == j:
                        runs[-1][2] += 1
                    else:
                        runs.append([x2, j, 1])
                for x2, j, n in runs:
                    dst = PT[:, j:j + n, qt * P:(qt + 1) * P]
                    src = TB[:, x2 * P:(x2 + n) * P].rearrange("p (j n) -> p j n", j=n)
                    tmp["tb"] = acopy(dst, src, [mt, buf["pt"], tmp["tb"]])
            buf["pb"][b] = mt
            return tmp["tb"]

        last = None
        for qt in range(4):
            b = qt % 2
            lq = QT[:, qt * P:(qt + 1) * P]
            if not band:
                mm(S[:, 0:512], lq, kt_[:, 0:512], True, True, [buf["s"], y_ready[0]] + kv_marks)
                m = mm(S[:, 512:768], lq, kt_[:, 512:768], True, True, sig=True)
                lo_, w = 0, None
                jobs = [(j, j * P) for j in range(6)]
            else:
                t0, t1 = max(0, qt - 1), min(3, qt + 1)
                nb = t1 - t0 + 1
                lo_ = 512 - nb * P
                mm(S[:, lo_:512], lq, kt_[:, t0 * P:(t1 + 1) * P], True, True, [buf["s"], y_ready[0]] + kv_marks)
                m = mm(S[:, 512:768], lq, kt_[:, 512:768], True, True, sig=True)
                if qt > 0:
                    m = tt(S[:, lo_:lo_ + P], S[:, lo_:lo_ + P], MK[:, 0, :], ADD, [m, m_mk])
                if qt < 3:
                    m = tt(S[:, 384:512], S[:, 384:512], MK[:, 1, :], ADD, [m, m_mk])
                jobs = [(t0 + j, lo_ + j * P) for j in range(nb)] + [(4, 512), (5, 640)]
            i = 24 + 4 * (buf["nm"] % 4)
            buf["nm"] += 1
            nm, rs = SM[:, i:i + 1], SM[:, i + 1:i + 2]
            src = S[:, lo_:768]
            d = dve.do(lambda e, nm=nm, src=src: e.tensor_reduce(nm, src, AX_X, MAX, negate=True), [m])
            if band:
                sk = SM[:, 8 + h - 8:9 + h - 8]
                d = ts(nm, nm, sk, None, MIN, None, [d, m_snk])
            a = af(PB[b][:, lo_:768], src, ACT.Exp, [d, buf["pb"][b], m_ctx_read], bias=nm, acc=rs)
            buf["s"] = a
            if band:
                es = SM[:, i + 2:i + 3]
                a2 = af(es, SM[:, 16 + h - 8:17 + h - 8], ACT.Exp, [a], bias=nm)
                d = tt(rs, rs, es, ADD, [a2])
            else:
                d = a
            d = dve.do(lambda e, rs=rs: e.reciprocal(rs, rs), [d])
            m_p = ts(PB[b][:, lo_:768], PB[b][:, lo_:768], rs, None, MUL, None, [d])
            pend.append((qt, b, jobs, m_p))
            yield
            if len(pend) == 2:
                last = spread(*pend.pop(0))
                yield
        last = spread(*pend.pop(0))
        buf["qt"] = m
        yield
        if not band:
            for j in range(6):
                m = mm(OB[:, :], VV[:, j, vcol], PT[:, j, :], j == 0, j == 5, [last, tmp["ob"]] + kv_marks,
                       sig=j == 5)
        else:
            for n, j in enumerate([4, 5, 0, 1, 2, 3]):
                c = slice(0, 512) if j > 3 else slice(max(0, j - 1) * P, min(4, j + 2) * P)
                m = mm(OB[:, c], VV[:, j, vcol], PT[:, j, c], n == 0, n == 5, [last, tmp["ob"]] + kv_marks,
                       sig=n == 5)
        buf["pt"] = m
        yield
        tmp["ob"] = tt(Y[:, h, :], OB[:, :], Y[:, h, :], MUL, [m, y_mark()])
        y_marks[h] = tmp["ob"]
        yield

    def silu_mul(dst, z, done, after):
        s = 0
        a = af(SQ2[s][:, :], z, ACT.Abs, [done, tmp["sq"][s]])
        a = af(SQ2[s][:, :], SQ2[s][:, :], ACT.Exp, [a], scale=-1.0)
        a = af(SQ2[s][:, :], SQ2[s][:, :], ACT.Ln, [a], bias=1.0)
        d = stt(SQ2[s][:, :], z, 0.0, SQ2[s][:, :], MIN, SUB, [a])
        a = af(SQ2[s][:, :], SQ2[s][:, :], ACT.Exp, [d])
        d = tt(dst, z, SQ2[s][:, :], MUL, [a] + list(after))
        tmp["sq"][s] = d
        return d

    QR = scratch("QR", [P, 2, SEQ], F32, 44 * K1)
    y_marks = [None] * KT
    qr_free = [None, None]
    z_marks = [None] * KT

    def pair_task(p, qm):
        for i in range(2):
            h = 2 * p + i
            fin = []
            src = QR[:, i, :]
            for _ in norm_rope(src, QT[:, :], SEQ, COL[:, 152:153] if h < 8 else None, True,
                               [qm[i], qm[2], buf["qt"]], fin):
                yield
            qr_free[i] = fin[0]
            for _ in softmax_head(h, lambda h=h: z_marks[h], fin):
                yield

    m_qs = ts(COL[:, 152:153], COL[:, 152:153], SCALE, None, MUL, None, [m_col])
    task = None
    for p in range(8):
        pair, banks, done = gemm(HHI, HLO, h_ready)
        for nt in range(2):
            z_marks[2 * p + nt] = silu_mul(Y[:, 2 * p + nt, :], banks[nt][:, :], done[nt], [m_ctx_read])
            bank_free[pair][nt] = z_marks[2 * p + nt]
        pair, banks, done = gemm(HHI, HLO, h_ready)
        if task is not None:
            finish(task)
        qm = []
        for nt in range(2):
            a = acopy(QR[:, nt, :], banks[nt][:, :], [done[nt], qr_free[nt], m_ctx_read], scale=SCALE if p >= 4 else 1.0)
            bank_free[pair][nt] = a
            qm.append(a)
        task = pair_task(p, qm + [m_qs])
        background.append(task)
    m_h_read = done[1]
    finish(task)

    def project_out(post, gate, m_gate, x_free):
        back = [pool.dma(XR[:, k, :], XS.ap()[k], s_back, list(x_free)) for k in range(KT)]
        ready = []
        for k in range(KT):
            a = acopy(HHI[:, k, :], Y[:, k, :], [y_marks[k], m_h_read_[0]])
            d = tt(HLO[:, k, :], Y[:, k, :], f(HHI[:, k, :]), SUB, [a])
            ready.append([d])
        all_split = ready[-1][0]
        stat = None
        sq_m = []
        for u in range(8):
            pair, banks, done = gemm(HHI, HLO, ready)
            for nt in range(2):
                k = 2 * u + nt
                if post:
                    a = acopy(Y[:, k, :], banks[nt][:, :], [done[nt], all_split])
                    a2 = af(SQ2[nt][:, :], banks[nt][:, :], ACT.Square, [done[nt], tmp["sq"][nt]])
                    bank_free[pair][nt] = a2
                    sq_m.append(a2)
                    y_marks[k] = a
                else:
                    if k == 0:
                        all_split_ = [all_split, back[-1]]
                    d = stt(Y[:, k, :], banks[nt][:, :], gate(k), XR[:, k, :], MUL, ADD,
                            [done[nt], m_gate()] + all_split_)
                    bank_free[pair][nt] = d
                    y_marks[k] = d
            if post:
                for nt in range(2):
                    k = 2 * u + nt
                    stat = mm(OB[:, :], ONE[:, :], SQ2[nt][:, :], k == 0, k == KT - 1,
                              [sq_m[k], tmp["ob"]], sig=True)
                    tmp["sq"][nt] = stat
        m_h_read_[0] = done[1]
        if post:
            m1, y_ = rstd(SEQ, OB[:, :], stat, D)
            tmp["ob"] = m1
            for k in range(KT):
                d = stt(Y[:, k, :], Y[:, k, :], gate(k), TY[:, :], MUL, MUL, [y_, y_marks[k], m_gate()])
                d = tt(Y[:, k, :], Y[:, k, :], XR[:, k, :], ADD, [d, back[-1]])
                y_marks[k] = d
            tmp["chain"] = d

    m_h_read_ = [m_h_read]
    gcol = {}

    def need_mods(name, nb):
        while (name, nb) not in mod_done:
            next(mods)
        return mod_done[(name, nb)]

    m = need_mods("ev", 23)
    m_gate0 = tt(MOD[:, 0, 32:48], MOD[:, 0, 32:48], COL[:, 64:80], MUL, [m])
    project_out(True, lambda k: MOD[:, 0, 32 + k:33 + k], lambda: m_gate0, [buf["pt"]])

    def next_layer(layer, gain, after_x):
        sp_ = [pool.dma(XS.ap()[k], Y[:, k, :], s_spill, [y_marks[k], m_back_all()]) for k in range(KT)]
        m_s = column_stats(Y, SEQ, [[y_marks[k]] for k in range(KT)], OB, tmp["ob"])
        m1, y_ = rstd(SEQ, OB[:, :], m_s, D)
        tmp["ob"] = m1
        g = gain_cols(MOD[:, layer, 16:32], MOD[:, layer, 16:32], gain, [after_x])
        ready, m_h = modulated(Y, SEQ, y_, lambda k: MOD[:, layer, 16 + k:17 + k],
                               lambda k: MOD[:, layer, k:k + 1], HHI, HLO, [m_h_read_[0]], [g])
        return sp_[-1], ready, m_h

    def m_back_all():
        return (s_back.sem, s_back.n)

    m = need_mods("od", 15)
    m_spill, h_ready, m_h = next_layer(1, COL[:, 80:96], m)

    pad = [vset(UP[i][:, :, :], 0.0, [y_marks[KT - 1]]) for i in range(3)]
    up_free = [None]
    ph_free = [None]
    pooled = [None]
    m_scr = y_marks[KT - 1]
    n_rc = [None]

    def pool_group(g, ev):
        rc = pool.dma(RC[:, :], T["t_rcnt"][g], s_rc, [n_rc[0], m_scr])
        cur = 0
        lo_, hi_ = 1, 544
        d = tt(UP[1][:, :, 1:544], UP[0][:, :, 0:543], UP[0][:, :, 1:544], ADD, ev + [up_free[0]])
        cur = 1
        yield
        sh = 1
        for lv in range(g):
            nxt = 2 if cur == 1 else 1
            a, b = lo_ + sh, hi_ - sh
            d = tt(UP[nxt][:, :, a:b], UP[cur][:, :, a - sh:b - sh], UP[cur][:, :, a + sh:b + sh], ADD, [d])
            lo_, hi_ = a, b
            sh *= 2
            cur = nxt
            yield
        o = 2 if cur == 1 else 1
        dst = UP[o][:, :, 16:528]
        for j in range(4):
            d = tt(dst[:, j, :], UP[cur][:, j, 16:528], RC[:, :], MUL, [d, rc])
        n_rc[0] = d
        d = tt(dst, dst, UP[0][:, :, 16:528], SUB, [d])
        yield
        a = acopy(PHI[:, :, :], dst, [d, ph_free[0]])
        d = tt(PLO[:, :, :], dst, f(PHI[:, :, :]), SUB, [a])
        up_free[0] = d
        pooled[0] = d
        yield

    for g in range(4):
        ev = []
        for u in range(2):
            pair, banks, done = gemm(HHI, HLO, h_ready)
            for nt in range(2):
                a = acopy(UP[0][:, 2 * u + nt, 16:528], banks[nt][:, :], [done[nt], pad[2], up_free[0]])
                bank_free[pair][nt] = a
                ev.append(a)
        task = pool_group(g, [ev[-1]])
        background.append(task)
        for u in range(2):
            pair, banks, done = gemm(HHI, HLO, h_ready)
            for nt in range(2):
                k = 4 * g + 2 * u + nt
                z = silu_mul(Y[:, k, :], banks[nt][:, :], done[nt], [m_spill, m_h])
                bank_free[pair][nt] = z
                z_marks[k] = ts(Y[:, k, :], Y[:, k, :], COL[:, 128 + k:129 + k], None, MUL, None, [z])
        m_h_read_[0] = done[1]
        finish(task)
        for u in range(2):
            pair, banks, done = gemm(PHI, PLO, [[pooled[0]]] * 4)
            for nt in range(2):
                k = 4 * g + 2 * u + nt
                d = tt(Y[:, k, :], banks[nt][:, :], Y[:, k, :], MUL, [done[nt], z_marks[k]])
                bank_free[pair][nt] = d
                y_marks[k] = d
        ph_free[0] = done[1]

    m = need_mods("od", 23)
    m_gate1 = tt(MOD[:, 1, 32:48], MOD[:, 1, 32:48], COL[:, 96:112], MUL, [m])
    project_out(True, lambda k: MOD[:, 1, 32 + k:33 + k], lambda: m_gate1, [ph_free[0], up_free[0]])
    m = need_mods("w2", 15)
    m_spill, h_ready, m_h = next_layer(2, COL[:, 112:128], m)

    m_rope = pool.dma(CS[:, :], T["t_rope_b"][0], s_rope, [y_marks[0]])
    m_rope = pool.dma(SN[:, :], T["t_rope_b"][1], s_rope)
    m_rp[0] = m_rope
    m_tri = pool.dma(MK[:, :, :], T["t_sb"].rearrange("a p n -> p a n"), s_tri, [y_marks[0]])
    m_scr = y_marks[KT - 1]
    m_sg = ts(COL[:, 154:155], COL[:, 154:155], SCALE, None, MUL, None, [m_col])
    bf = {"q": [m_scr, m_scr], "k": [m_scr, m_scr], "v": [m_scr, m_scr], "ls": [None, None],
          "sp": None, "w": [None, None], "dk": m_scr, "ta": [None, None], "s": [buf["s"], buf["s"]],
          "n": 0, "wn": 0, "sn": 0}
    LS2 = [LS, LSB]

    def stick_head(h, b, i, vm):
        q, k_, v = Q2[b][:, i, :], K2[b][:, i, :], V2[b]
        first_o = True
        prev = None
        for kt in (3, 2, 1, 0):
            c0 = kt * P
            n = SEQ - c0
            sb_ = bf["sn"] % 2
            bf["sn"] += 1
            Z = S[:, sb_ * 512 + c0:sb_ * 512 + 512]
            m = mm(Z, k_[:, c0:c0 + P], q[:, c0:SEQ], True, True, [bf["s"][sb_]] + vm, sig=True)
            yield
            ls, spt = LS2[sb_][:, c0:SEQ], SP[:, kt, c0:SEQ]
            ta = TA[0][:, c0:SEQ]
            a = af(ta, Z, ACT.Abs, [m, bf["ta"][0], m_scr])
            a = af(ta, ta, ACT.Exp, [a], scale=-1.0)
            a = af(ta, ta, ACT.Ln, [a], bias=1.0)
            d = stt(ls, Z, 0.0, ta, MIN, SUB, [a, bf["ls"][sb_]])
            d2 = stt(spt, Z, 0.0, ta, MAX, ADD, [a, bf["sp"]])
            bf["s"][sb_] = d2
            bf["ta"][0] = d2
            d3 = tt(SP[:, kt, c0:c0 + P], SP[:, kt, c0:c0 + P], MK[:, 1, :], MUL, [d2, m_tri])
            d4 = tt(LS2[sb_][:, c0:c0 + P], LS2[sb_][:, c0:c0 + P], MK[:, 2, :], ADD, [d3])
            yield
            C = TB[:, c0:SEQ]
            mc = mm(C, MK[:, 0, :], spt, True, kt == 3, [d3, tmp["tb"]], sig=True)
            for k2 in range(kt + 1, 4):
                mc = mm(TB[:, k2 * P:SEQ], ONE[:, :], SP[:, k2, k2 * P:SEQ], False, k2 == 3, sig=True)
            d = tt(ls, ls, C, SUB, [mc, d4])
            tmp["tb"] = d
            wi = bf["wn"] % 2
            bf["wn"] += 1
            w = WB[wi][:, c0:SEQ]
            a = af(w, ls, ACT.Exp, [d, bf["w"][wi]])
            bf["ls"][sb_] = a
            yield
            if first_o:
                zz = WB[wi][:, 0:c0]
                a = act.do(lambda e, zz=zz, src=MKZ[:, 0:c0]: e.activation(zz, src, ACT.Copy), [a, m_zero])
            mo = mm(OB[:, (0 if first_o else c0):SEQ], v[:, kt, i * P:(i + 1) * P],
                    WB[wi][:, (0 if first_o else c0):SEQ], first_o, kt == 0, [a, tmp["ob"]], sig=True)
            bf["w"][wi] = mo
            first_o = False
        bf["sp"] = mo
        yield
        tmp["ob"] = tt(Y[:, h, :], OB[:, :], Y[:, h, :], MUL, [mo, z_marks[h]])
        y_marks[h] = tmp["ob"]
        yield
        readers.append(mo)

    readers = []
    MKZ = TA[1]
    m_zero = vset(TA[1][:, :], 0.0, [m_scr])

    def sb_task(p, b, qm, km, vmk, fin):
        for i in range(2):
            f1 = []
            for _ in norm_rope_plain(Q2[b][:, i, :], COL[:, 154:155], [qm[i]], f1):
                yield
            for _ in norm_rope_plain(K2[b][:, i, :], COL[:, 155:156], [km[i]], f1):
                yield
            for _ in stick_head(2 * p + i, b, i, f1 + [vmk]):
                yield
        bf["q"][b] = bf["k"][b] = bf["v"][b] = readers[-1]

    def norm_rope_plain(t, gcol_, after, fin):
        a = af(SQ2[1][:, :], t, ACT.Square, list(after) + [tmp["sq"][1]])
        yield
        m = mm(TB[:, :], ONE[:, :], SQ2[1][:, :], True, True, [a, tmp["tb"]], sig=True)
        tmp["sq"][1] = m
        m_, y = rstd(SEQ, TB[:, :], m, 128)
        tmp["tb"] = m_
        yield
        d = stt(t, t, gcol_, TY[:, :], MUL, MUL, [y])
        tmp["chain"] = d
        fin.append(d)
        yield

    def rope_only(t, after, fin):
        h = 64
        d1 = tt(TT_[h:P, :], t[0:h, :], SN[0:h, :], MUL, [tmp["chain"], m_rp[0]] + list(after))
        d2 = tt(TT_[0:h, :], t[h:P, :], SN[h:P, :], MUL, [d1])
        d3 = tt(t, t, CS[:, :], MUL, [d2])
        d4 = tt(t, t, TT_[:, :], ADD, [d3])
        tmp["chain"] = d4
        fin.append(d4)
        yield

    def ret_head(h, b, i, vm):
        q, k_, v = Q2[b][:, i, :], K2[b][:, i, :], V2[b]
        dk = pool.dma(DK[:, :], T["t_decay"][h], s_dk, [bf["dk"]])
        yield
        mo = None
        for kt in range(4):
            c0 = kt * P
            sb_ = bf["sn"] % 2
            bf["sn"] += 1
            Z = S[:, sb_ * 512 + c0:sb_ * 512 + 512]
            m = mm(Z, k_[:, c0:c0 + P], q[:, c0:SEQ], True, True, [bf["s"][sb_]] + vm, sig=True)
            wi = bf["wn"] % 2
            bf["wn"] += 1
            d = tt(WB[wi][:, c0:SEQ], Z, DK[:, 0:SEQ - c0], MUL, [m, dk, bf["w"][wi]])
            bf["s"][sb_] = d
            yield
            mo = mm(OB[:, c0:SEQ], v[:, kt, i * P:(i + 1) * P], WB[wi][:, c0:SEQ], kt == 0, kt == 3,
                    [d, tmp["ob"]], sig=True)
            bf["w"][wi] = mo
        bf["dk"] = d
        readers.append(mo)
        a = acopy(LS[:, :], OB[:, :], [mo, bf["ls"][0]])
        tmp["ob"] = a
        yield
        m = mm(TB[:, :], ONE[:, :], LS[:, :], True, True, [a, tmp["tb"]], sig=True)
        d = stt(LS[:, :], TB[:, :], -1.0 / 128, LS[:, :], MUL, ADD, [m])
        tmp["tb"] = d
        a = af(SQ2[1][:, :], LS[:, :], ACT.Square, [d, tmp["sq"][1]])
        yield
        m = mm(TB[:, :], ONE[:, :], SQ2[1][:, :], True, True, [a, tmp["tb"]], sig=True)
        tmp["sq"][1] = m
        m_, y = rstd(SEQ, TB[:, :], m, 128)
        tmp["tb"] = m_
        d = stt(LS[:, :], LS[:, :], COL[:, 144 + h:145 + h], TY[:, :], MUL, MUL, [y])
        tmp["chain"] = d
        yield
        d = tt(Y[:, 8 + h, :], LS[:, :], Y[:, 8 + h, :], MUL, [d, z_marks[8 + h]])
        bf["ls"][0] = d
        y_marks[8 + h] = d
        yield

    def ret_task(p, b, qm, km, vmk):
        for i in range(2):
            f1 = []
            for _ in rope_only(Q2[b][:, i, :], [qm[i]], f1):
                yield
            for _ in rope_only(K2[b][:, i, :], [km[i]], f1):
                yield
            for _ in ret_head(2 * p + i, b, i, f1 + [vmk]):
                yield
        bf["q"][b] = bf["k"][b] = bf["v"][b] = readers[-1]

    x_tiles = [(lambda k, i=i: HHI[:, k, i * P:(i + 1) * P], lambda k, i=i: HLO[:, k, i * P:(i + 1) * P], h_ready)
               for i in range(4)]
    task = None
    for n in range(8):
        b = n % 2
        sides = []
        for what, dst in (("q", Q2[b]), ("k", K2[b])):
            pair, banks, done = gemm(HHI, HLO, h_ready)
            ms = []
            for nt in range(2):
                a = acopy(dst[:, nt, :], banks[nt][:, :], [done[nt], bf[what][b]])
                bank_free[pair][nt] = a
                ms.append(a)
            sides.append(ms)
        pair = at["unit"] % 2
        outs2 = [G[pair][i // 2][:, (i % 2) * 256:(i % 2) * 256 + 256] for i in range(4)]
        done = gemm_tok(x_tiles, lambda i, outs2=outs2: outs2[i], [bank_free[pair][0], bank_free[pair][1]])
        for i in range(2):
            a = acopy(V2[b][:, 2 * i:2 * i + 2, :], G[pair][i][:, :].rearrange("p (t n) -> p t n", t=2),
                      [done, bf["v"][b]])
            bank_free[pair][i] = a
        vmk = a
        pair, banks, done = gemm(HHI, HLO, h_ready)
        for nt in range(2):
            k = 2 * n + nt
            z_marks[k] = silu_mul(Y[:, k, :], banks[nt][:, :], done[nt], [m_spill, m_h])
            bank_free[pair][nt] = z_marks[k]
        if task is not None:
            finish(task)
        if n < 4:
            task = sb_task(n, b, sides[0], sides[1], vmk, None)
        else:
            task = ret_task(n - 4, b, sides[0], sides[1], vmk)
        background.append(task)
    m_h_read_[0] = done[1]
    finish(task)
    m = need_mods("w2", 23)
    project_out(False, lambda k: MOD[:, 2, 32 + k:33 + k], lambda: m, [readers[-1], y_marks[KT - 1]])

    write_out()


def chain(gens):
    for g in gens:
        for _ in g:
            yield


def norm_rope_copy(norm_rope, KTA, kh, SQ2, tmp, a, marks, vcopy):
    for _ in norm_rope(KTA[:, kh, 0:SEQ], KTA[:, kh, 0:SEQ], SEQ, None, True, [a], marks):
        yield


def tables():
    import numpy as np
    f4 = np.float32
    i = np.arange(P)
    sq = np.stack([np.eye(P), np.ones((P, P))]).astype(f4)
    low = np.where(i[None, :] >= i[:, None], 0.0, -1e30)
    high = np.where(i[None, :] <= i[:, None], 0.0, -1e30)
    mask = np.stack([low, high]).astype(f4)
    tri = (i[:, None] > i[None, :]).astype(f4)
    past = (i[:, None] < i[None, :]).astype(f4)
    sb = np.stack([tri, past, np.where(past > 0, 0.0, -1e30)]).astype(f4)

    def rope(ang):
        c, s = np.cos(ang).T, np.sin(ang).T
        return np.stack([np.concatenate([c, c]), np.concatenate([s, -s])]).astype(f4)

    t = np.arange(SEQ)
    inv = (10000.0 ** (-np.arange(32) / 32.0)).astype(f4)
    ang = np.concatenate([(t // 64).astype(f4)[:, None] * inv, (t % 64).astype(f4)[:, None] * inv], axis=1)
    inv2 = (10000.0 ** (-np.arange(64) / 64.0)).astype(f4)
    ang2 = t.astype(f4)[:, None] * inv2
    rc = np.stack([1.0 / (np.clip(t + w // 2, 0, SEQ) - np.clip(t - w // 2, 0, SEQ)) for w in (2, 4, 8, 16)])
    rc = np.ascontiguousarray(np.broadcast_to(rc[:, None, :], (4, P, SEQ))).astype(f4)
    g = np.log1p(-np.exp2(-5.0 - np.arange(8)))
    rel = t[None, :] - i[:, None]
    dec = np.where(rel[None] >= 0, np.exp(np.maximum(rel, 0)[None] * g[:, None, None]), 0.0) * SCALE
    return {"t_sq": sq, "t_mask": mask, "t_sb": sb, "t_rope_a": rope(ang.astype(np.float64)),
            "t_rope_b": rope(ang2.astype(np.float64)), "t_rcnt": rc, "t_decay": dec.astype(f4)}


def kernel(**inputs):
    import numpy as np
    import concourse.bacc as bacc
    from concourse.bass_utils import run_bass_kernel_spmd as run

    nc = bacc.Bacc("TRN2", target_bir_lowering=False, num_devices=1)
    arrays, T = {}, {}
    const = tables()
    for name in INPUTS + TABLES:
        a = np.ascontiguousarray(const[name] if name in const else inputs[name])
        arrays[f"in_{name}"] = a
        T[name] = nc.dram_tensor(f"in_{name}", a.shape, F32, kind="ExternalInput").ap()
    out = nc.dram_tensor("out_x", (1, SEQ, D), F32, kind="ExternalOutput").ap()
    program(nc, T, out)
    r = run(nc, [arrays], core_ids=[0])
    return r.results[0]["out_x"]
```

```python
from contextlib import ExitStack

import concourse.bass as bass
from concourse import mybir

F32 = mybir.dt.float32
F32R = mybir.dt.float32r
ALU = mybir.AluOpType
ACT = mybir.ActivationFunctionType
AX_X = mybir.AxisListType.X

P = 128
D = 2048
KT = 16
SEQ = 512
CTX = 256
EPS = 1e-6
SCALE = 128.0 ** -0.5
NAT_LOG_EXP = 6

INPUTS = [
    "x", "c", "ctx", "c_ctx", "ev_mod_w", "ev_mod_b", "ev_pre_g", "ev_post_g", "ev_w_in", "ev_q_norm",
    "ev_k_norm", "ev_sink", "ev_w_out", "od_mod_w", "od_mod_b", "od_pre_g", "od_post_g", "od_w_in",
    "od_pool_w", "od_pool_scale", "od_w_out", "c_2", "w_ada_2", "b_ada_2", "norm_gain_2", "w_in_2",
    "sb_q_gain_2", "sb_k_gain_2", "ret_norm_gain_2", "w_out_2",
]
TABLES = ["t_sq", "t_mask", "t_sb", "t_r4", "t_rope_a", "t_rope_b", "t_rcnt", "t_decay"]


class Line:

    def __init__(self, sem):
        self.sem, self.n, self.ops = sem, 0, []

    def do(self, fn, after=(), sig=True):
        if sig:
            self.n += 1
        self.ops.append((fn, [m for m in after if m is not None], self.sem if sig else None, 1))
        return (self.sem, self.n) if sig else None

    def dma(self, out, in_, slot, after=()):
        slot.n += 16
        self.ops.append((lambda e: e.dma_start(out, in_), [m for m in after if m is not None], slot.sem, 16))
        return (slot.sem, slot.n)

    def emit(self, eng):
        seen = {}
        for fn, after, sem, by in self.ops:
            for s, v in after:
                if seen.get(s.name, 0) < v:
                    eng.wait_ge(s, v)
                    seen[s.name] = v
            ins = fn(eng)
            if sem is not None:
                ins.then_inc(sem, by)


class Slot:

    def __init__(self, sem):
        self.sem, self.n = sem, 0


def program(nc, T, out):
    with ExitStack() as ctx:
        build(nc, ctx, T, out)


def build(nc, ctx, T, out):
    base = nc.sbuf_base
    end = nc.sbuf_usable_end
    arena = ctx.enter_context(nc.sbuf_tensor("arena", [P, (end - base) // 4 - 64], F32))
    del arena
    top = [(base + 63) // 64 * 64]

    def place(name, shape, dt, at=None):
        size = 4
        for s in shape[1:]:
            size *= s
        if at is None:
            at = top[0]
            top[0] += (size + 31) // 32 * 32
            assert top[0] <= end - 32, (name, top[0], end)
        return nc.alloc_sbuf_tensor_at(name, list(shape), dt, offset=at), at

    def sem(name):
        return ctx.enter_context(nc.semaphore(name))

    def slot(name):
        return Slot(sem(name))

    HHI, _ = place("HHI", [P, KT, SEQ], F32R)
    HLO, _ = place("HLO", [P, KT, SEQ], F32R)
    Y, y0 = place("Y", [P, KT, SEQ], F32)
    CLO, _ = place("CLO", [P, KT, CTX], F32R, y0)
    NR, NS = 3, 3
    RAW = [place(f"RAW{i}", [P, 4, 256], F32)[0] for i in range(NR)]
    WHI = [place(f"WHI{i}", [P, 4, 256], F32R)[0] for i in range(NS)]
    WLO = [place(f"WLO{i}", [P, 4, 256], F32R)[0] for i in range(NS)]
    MRAW = [place(f"MRAW{i}", [P, 4, 256], F32)[0] for i in range(2)]
    MACC, _ = place("MACC", [P, 256], F32)
    SQ2 = [place(f"SQ{i}", [P, SEQ], F32)[0] for i in range(2)]
    TM, _ = place("TM", [P, SEQ], F32)
    TY, _ = place("TY", [P, SEQ], F32)
    TT_, _ = place("TT", [P, SEQ], F32)
    IDN, _ = place("IDN", [P, P], F32)
    ONE, _ = place("ONE", [P, P], F32)
    CS, _ = place("CS", [P, SEQ], F32)
    SN, _ = place("SN", [P, SEQ], F32)
    MK, _ = place("MK", [P, 3, P], F32)
    COL, _ = place("COL", [P, 304], F32)
    MOD, _ = place("MOD", [P, 3, 48], F32)
    MODX, _ = place("MODX", [P, 32], F32)
    SC, _ = place("SC", [P, 48], F32)
    SM, _ = place("SM", [P, 64], F32)
    s0 = top[0]
    room = end - 32 - s0

    def scratch(name, shape, dt, off):
        size = 4
        for s in shape[1:]:
            size *= s
        assert off + size <= room, (name, off, size, room)
        return place(name, shape, dt, s0 + off)[0]

    K1 = 1024
    PR = [scratch(f"PR{i}", [P, P], F32, 46 * K1 - 1536 + i * 512) for i in range(3)]
    XN = [scratch(f"XN{i}", [P, D], F32, 16 * K1 + i * 8 * K1) for i in range(3)]
    CT = scratch("CT", [P, KT, CTX], F32, 0)
    KTA = scratch("KTA", [P, 4, 768], F32, 0)
    VV = scratch("VV", [P, 6, 512], F32, 12 * K1)
    PB = [scratch(f"PB{i}", [P, 768], F32, 24 * K1 + i * 3 * K1) for i in range(2)]
    PT = scratch("PT", [P, 6, SEQ], F32, 30 * K1)
    CHI = scratch("CHI", [P, KT, CTX], F32R, 24 * K1)
    ROW = [scratch(f"ROW{i}", [4, 256], F32, 40 * K1 + i * K1) for i in range(2)]
    SCR = scratch("SCR", [P, KT, 4], F32R, 42 * K1)
    SC4 = scratch("SC4", [P, KT, 4], F32, 42 * K1 + 256)
    XR = scratch("XR", [P, KT, SEQ], F32, 0)
    UP = [scratch(f"UP{i}", [P, 4, 544], F32, i * 8704) for i in range(3)]
    PHI = scratch("PHI", [P, 4, SEQ], F32R, 26112)
    PLO = scratch("PLO", [P, 4, SEQ], F32R, 26112 + 8192)
    RC = scratch("RC", [P, SEQ], F32, 26112 + 16384)
    Q2 = [scratch(f"Q2{i}", [P, 2, SEQ], F32, i * 4 * K1) for i in range(2)]
    K2 = [scratch(f"K2{i}", [P, 2, SEQ], F32, 8 * K1 + i * 4 * K1) for i in range(2)]
    V2 = [scratch(f"V2{i}", [P, 4, 256], F32, 16 * K1 + i * 4 * K1) for i in range(2)]
    SPH = scratch("SPH", [P, 1280], F32R, 24 * K1)
    SPL = scratch("SPL", [P, 1280], F32R, 29 * K1)
    DK = scratch("DK", [P, SEQ], F32, 24 * K1)
    LS = scratch("LS", [P, SEQ], F32, 34 * K1)
    LSB = scratch("LSB", [P, SEQ], F32, 36 * K1)
    WB = [scratch(f"WB{i}", [P, SEQ], F32, 38 * K1 + i * 2 * K1) for i in range(2)]
    TA = [scratch(f"TA{i}", [P, SEQ], F32, 42 * K1 + i * 2 * K1) for i in range(2)]
    TRIR = scratch("TRIR", [P, P], F32R, 46 * K1)
    ONER = scratch("ONER", [P, P], F32R, 46 * K1 + 512)

    def bank(name, n=512):
        return ctx.enter_context(nc.psum_tensor(name, [P, n], F32))

    G = [[bank("G0"), bank("G1")], [bank("G2"), bank("G3")]]
    S = bank("S", 1024)
    TB = bank("TB")
    OB = bank("OB")

    pe, act, dve, pool, sp = (Line(sem(n)) for n in ("s_pe", "s_act", "s_dve", "s_pool", "s_sp"))
    s_raw = [slot(f"s_raw{i}") for i in range(NR)]
    s_mraw = [slot(f"s_mraw{i}") for i in range(2)]
    s_par = slot("s_par")
    s_cst = slot("s_cst")
    s_xn = [slot(f"s_xn{i}") for i in range(3)]
    s_rope = slot("s_rope")
    s_tri = slot("s_tri")
    s_spill = slot("s_spill")
    s_back = slot("s_back")
    s_rc = slot("s_rc")
    s_dk = slot("s_dk")
    s_out = [slot(f"s_out{i}") for i in range(2)]
    XS = nc.dram_tensor("x_spill", [P, KT, SEQ], F32)

    def write_out():
        OUT = [HHI, HLO]
        XO, _ = place("XO", [P, 2, D], F32, s0)
        ofree = [None, None]
        tb2 = [TB, OB]
        tf = [tmp["tb"], tmp["ob"]]
        cnt = 0
        for i in range(4):
            r = i % 2
            for q in range(4):
                b = cnt % 2
                cnt += 1
                for j in range(4):
                    k = 4 * q + j
                    m = tr(tb2[b][:, j * P:(j + 1) * P], Y[:, k, i * P:(i + 1) * P], [y_marks[k], tf[b]], sig=j == 3)
                dst = XO[:, r, 512 * q:512 * q + 512]
                if b:
                    tf[b] = vcopy(dst, tb2[b][:, :], [m, ofree[r], y_marks[KT - 1]])
                else:
                    tf[b] = acopy(dst, tb2[b][:, :], [m, ofree[r], y_marks[KT - 1]])
            ofree[r] = pool.dma(out[0, i * P:(i + 1) * P, :], XO[:, r, :], s_out[r], [tf[0], tf[1]])
        last_out = ofree[1]

        with nc.Block() as block:
            @block.sync
            def _(eng):
                sp.emit(eng)

            @block.gpsimd
            def _(eng):
                pool.emit(eng)
                for s in s_out + s_raw + s_mraw:
                    eng.wait_ge(s.sem, s.n)
                eng.wait_ge(s_spill.sem, s_spill.n)

            @block.scalar
            def _(eng):
                act.emit(eng)

            @block.vector
            def _(eng):
                dve.emit(eng)

            @block.tensor
            def _(eng):
                pe.emit(eng)

    def mm(o, l, r, start, stop, after=(), sig=False):
        return pe.do(lambda e: e.matmul(o, l, r, start=start, stop=stop, skip_group_check=True), after, sig)

    def tr(o, i, after=(), sig=False):
        return pe.do(lambda e: e.transpose(o, i, IDN[:, :]), after, sig)

    def af(o, i, f, after=(), bias=0.0, scale=1.0, acc=None):
        if acc is None:
            return act.do(lambda e: e.activation(o, i, f, bias=bias, scale=scale), after)
        return act.do(lambda e: e.activation(o, i, f, bias=bias, scale=scale, accum_out=acc), after)

    def acopy(o, i, after=(), scale=1.0):
        return act.do(lambda e: e.activation(o, i, ACT.Copy, scale=scale), after)

    def tt(o, a, b, op, after=()):
        return dve.do(lambda e: e.tensor_tensor(o, a, b, op), after)

    def ts(o, a, s1, s2, op0, op1, after=()):
        if op1 is None:
            return dve.do(lambda e: e.tensor_scalar(o, a, s1, None, op0), after)
        return dve.do(lambda e: e.tensor_scalar(o, a, s1, s2, op0, op1), after)

    def stt(o, a, s, b, op0, op1, after=()):
        return dve.do(lambda e: e.scalar_tensor_tensor(out=o, in0=a, scalar=s, in1=b, op0=op0, op1=op1), after)

    def vcopy(o, i, after=()):
        return dve.do(lambda e: e.tensor_copy(o, i), after)

    def vset(o, v, after=()):
        return dve.do(lambda e: e.memset(o, v), after)

    def f(t):
        return t.bitcast(F32)

    MUL, ADD, SUB, MAX, MIN = ALU.mult, ALU.add, ALU.subtract, ALU.max, ALU.min

    def weight(w, n0, nk=KT, k0=0):
        return [w[(k0 + c) * P:(k0 + c + 4) * P, n0:n0 + 256].rearrange("(t p) n -> p t n", p=P)
                for c in range(0, nk, 4)]

    ev_w = T["ev_w_in"][0]
    od_w = T["od_w_in"][0]
    w2 = T["w_in_2"][0]
    units = []
    units += [weight(ev_w, 2048 + 256 * i) for i in range(4)]
    for p in range(8):
        units += [weight(ev_w, 3072 + 256 * p), weight(ev_w, 256 * p)]
    units += [weight(T["ev_w_out"][0], 256 * i) for i in range(8)]
    for g in range(4):
        units += [weight(od_w, 512 * g), weight(od_w, 512 * g + 256)]
        units += [weight(od_w, 2048 + 512 * g), weight(od_w, 2048 + 512 * g + 256)]
        units += [weight(T["od_pool_w"][0, g], 0, 4), weight(T["od_pool_w"][0, g], 256, 4)]
    units += [weight(T["od_w_out"][0], 256 * i) for i in range(8)]
    for p in range(4):
        units += [weight(w2, 1024 * i + 256 * p) for i in range(4)]
    for p in range(4):
        units += [weight(w2, 4096 + 1024 * i + 256 * p) for i in range(4)]
    units += [weight(T["w_out_2"][0], 256 * i) for i in range(8)]
    chunks = [c for u in units for c in u]
    raw_free = [None] * NR
    split_free = [None] * NS
    loaded = {}
    split = {}
    at = {"load": 0, "split": 0, "use": 0, "unit": 0}

    def load_next():
        i = at["load"]
        if i < len(chunks):
            loaded[i] = sp.dma(RAW[i % NR][:, :, :], chunks[i], s_raw[i % NR], [raw_free[i % NR]])
            at["load"] += 1

    def split_next():
        i = at["split"]
        if i < len(chunks):
            r, s = i % NR, i % NS
            a = acopy(WHI[s][:, :, :], RAW[r][:, :, :], [loaded[i], split_free[s]])
            b = tt(WLO[s][:, :, :], RAW[r][:, :, :], f(WHI[s][:, :, :]), SUB, [a])
            raw_free[r] = b
            split[i] = (a, b)
            at["split"] += 1
            load_next()

    background = []

    def step(gens):
        for g in list(gens):
            try:
                next(g)
            except StopIteration:
                if g in background:
                    background.remove(g)

    def finish(g):
        if g in background:
            for _ in g:
                pass
            background.remove(g)

    bank_free = [[None, None], [None, None]]

    def unit(work):
        u = at["unit"]
        at["unit"] += 1
        nch = len(units[u])
        done = None
        for c in range(nch):
            i = at["use"]
            at["use"] += 1
            while at["split"] < min(i + NS, len(chunks)) and at["split"] <= i:
                split_next()
            s = i % NS
            after = list(split[i])
            done = work(4 * c, WHI[s], WLO[s], c == 0, c == nch - 1, after)
            split_free[s] = done
            while at["split"] < min(i + NS, len(chunks)):
                split_next()
            step([mods])
        return done

    def gemm(hi, lo, ready, extra=None):
        pair = at["unit"] % 2
        banks, free = G[pair], bank_free[pair]

        def work(k0, wh, wl, first, last, after):
            done = None
            for nt in range(2):
                cols = slice(nt * P, nt * P + P)
                for j in range(4):
                    k = k0 + j
                    w = after + [m for m in ready[k]]
                    if first and j == 0:
                        w = w + [free[nt]]
                    o = banks[nt][:, :]
                    a, b = wh[:, j, cols], wl[:, j, cols]
                    end = last and j == 3
                    fin = nt == 1 and j == 3
                    mm(o, a, hi[:, k, :], first and j == 0, False, w)
                    mm(o, a, lo[:, k, :], False, False)
                    done = mm(o, b, hi[:, k, :], False, end, sig=(fin or end) and extra is None)
                    if extra is not None:
                        eo, ehi, elo, eready, efree = extra
                        w = [m for m in eready[k]]
                        if first and j == 0 and nt == 0:
                            w = w + [efree]
                        mm(eo(nt), a, ehi[:, k, :], first and j == 0 and nt == 0, False, w)
                        mm(eo(nt), a, elo[:, k, :], False, False)
                        done = mm(eo(nt), b, ehi[:, k, :], False, end, sig=fin or end)
                    if end and nt == 0:
                        half.append(done)
                    if j % 2:
                        step(background)
            return done

        half = []
        done = unit(work)
        return pair, banks, [half[0], done]

    def gemm_tok(tiles, outs, frees):
        def work(k0, wh, wl, first, last, after):
            done = None
            for i, (hi, lo, ready) in enumerate(tiles):
                for j in range(4):
                    k = k0 + j
                    w = after + [m for m in ready[k]]
                    begin = first and j == 0 and i % 2 == 0
                    if begin:
                        w = w + [frees[i // 2]]
                    mm(outs(i), hi(k), wh[:, j, :], begin, False, w)
                    mm(outs(i), lo(k), wh[:, j, :], False, False)
                    done = mm(outs(i), hi(k), wl[:, j, :], False, last and j == 3,
                              sig=i == len(tiles) - 1 and j == 3)
                step(background)
            return done

        return unit(work)

    pool.dma(IDN[:, :], T["t_sq"][0], s_cst)
    m_cst = pool.dma(ONE[:, :], T["t_sq"][1], s_cst)
    z0 = vset(PR[1][:, :], 0.0)
    z1 = vset(PR[2][:, :], 0.0)

    def params(pr, r, src, n, after=()):
        return pool.dma(PR[pr][r:r + n, :], src.rearrange("(t p) -> t p", p=P), s_par, after)

    params(0, 0, T["c"][0], 16)
    params(0, 16, T["c_ctx"], 16)
    params(0, 32, T["c_2"][0], 16)
    params(0, 48, T["ev_pre_g"][0], 16)
    params(0, 64, T["ev_post_g"][0], 16)
    params(0, 80, T["od_pre_g"][0], 16)
    params(0, 96, T["od_post_g"][0], 16)
    params(0, 112, T["norm_gain_2"][0], 16)
    params(1, 0, T["od_pool_scale"][0], 16, [z0, z1])
    params(1, 16, T["ret_norm_gain_2"][0], 8)
    params(1, 24, T["ev_q_norm"][0], 1)
    params(1, 25, T["ev_k_norm"][0], 1)
    params(1, 26, T["sb_q_gain_2"][0], 1)
    params(1, 27, T["sb_k_gain_2"][0], 1)
    params(1, 32, T["ev_mod_b"][0], 48)
    params(1, 80, T["od_mod_b"][0], 48)
    params(2, 0, T["b_ada_2"][0], 48)
    pool.dma(SM[0:4, 40:42], T["t_r4"], s_par)
    m_par = pool.dma(SM[0:1, 0:8], T["ev_sink"], s_par)
    m_xn = [pool.dma(XN[i][:, :], T["ctx"][0, i * P:(i + 1) * P, :], s_xn[i]) for i in range(2)]
    m_xn.append(pool.dma(XN[2][:, :], T["x"][0, 0:P, :], s_xn[2]))
    m_rope = pool.dma(CS[:, :], T["t_rope_a"][0], s_rope)
    m_rope = pool.dma(SN[:, :], T["t_rope_a"][1], s_rope)
    m_mk = pool.dma(MK[:, 0:2, :], T["t_mask"].rearrange("a p n -> p a n"), s_tri)

    act.do(lambda e: e.add_instruction(mybir.InstLoadActFuncSet(
        act_func_set_id=NAT_LOG_EXP, name=nc.get_next_instruction_name(),
        engine=mybir.EngineType.Activation, ins=[], outs=[])), (), False)

    tr(TB[:, 0:P], PR[0][:, :], [m_cst, m_par])
    tr(TB[:, P:2 * P], PR[1][:, :])
    tr(TB[:, 2 * P:3 * P], PR[2][:, :])
    m_t = mm(TB[:, 384:392], ONE[0:1, :], SM[0:1, 0:8], True, True, sig=True)
    m_col = vcopy(COL[:, :], TB[:, 0:304], [m_t])
    m_snk = ts(SM[:, 8:16], TB[:, 384:392], -1.0, None, MUL, None, [m_t])
    m_snk = ts(SM[:, 16:24], TB[:, 384:392], 1.0, None, MUL, None, [m_snk])

    a1 = af(SC[:, :], COL[:, 0:48], ACT.Abs, [m_col])
    a1 = af(SC[:, :], SC[:, :], ACT.Exp, [a1], scale=-1.0)
    a1 = af(SC[:, :], SC[:, :], ACT.Ln, [a1], bias=1.0)
    d1 = stt(SC[:, :], COL[:, 0:48], 0.0, SC[:, :], MIN, SUB, [a1])
    a1 = af(SC[:, :], SC[:, :], ACT.Exp, [d1])
    m_sc = tt(SC[:, :], COL[:, 0:48], SC[:, :], MUL, [a1])
    scv = SC[:, :].rearrange("p (v k) -> p k v", k=KT)[:, :, 0:2]
    z2 = vset(SC4[:, :, :], 0.0, [m_col])
    z2 = vcopy(SC4[:, :, 0:2], scv, [z2, m_sc])
    a1 = acopy(SCR[:, :, 0:2], scv, [m_sc])
    m_scr4 = tt(SCR[:, :, 2:4], scv, f(SCR[:, :, 0:2]), SUB, [a1, z2])

    tmp = {"sq": [None, None], "chain": None, "tb": m_snk, "ob": None}


    def rstd(n, bank_ap, m_stat, count, extra=()):
        m = ts(TM[:, 0:n], bank_ap, 1.0 / count, EPS, MUL, ADD, [m_stat, tmp["chain"]] + list(extra))
        a = af(TY[:, 0:n], TM[:, 0:n], ACT.Ln, [m])
        a = af(TY[:, 0:n], TY[:, 0:n], ACT.Exp, [a], scale=-0.5)
        b = tt(TT_[:, 0:n], TY[:, 0:n], TY[:, 0:n], MUL, [a])
        b = stt(TT_[:, 0:n], TT_[:, 0:n], -0.5, TM[:, 0:n], MUL, MUL, [b])
        b = stt(TY[:, 0:n], TT_[:, 0:n], 1.5, TY[:, 0:n], ADD, MUL, [b])
        return m, b

    nat = [("c", 0), ("c", 1)] + [("x", i) for i in range(4)]
    xs = {}

    def x_prep():
        ring = [None] * 3
        bank2, key = [TB, OB], ["tb", "ob"]
        cnt = 0
        for n, (what, i) in enumerate(nat):
            r = n % 3
            if n >= 3:
                m_xn.append(pool.dma(XN[r][:, :], T["x"][0, i * P:(i + 1) * P, :], s_xn[r], [ring[r]]))
            for q in range(4):
                b = cnt % 2
                for j in range(4):
                    k = 4 * q + j
                    m = tr(bank2[b][:, j * P:(j + 1) * P], XN[r][:, k * P:(k + 1) * P],
                           [m_xn[n], tmp[key[b]], m_cst], sig=j == 3)
                dst = (CT if what == "c" else Y)[:, 4 * q:4 * q + 4, i * P:(i + 1) * P]
                src = bank2[b][:, :].rearrange("p (j n) -> p j n", j=4)
                if b:
                    tmp["ob"] = vcopy(dst, src, [m])
                else:
                    tmp["tb"] = acopy(dst, src, [m])
                cnt += 1
                if q % 2:
                    yield
            ring[r] = m
        both = [tmp["tb"], tmp["ob"]]
        xs["in"] = [m]
        xs["spill"] = pool.dma(XS.ap(), Y[:, :, :], s_spill, both)
        for name, tiles, n, bank_, key_ in (("x", Y, SEQ, TB, "tb"), ("c", CT, CTX, OB, "ob")):
            m = None
            for k in range(KT):
                m = stat_tile(tiles, n, k, both, bank_, tmp[key_])
                if k % 2:
                    yield
            tmp[key_], y_ = rstd(n, bank_[:, 0:n], m, D)
            yield
            for k in range(KT):
                if name == "x":
                    d = tt(Y[:, k, :], Y[:, k, :], TY[:, 0:n], MUL, [y_, xs["spill"]])
                else:
                    d = tt(CT[:, k, :], CT[:, k, :], TY[:, 0:n], MUL, [y_])
                if k % 2:
                    yield
            tmp["chain"] = d
            xs[name] = d
        yield

    def stat_tile(tiles, n, k, ready, bank, free):
        s = k % 2
        a = af(SQ2[s][:, 0:n], tiles[:, k, 0:n], ACT.Square, list(ready) + [tmp["sq"][s]])
        m = mm(bank[:, 0:n], ONE[:, :], SQ2[s][:, 0:n], k == 0, k == KT - 1, [a, free], sig=True)
        tmp["sq"][s] = m
        return m

    h_ready, hc_ready = [None] * KT, [None] * KT

    def split_tile(k, src, n, gain, shift, hi, lo, after, ready):
        s = k % 2
        d = ts(SQ2[s][:, 0:n], src, gain, shift, MUL, ADD, [tmp["sq"][s]] + list(after))
        a = act.do(lambda e: e.activation(hi, src, ACT.Identity, bias=shift, scale=gain), list(after))
        d = tt(lo, SQ2[s][:, 0:n], f(hi), SUB, [d, a])
        tmp["sq"][s] = d
        ready[k] = [d]
        return d

    ev_mw = T["ev_mod_w"][0]
    rings, rsem, rfree = RAW + MRAW, s_raw + s_mraw, [None] * 5
    order = [nb for i in range(8) for nb in (i, 8 + i)]
    jobs0 = [(nb, c) for nb in order for c in range(4)]
    arrived, parts0, sfree0 = {}, {}, [None] * NS
    rows_free, cols_free, row_m = [None, None], [None, None], {}
    mfree = [None, None]

    def direct(i):
        return i % 4 == 3

    nsplit = [0]

    def mod_load(i):
        if i < len(jobs0):
            nb, c = jobs0[i]
            arrived[i] = sp.dma(rings[i % 5][:, :, :], weight(ev_mw, 256 * nb)[c], rsem[i % 5], [rfree[i % 5]])

    def mod_split(i):
        if i < len(jobs0) and not direct(i):
            r, q = i % 5, nsplit[0] % NS
            nsplit[0] += 1
            a = acopy(WHI[q][:, :, :], rings[r][:, :, :], [arrived[i], sfree0[q]])
            b = tt(WLO[q][:, :, :], rings[r][:, :, :], f(WHI[q][:, :, :]), SUB, [a])
            parts0[i] = (q, b)
            rfree[r] = b

    def mod_cols(n):
        nb, b, a = row_m.pop(n)
        o = G[1][b]
        for nt in range(2):
            m = mm(o[:, 2 * nt:2 * nt + 2], ROW[b][:, nt * P:(nt + 1) * P], SM[0:4, 40:42], nt == 0, nt == 1,
                   [a, cols_free[b], m_par], sig=nt == 1)
        rows_free[b] = m
        v = o[:, 0:4].rearrange("p (n v) -> p v n", v=2)
        d = tt(MOD[:, 0, 2 * nb:2 * nb + 2], v[:, 0, :], COL[:, 160 + 2 * nb:162 + 2 * nb], ADD, [m, m_col])
        d = tt(MODX[:, 2 * nb:2 * nb + 2], v[:, 1, :], COL[:, 160 + 2 * nb:162 + 2 * nb], ADD, [m, d])
        cols_free[b] = d
        if nb >= 8:
            k = 2 * nb - 16
            d = stt(MOD[:, 0, 16 + k:18 + k], MOD[:, 0, 16 + k:18 + k], 1.0, COL[:, 48 + k:50 + k], ADD, MUL, [d])
            d = stt(MODX[:, 16 + k:18 + k], MODX[:, 16 + k:18 + k], 1.0, COL[:, 48 + k:50 + k], ADD, MUL, [d])
            queue.extend([(k, d), (k + 1, d)])

    queue = []

    def h_tile():
        k, d = queue.pop(0)
        m = split_tile(k, Y[:, k, :], SEQ, MOD[:, 0, 16 + k:17 + k], MOD[:, 0, k:k + 1], HHI[:, k, :],
                       HLO[:, k, :], [d, xs["x"]], h_ready)
        split_tile(k, CT[:, k, :], CTX, MODX[:, 16 + k:17 + k], MODX[:, k:k + 1], CHI[:, k, :], CLO[:, k, :],
                   [d, xs["c"], m] + xs["in"], hc_ready)

    prep = x_prep()
    for i in range(5):
        mod_load(i)
    for i in range(2):
        mod_split(i)
    last_q = None
    for i, (nb, c) in enumerate(jobs0):
        n, r = i // 4, i % 5
        b = n % 2
        mod_split(i + 2)
        row = G[0][b][0:4, 0:256]
        for j in range(4):
            first, end = c == 0 and j == 0, c == 3 and j == 3
            if direct(i):
                m = mm(row, SC4[:, 4 * c + j, :], rings[r][:, j, :], first, end,
                       [arrived[i], m_scr4, mfree[b]], sig=j == 3)
            else:
                q, w = parts0[i]
                mm(row, SCR[:, 4 * c + j, :], WHI[q][:, j, :], first, False, [w, m_scr4, mfree[b]])
                m = mm(row, SCR[:, 4 * c + j, :], WLO[q][:, j, :], False, end, sig=j == 3)
        if direct(i):
            rfree[r] = m
        else:
            sfree0[q] = m
        mod_load(i + 5)
        if c == 3:
            a = acopy(ROW[b][:, :], row, [m, rows_free[b]])
            mfree[b] = a
            row_m[n] = (nb, b, a)
        if c == 1 and n > 0:
            mod_cols(n - 1)
        for _ in range(2):
            next(prep, None)
        if "c" in xs and queue:
            h_tile()
    for _ in prep:
        pass
    mod_cols(len(order) - 1)
    while queue:
        h_tile()
    for q in range(NS):
        split_free[q] = sfree0[q]
    for r in range(NR):
        raw_free[r] = rfree[r]
    mraw_free = [rfree[3], rfree[4]]
    bank_free[0] = [mfree[0], mfree[1]]
    bank_free[1] = [cols_free[0], cols_free[1]]
    m_spill = xs["spill"]

    mod_jobs = [("ev", T["ev_mod_w"][0], 0, 0, 16, 24, 160), ("od", T["od_mod_w"][0], 1, 0, 0, 24, 208),
                ("w2", T["w_ada_2"][0], 2, 32, 0, 24, 256)]
    mod_done = {}

    def mod_stream():
        n = 0
        acc_free = None
        last = None
        for name, w, layer, c0, nb0, nb1, bias in mod_jobs:
            for nb in range(nb0, nb1):
                d = None
                for c in range(4):
                    r = n % 2
                    n += 1
                    m_l = sp.dma(MRAW[r][:, :, :], weight(w, 256 * nb)[c], s_mraw[r], [mraw_free[r]])
                    yield
                    if c == 0 and last is not None:
                        acc_free = mod_reduce(*last)
                    for j in range(4):
                        col = SC[:, c0 + 4 * c + j:c0 + 4 * c + j + 1]
                        if c == 0 and j == 0:
                            d = ts(MACC[:, :], MRAW[r][:, j, :], col, None, MUL, None, [m_l, m_sc, acc_free])
                        else:
                            d = stt(MACC[:, :], MRAW[r][:, j, :], col, MACC[:, :], MUL, ADD, [m_l, d])
                    mraw_free[r] = d
                last = (name, nb, layer, bias, d)
        yield
        mod_reduce(*last)
        yield

    def mod_reduce(name, nb, layer, bias, d):
        mm(TB[:, 0:1], MACC[:, 0:P], ONE[:, 0:1], True, True, [d, tmp["tb"]])
        m = mm(TB[:, 1:2], MACC[:, P:2 * P], ONE[:, 0:1], True, True, sig=True)
        v = tt(MOD[:, layer, 2 * nb:2 * nb + 2], TB[:, 0:2], COL[:, bias + 2 * nb:bias + 2 * nb + 2], ADD, [m])
        tmp["tb"] = v
        mod_done[(name, nb)] = v
        return m

    load_next()
    load_next()
    load_next()
    mods = mod_stream()
    m_hc = hc_ready[KT - 1][0]

    def norm_rope(src, dst, n, gcol, rope, after, fin):
        a = af(SQ2[1][:, 0:n], src, ACT.Square, list(after) + [tmp["sq"][1]])
        yield
        if gcol is not None:
            m = mm(TB[:, 0:n], ONE[:, :], SQ2[1][:, 0:n], True, True, [a, tmp["tb"]], sig=True)
            tmp["sq"][1] = m
            mm_, y = rstd(n, TB[:, 0:n], m, 128)
            tmp["tb"] = mm_
            yield
            d = stt(TM[:, 0:n], src, gcol, TY[:, 0:n], MUL, MUL, [y])
            cur = TM[:, 0:n]
            tmp["chain"] = d
        else:
            tmp["sq"][1] = a
            cur, d = src, a
        if rope:
            h = 64
            cl = cur
            d1 = tt(TT_[h:P, 0:n], cl[0:h, :], SN[0:h, 0:n], MUL, [d, m_rp[0], tmp["chain"]] + list(after))
            d2 = tt(TT_[0:h, 0:n], cl[h:P, :], SN[h:P, 0:n], MUL, [d1])
            d3 = tt(dst, cur, CS[:, 0:n], MUL, [d2])
            d4 = tt(dst, dst, TT_[:, 0:n], ADD, [d3])
        else:
            d4 = vcopy(dst, cur, [d])
        tmp["chain"] = d4
        fin.append(d4)
        yield

    def run(g):
        for _ in g:
            pass

    m_rp = [m_rope]

    ctx_place = lambda nt: OB[:, nt * CTX:(nt + 1) * CTX]
    kv_marks = []
    scr_free = [m_hc]
    x_tiles = [(lambda k, i=i: HHI[:, k, i * P:(i + 1) * P], lambda k, i=i: HLO[:, k, i * P:(i + 1) * P], h_ready)
               for i in range(4)]
    c_tiles = [(lambda k, i=i: CHI[:, k, i * P:(i + 1) * P], lambda k, i=i: CLO[:, k, i * P:(i + 1) * P], hc_ready)
               for i in range(2)]
    for side in range(2):
        pair, banks, done = gemm(HHI, HLO, h_ready, (ctx_place, CHI, CLO, hc_ready, tmp["ob"]))
        ev = []
        for nt in range(2):
            kh = 2 * side + nt
            a = acopy(KTA[:, kh, 0:SEQ], banks[nt][:, :], [done[1]] + scr_free)
            bank_free[pair][nt] = a
            a2 = acopy(KTA[:, kh, SEQ:768], ctx_place(nt), [done[1]])
            tmp["ob"] = a2
            ev.append((kh, a, a2))
        parts = []
        for kh, a, a2 in ev:
            if side == 0:
                parts.append(chain([
                    norm_rope(KTA[:, kh, 0:SEQ], KTA[:, kh, 0:SEQ], SEQ, COL[:, 153:154], True, [a], kv_marks),
                    norm_rope(KTA[:, kh, SEQ:768], KTA[:, kh, SEQ:768], CTX, COL[:, 153:154], False, [a2],
                              kv_marks)]))
            else:
                parts.append(norm_rope_copy(norm_rope, KTA, kh, SQ2, tmp, a, kv_marks, vcopy))
        task = chain(parts)
        background.append(task)
        pair = at["unit"] % 2
        outs = [G[pair][0][:, 0:256], G[pair][0][:, 256:512], G[pair][1][:, 0:256], G[pair][1][:, 256:512],
                OB[:, 0:256], OB[:, 256:512]]
        done = gemm_tok(x_tiles + c_tiles, lambda i: outs[i],
                        [bank_free[pair][0], bank_free[pair][1], tmp["ob"]])
        for i, b in enumerate([G[pair][0], G[pair][1], OB]):
            a = acopy(VV[:, 2 * i:2 * i + 2, side * 256:side * 256 + 256],
                      b[:, :].rearrange("p (t n) -> p t n", t=2), [done] + scr_free)
            if i < 2:
                bank_free[pair][i] = a
            else:
                tmp["ob"] = a
            kv_marks.append(a)
        finish(task)
    m_ctx_read = done

    buf = {"qt": None, "pb": [None, None], "pt": None, "s": None, "nm": 0}

    def score_rows(h, q, qt, ready):
        band = h >= 8
        kv = (h // 4) if not band else 2 + (h - 8) // 4
        kt_ = KTA[:, kv, :]
        b = buf["nm"] % 2
        lq = QR[:, q, qt * P:(qt + 1) * P]
        need = [buf["s"]] + ready + kv_marks
        if not band:
            mm(S[:, 0:512], lq, kt_[:, 0:512], True, True, need)
            m = mm(S[:, 512:768], lq, kt_[:, 512:768], True, True, sig=True)
            lo_ = 0
            jobs = [(j, j * P) for j in range(6)]
        else:
            t0, t1 = max(0, qt - 1), min(3, qt + 1)
            nb = t1 - t0 + 1
            lo_ = 512 - nb * P
            mm(S[:, lo_:512], lq, kt_[:, t0 * P:(t1 + 1) * P], True, True, need)
            m = mm(S[:, 512:768], lq, kt_[:, 512:768], True, True, sig=True)
            if qt > 0:
                m = tt(S[:, lo_:lo_ + P], S[:, lo_:lo_ + P], MK[:, 0, :], ADD, [m, m_mk])
            if qt < 3:
                m = tt(S[:, 384:512], S[:, 384:512], MK[:, 1, :], ADD, [m, m_mk])
            jobs = [(t0 + j, lo_ + j * P) for j in range(nb)] + [(4, 512), (5, 640)]
        m_q = (pe.sem, pe.n)
        i = 24 + 4 * (buf["nm"] % 4)
        buf["nm"] += 1
        nm, rs = SM[:, i:i + 1], SM[:, i + 1:i + 2]
        src = S[:, lo_:768]
        d = dve.do(lambda e: e.tensor_reduce(nm, src, AX_X, MAX, negate=True), [m])
        if band:
            d = ts(nm, nm, SM[:, h:h + 1], None, MIN, None, [d, m_snk])
        a = af(PB[b][:, lo_:768], src, ACT.Exp, [d, buf["pb"][b], m_ctx_read], bias=nm, acc=rs)
        buf["s"] = a
        if band:
            es = SM[:, i + 2:i + 3]
            a2 = af(es, SM[:, 8 + h:9 + h], ACT.Exp, [a], bias=nm)
            d = tt(rs, rs, es, ADD, [a2])
        else:
            d = a
        d = dve.do(lambda e: e.reciprocal(rs, rs), [d])
        m_p = ts(PB[b][:, lo_:768], PB[b][:, lo_:768], rs, None, MUL, None, [d])
        return (qt, b, jobs, m_p), m_q

    def spread(qt, b, part, m_p, final):
        for x_, (j, c0) in enumerate(part):
            mt = tr(TB[:, x_ * P:(x_ + 1) * P], PB[b][:, c0:c0 + P], [m_p, tmp["tb"]], sig=x_ == len(part) - 1)
        if final:
            buf["pb"][b] = mt
        runs = []
        for x2, (j, c0) in enumerate(part):
            if runs and runs[-1][1] + runs[-1][2] == j:
                runs[-1][2] += 1
            else:
                runs.append([x2, j, 1])
        for x2, j, n in runs:
            dst = PT[:, j:j + n, qt * P:(qt + 1) * P]
            src = TB[:, x2 * P:(x2 + n) * P].rearrange("p (j n) -> p j n", j=n)
            tmp["tb"] = acopy(dst, src, [mt, buf["pt"], tmp["tb"]])
        return tmp["tb"]

    def values(h, last):
        band = h >= 8
        kv = (h // 4) if not band else 2 + (h - 8) // 4
        vcol = slice(kv * P, kv * P + P)
        for n, j in enumerate([4, 5, 0, 1, 2, 3]):
            c = slice(0, 512) if j > 3 or not band else slice(max(0, j - 1) * P, min(4, j + 2) * P)
            m = mm(OB[:, c], VV[:, j, vcol], PT[:, j, c], n == 0, n == 5, [last, tmp["ob"]], sig=n == 5)
        buf["pt"] = m
        return m

    def silu_mul(dst, z, done, after):
        s = 0
        a = af(SQ2[s][:, :], z, ACT.Abs, [done, tmp["sq"][s]])
        a = af(SQ2[s][:, :], SQ2[s][:, :], ACT.Exp, [a], scale=-1.0)
        a = af(SQ2[s][:, :], SQ2[s][:, :], ACT.Ln, [a], bias=1.0)
        d = stt(SQ2[s][:, :], z, 0.0, SQ2[s][:, :], MIN, SUB, [a])
        a = af(SQ2[s][:, :], SQ2[s][:, :], ACT.Exp, [d])
        d = tt(dst, z, SQ2[s][:, :], MUL, [a] + list(after))
        tmp["sq"][s] = d
        return d

    QR = scratch("QR", [P, 2, SEQ], F32, 42 * K1)
    y_marks = [None] * KT
    qr_free = [None, None]
    task_rows = []
    z_marks = [None] * KT

    def pair_task(p, qm):
        gens, ready = [], []
        for i in range(2):
            fin = []
            src = QR[:, i, :]
            gens.append(norm_rope(src, src, SEQ, COL[:, 152:153] if p < 4 else None, True, [qm[i], qm[2]], fin))
            ready.append(fin)
        for g in gens:
            for _ in g:
                yield
        events = {}

        def plan(t, fn):
            events.setdefault(t, []).append(fn)

        def rows(t, n):
            i, qt = divmod(n, 4)
            task_rows.append(n)
            (qt, b, jobs, m_p), qr_free[i] = score_rows(2 * p + i, i, qt, ready[i])
            two = len(jobs) > 4
            plan(t + 3, lambda: spread(qt, b, jobs[:4], m_p, not two))
            if two:
                plan(t + 4, lambda: spread(qt, b, jobs[4:], m_p, True))
            if qt == 3:
                plan(t + 5, lambda: pv(t + 5, 2 * p + i))

        def pv(t, h):
            m = values(h, tmp["tb"])
            plan(t + 1, lambda: gate_y(h, m))

        def gate_y(h, m):
            tmp["ob"] = tt(Y[:, h, :], OB[:, :], Y[:, h, :], MUL, [m, z_marks[h]])
            y_marks[h] = tmp["ob"]

        for n in range(8):
            plan(3 * n, lambda n=n: rows(3 * n, n))
        t = 0
        while events:
            for fn in reversed(events.pop(t, [])):
                fn()
            t += 1
            yield

    m_qs = ts(COL[:, 152:153], COL[:, 152:153], SCALE, None, MUL, None, [m_col])
    task = None
    for p in range(8):
        pair, banks, done = gemm(HHI, HLO, h_ready)
        for nt in range(2):
            z_marks[2 * p + nt] = silu_mul(Y[:, 2 * p + nt, :], banks[nt][:, :], done[nt], [m_ctx_read])
            bank_free[pair][nt] = z_marks[2 * p + nt]
        pair, banks, done = gemm(HHI, HLO, h_ready)
        while task is not None and task in background and len(task_rows) < 8 * p:
            step(background)
        qm = []
        for nt in range(2):
            a = acopy(QR[:, nt, :], banks[nt][:, :], [done[nt], qr_free[nt], m_ctx_read], scale=SCALE if p >= 4 else 1.0)
            bank_free[pair][nt] = a
            qm.append(a)
        task = pair_task(p, qm + [m_qs])
        background.append(task)
    m_h_read = done[1]
    for g in list(background):
        finish(g)

    def project_out(post, gate, m_gate, x_free):
        back = pool.dma(XR[:, :, :], XS.ap(), s_back, list(x_free))
        ready = []
        for k in range(KT):
            a = acopy(HHI[:, k, :], Y[:, k, :], [y_marks[k], m_h_read_[0]])
            d = tt(HLO[:, k, :], Y[:, k, :], f(HHI[:, k, :]), SUB, [a])
            ready.append([d])
        all_split = ready[-1][0]
        stat = None
        sq_m = []

        def stat_mm(k):
            m = mm(OB[:, :], ONE[:, :], SQ2[k % 2][:, :], k == 0, k == KT - 1, [sq_m[k], tmp["ob"]], sig=True)
            tmp["sq"][k % 2] = m
            return m

        def late():
            for _ in range(3):
                yield
            for k in (len(sq_m) - 2, len(sq_m) - 1):
                stat_mm(k)
                yield

        for u in range(8):
            pair, banks, done = gemm(HHI, HLO, ready)
            for nt in range(2):
                k = 2 * u + nt
                if post:
                    a2 = af(SQ2[nt][:, :], banks[nt][:, :], ACT.Square, [done[nt], tmp["sq"][nt]])
                    a = act.do(lambda e, k=k, b=banks[nt]: e.activation(Y[:, k, :], b[:, :], ACT.Copy,
                                                                        scale=gate(k)),
                               [done[nt], all_split, m_gate()])
                    bank_free[pair][nt] = a
                    sq_m.append(a2)
                    y_marks[k] = a
                else:
                    d = stt(Y[:, k, :], banks[nt][:, :], gate(k), XR[:, k, :], MUL, ADD,
                            [done[nt], m_gate(), all_split, back])
                    bank_free[pair][nt] = d
                    y_marks[k] = d
            if post and u < 7:
                background.append(late())
        m_h_read_[0] = done[1]
        if post:
            for g in list(background):
                finish(g)
            stat_mm(KT - 2)
            stat = stat_mm(KT - 1)
            m1, y_ = rstd(SEQ, OB[:, :], stat, D)
            tmp["ob"] = m1
            for k in range(KT):
                d = tt(Y[:, k, :], Y[:, k, :], TY[:, :], MUL, [y_, y_marks[k]])
                if k % 4 == 3:
                    y_marks[k] = pool.do(lambda e, k=k: e.tensor_tensor(Y[:, k, :], Y[:, k, :], XR[:, k, :], ADD),
                                         [d, back])
                else:
                    y_marks[k] = tt(Y[:, k, :], Y[:, k, :], XR[:, k, :], ADD, [d, back])
                if k % 4 == 3:
                    order_x[k - 3:k + 1] = [k - 3, k - 2, k - 1, k]
            tmp["chain"] = d

    order_x = list(range(KT))

    m_h_read_ = [m_h_read]
    gcol = {}

    def need_mods(name, nb):
        while (name, nb) not in mod_done:
            next(mods)
        return mod_done[(name, nb)]

    m = need_mods("ev", 23)
    m_gate0 = tt(MOD[:, 0, 32:48], MOD[:, 0, 32:48], COL[:, 64:80], MUL, [m])
    project_out(True, lambda k: MOD[:, 0, 32 + k:33 + k], lambda: m_gate0, [buf["pt"]])

    def next_layer(layer, gain, after_x):
        sp_ = pool.dma(XS.ap(), Y[:, :, :], s_spill, y_marks + [m_back_all()])
        for k in range(KT):
            m_s = stat_tile(Y, SEQ, k, [y_marks[k]], OB, tmp["ob"])
        m1, y_ = rstd(SEQ, OB[:, :], m_s, D)
        tmp["ob"] = m1
        g = stt(MOD[:, layer, 16:32], MOD[:, layer, 16:32], 1.0, gain, ADD, MUL, [after_x])
        ready = [None] * KT
        for k in range(KT):
            s = k % 2
            d = tt(SQ2[s][:, :], Y[:, k, :], TY[:, :], MUL, [y_, tmp["sq"][s]])
            a = act.do(lambda e, k=k, s=s: e.activation(HHI[:, k, :], SQ2[s][:, :], ACT.Identity,
                                                        bias=MOD[:, layer, k:k + 1],
                                                        scale=MOD[:, layer, 16 + k:17 + k]), [d, m_h_read_[0], g])
            d = ts(TT2[s][:, :], SQ2[s][:, :], MOD[:, layer, 16 + k:17 + k], MOD[:, layer, k:k + 1], MUL, ADD,
                   [d, g, tt2_free[s]])
            d = tt(HLO[:, k, :], TT2[s][:, :], f(HHI[:, k, :]), SUB, [a, d])
            tmp["sq"][s] = d
            tt2_free[s] = d
            ready[k] = [d]
        tmp["chain"] = d
        return sp_, ready, d

    TT2 = [TM, TT_]
    tt2_free = [None, None]

    def m_back_all():
        return (s_back.sem, s_back.n)

    m = need_mods("od", 15)
    m_spill, h_ready, m_h = next_layer(1, COL[:, 80:96], m)

    pad = [vset(UP[i][:, :, :], 0.0, [y_marks[KT - 1]]) for i in range(3)]
    up_free = [None]
    ph_free = [None]
    pooled = [None]
    m_scr = y_marks[KT - 1]
    n_rc = [None]

    def pool_group(g, ev):
        rc = pool.dma(RC[:, :], T["t_rcnt"][g], s_rc, [n_rc[0], m_scr])
        cur = 0
        lo_, hi_ = 1, 544
        d = tt(UP[1][:, :, 1:544], UP[0][:, :, 0:543], UP[0][:, :, 1:544], ADD, ev + [up_free[0]])
        cur = 1
        yield
        sh = 1
        for lv in range(g):
            nxt = 2 if cur == 1 else 1
            a, b = lo_ + sh, hi_ - sh
            d = tt(UP[nxt][:, :, a:b], UP[cur][:, :, a - sh:b - sh], UP[cur][:, :, a + sh:b + sh], ADD, [d])
            lo_, hi_ = a, b
            sh *= 2
            cur = nxt
            yield
        o = 2 if cur == 1 else 1
        dst = UP[o][:, :, 16:528]
        for j in range(4):
            d = tt(dst[:, j, :], UP[cur][:, j, 16:528], RC[:, :], MUL, [d, rc])
        n_rc[0] = d
        d = tt(dst, dst, UP[0][:, :, 16:528], SUB, [d])
        yield
        a = acopy(PHI[:, :, :], dst, [d, ph_free[0]])
        d = tt(PLO[:, :, :], dst, f(PHI[:, :, :]), SUB, [a])
        up_free[0] = d
        pooled[0] = d
        yield

    for g in range(4):
        ev = []
        for u in range(2):
            pair, banks, done = gemm(HHI, HLO, h_ready)
            for nt in range(2):
                a = acopy(UP[0][:, 2 * u + nt, 16:528], banks[nt][:, :], [done[nt], pad[2], up_free[0]])
                bank_free[pair][nt] = a
                ev.append(a)
        task = pool_group(g, [ev[-1]])
        background.append(task)
        for u in range(2):
            pair, banks, done = gemm(HHI, HLO, h_ready)
            for nt in range(2):
                k = 4 * g + 2 * u + nt
                z = silu_mul(Y[:, k, :], banks[nt][:, :], done[nt], [m_spill, m_h])
                bank_free[pair][nt] = z
                z_marks[k] = ts(Y[:, k, :], Y[:, k, :], COL[:, 128 + k:129 + k], None, MUL, None, [z])
        m_h_read_[0] = done[1]
        finish(task)
        for u in range(2):
            pair, banks, done = gemm(PHI, PLO, [[pooled[0]]] * 4)
            for nt in range(2):
                k = 4 * g + 2 * u + nt
                d = tt(Y[:, k, :], banks[nt][:, :], Y[:, k, :], MUL, [done[nt], z_marks[k]])
                bank_free[pair][nt] = d
                y_marks[k] = d
        ph_free[0] = done[1]

    m = need_mods("od", 23)
    m_gate1 = tt(MOD[:, 1, 32:48], MOD[:, 1, 32:48], COL[:, 96:112], MUL, [m])
    project_out(True, lambda k: MOD[:, 1, 32 + k:33 + k], lambda: m_gate1, [ph_free[0], up_free[0]])
    m = need_mods("w2", 15)
    m_spill, h_ready, m_h = next_layer(2, COL[:, 112:128], m)

    m_rope = pool.dma(CS[:, :], T["t_rope_b"][0], s_rope, [y_marks[0]])
    m_rope = pool.dma(SN[:, :], T["t_rope_b"][1], s_rope)
    m_rp[0] = m_rope
    m_tri = pool.dma(MK[:, :, :], T["t_sb"].rearrange("a p n -> p a n"), s_tri, [y_marks[0]])
    m_scr = y_marks[KT - 1]
    m_sg = ts(COL[:, 154:155], COL[:, 154:155], SCALE, None, MUL, None, [m_col])
    bf = {"q": [m_scr, m_scr], "k": [m_scr, m_scr], "v": [m_scr, m_scr], "ls": [None, None],
          "sp": None, "w": [None, None], "dk": None, "ta": [None, None], "s": [buf["s"], buf["s"]],
          "n": 0, "wn": 0, "sn": 0}
    LS2 = [LS, LSB]
    OFF = {3: 0, 2: 128, 1: 384, 0: 768}
    m_tri = acopy(TRIR[:, :], MK[:, 0, :], [m_tri])
    m_oner = acopy(ONER[:, :], ONE[:, :], [m_scr])

    def stick_head(h, b, i, vm):
        q, k_, v = Q2[b][:, i, :], K2[b][:, i, :], V2[b]
        first_o = True
        prev = None
        for kt in (3, 2, 1, 0):
            c0 = kt * P
            n = SEQ - c0
            sb_ = bf["sn"] % 2
            bf["sn"] += 1
            Z = S[:, sb_ * 512 + c0:sb_ * 512 + 512]
            m = mm(Z, k_[:, c0:c0 + P], q[:, c0:SEQ], True, True, [bf["s"][sb_]] + vm, sig=True)
            ls, spt = LS2[sb_][:, c0:SEQ], TA[1][:, c0:SEQ]
            ta = TA[0][:, c0:SEQ]
            hi, lo = SPH[:, OFF[kt]:OFF[kt] + n], SPL[:, OFF[kt]:OFF[kt] + n]
            a = af(ta, Z, ACT.Abs, [m, bf["ta"][0], m_scr])
            a = af(ta, ta, ACT.Exp, [a], scale=-1.0)
            a = af(ta, ta, ACT.Ln, [a], bias=1.0)
            d = stt(ls, Z, 0.0, ta, MIN, SUB, [a, bf["ls"][sb_]])
            d2 = stt(spt, Z, 0.0, ta, MAX, ADD, [a, bf["ta"][1], m_zero])
            bf["s"][sb_] = d2
            bf["ta"][0] = d2
            d3 = tt(TA[1][:, c0:c0 + P], TA[1][:, c0:c0 + P], MK[:, 1, :], MUL, [d2, m_tri])
            ah = acopy(hi, spt, [d3, bf["sp"]])
            d3 = tt(lo, spt, f(hi), SUB, [ah])
            bf["ta"][1] = d3
            d4 = tt(LS2[sb_][:, c0:c0 + P], LS2[sb_][:, c0:c0 + P], MK[:, 2, :], ADD, [d3])
            for _ in range(4):
                yield
            C = TB[:, c0:SEQ]
            mm(C, TRIR[:, :], hi, True, False, [d3, tmp["tb"], m_oner])
            mc = mm(C, TRIR[:, :], lo, False, kt == 3, sig=True)
            for k2 in range(kt + 1, 4):
                w = SEQ - k2 * P
                mm(TB[:, k2 * P:SEQ], ONER[:, :], SPH[:, OFF[k2]:OFF[k2] + w], False, False)
                mc = mm(TB[:, k2 * P:SEQ], ONER[:, :], SPL[:, OFF[k2]:OFF[k2] + w], False, k2 == 3, sig=True)
            d = tt(ls, ls, C, SUB, [mc, d4])
            tmp["tb"] = d
            wi = bf["wn"] % 2
            bf["wn"] += 1
            w = WB[wi][:, c0:SEQ]
            a = af(w, ls, ACT.Exp, [d, bf["w"][wi]])
            bf["ls"][sb_] = a
            yield
            yield
            if first_o:
                zz = WB[wi][:, 0:c0]
                a = vset(zz, 0.0, [a])
            mo = mm(OB[:, (0 if first_o else c0):SEQ], v[:, kt, i * P:(i + 1) * P],
                    WB[wi][:, (0 if first_o else c0):SEQ], first_o, kt == 0, [a, tmp["ob"]], sig=True)
            bf["w"][wi] = mo
            first_o = False
        bf["sp"] = mo
        yield
        tmp["ob"] = tt(Y[:, h, :], OB[:, :], Y[:, h, :], MUL, [mo, z_marks[h]])
        y_marks[h] = tmp["ob"]
        yield
        readers.append(mo)

    readers = []
    m_zero = m_scr

    def sb_task(p, b, qm, km, vmk, fin):
        for i in range(2):
            f1 = []
            for _ in norm_rope_plain(Q2[b][:, i, :], COL[:, 154:155], [qm[i]], f1):
                yield
            for _ in norm_rope_plain(K2[b][:, i, :], COL[:, 155:156], [km[i]], f1):
                yield
            for _ in stick_head(2 * p + i, b, i, f1 + [vmk]):
                yield
        bf["q"][b] = bf["k"][b] = bf["v"][b] = readers[-1]

    def norm_rope_plain(t, gcol_, after, fin):
        a = af(SQ2[1][:, :], t, ACT.Square, list(after) + [tmp["sq"][1]])
        yield
        m = mm(TB[:, :], ONE[:, :], SQ2[1][:, :], True, True, [a, tmp["tb"]], sig=True)
        tmp["sq"][1] = m
        m_, y = rstd(SEQ, TB[:, :], m, 128)
        tmp["tb"] = m_
        yield
        d = stt(t, t, gcol_, TY[:, :], MUL, MUL, [y])
        tmp["chain"] = d
        fin.append(d)
        yield

    def rope_only(t, after, fin):
        h = 64
        d1 = tt(TT_[h:P, :], t[0:h, :], SN[0:h, :], MUL, [tmp["chain"], m_rp[0]] + list(after))
        d2 = tt(TT_[0:h, :], t[h:P, :], SN[h:P, :], MUL, [d1])
        d3 = tt(t, t, CS[:, :], MUL, [d2])
        d4 = tt(t, t, TT_[:, :], ADD, [d3])
        tmp["chain"] = d4
        fin.append(d4)
        yield

    def ret_head(h, b, i, vm):
        q, k_, v = Q2[b][:, i, :], K2[b][:, i, :], V2[b]
        dk = pool.dma(DK[:, :], T["t_decay"][h], s_dk, [bf["dk"] or readers[-1]])
        yield
        mo = None
        for kt in range(4):
            c0 = kt * P
            sb_ = bf["sn"] % 2
            bf["sn"] += 1
            Z = S[:, sb_ * 512 + c0:sb_ * 512 + 512]
            m = mm(Z, k_[:, c0:c0 + P], q[:, c0:SEQ], True, True, [bf["s"][sb_]] + vm, sig=True)
            wi = bf["wn"] % 2
            bf["wn"] += 1
            d = tt(WB[wi][:, c0:SEQ], Z, DK[:, 0:SEQ - c0], MUL, [m, dk, bf["w"][wi]])
            bf["s"][sb_] = d
            yield
            mo = mm(OB[:, c0:SEQ], v[:, kt, i * P:(i + 1) * P], WB[wi][:, c0:SEQ], kt == 0, kt == 3,
                    [d, tmp["ob"]], sig=True)
            bf["w"][wi] = mo
        bf["dk"] = d
        readers.append(mo)
        a = acopy(LS[:, :], OB[:, :], [mo, bf["ls"][0]])
        tmp["ob"] = a
        yield
        m = mm(TB[:, :], ONE[:, :], LS[:, :], True, True, [a, tmp["tb"]], sig=True)
        d = stt(LS[:, :], TB[:, :], -1.0 / 128, LS[:, :], MUL, ADD, [m])
        tmp["tb"] = d
        a = af(SQ2[1][:, :], LS[:, :], ACT.Square, [d, tmp["sq"][1]])
        yield
        m = mm(TB[:, :], ONE[:, :], SQ2[1][:, :], True, True, [a, tmp["tb"]], sig=True)
        tmp["sq"][1] = m
        m_, y = rstd(SEQ, TB[:, :], m, 128)
        tmp["tb"] = m_
        d = stt(LS[:, :], LS[:, :], COL[:, 144 + h:145 + h], TY[:, :], MUL, MUL, [y])
        tmp["chain"] = d
        yield
        d = tt(Y[:, 8 + h, :], LS[:, :], Y[:, 8 + h, :], MUL, [d, z_marks[8 + h]])
        bf["ls"][0] = d
        y_marks[8 + h] = d
        yield

    def ret_task(p, b, qm, km, vmk):
        for i in range(2):
            f1 = []
            for _ in rope_only(Q2[b][:, i, :], [qm[i]], f1):
                yield
            for _ in rope_only(K2[b][:, i, :], [km[i]], f1):
                yield
            for _ in ret_head(2 * p + i, b, i, f1 + [vmk]):
                yield
        bf["q"][b] = bf["k"][b] = bf["v"][b] = readers[-1]

    x_tiles = [(lambda k, i=i: HHI[:, k, i * P:(i + 1) * P], lambda k, i=i: HLO[:, k, i * P:(i + 1) * P], h_ready)
               for i in range(4)]
    task = None
    for n in range(8):
        b = n % 2
        sides = []
        for what, dst in (("q", Q2[b]), ("k", K2[b])):
            pair, banks, done = gemm(HHI, HLO, h_ready)
            ms = []
            for nt in range(2):
                a = acopy(dst[:, nt, :], banks[nt][:, :], [done[nt], bf[what][b]])
                bank_free[pair][nt] = a
                ms.append(a)
            sides.append(ms)
        pair = at["unit"] % 2
        outs2 = [G[pair][i // 2][:, (i % 2) * 256:(i % 2) * 256 + 256] for i in range(4)]
        done = gemm_tok(x_tiles, lambda i, outs2=outs2: outs2[i], [bank_free[pair][0], bank_free[pair][1]])
        for i in range(2):
            a = acopy(V2[b][:, 2 * i:2 * i + 2, :], G[pair][i][:, :].rearrange("p (t n) -> p t n", t=2),
                      [done, bf["v"][b]])
            bank_free[pair][i] = a
        vmk = a
        pair, banks, done = gemm(HHI, HLO, h_ready)
        for nt in range(2):
            k = 2 * n + nt
            z_marks[k] = silu_mul(Y[:, k, :], banks[nt][:, :], done[nt], [m_spill, m_h])
            bank_free[pair][nt] = z_marks[k]
        if task is not None:
            finish(task)
        if n < 4:
            task = sb_task(n, b, sides[0], sides[1], vmk, None)
        else:
            task = ret_task(n - 4, b, sides[0], sides[1], vmk)
        background.append(task)
    m_h_read_[0] = done[1]
    finish(task)
    m = need_mods("w2", 23)
    project_out(False, lambda k: MOD[:, 2, 32 + k:33 + k], lambda: m, [readers[-1], y_marks[KT - 1]])

    write_out()


def chain(gens):
    for g in gens:
        for _ in g:
            yield


def norm_rope_copy(norm_rope, KTA, kh, SQ2, tmp, a, marks, vcopy):
    for _ in norm_rope(KTA[:, kh, 0:SEQ], KTA[:, kh, 0:SEQ], SEQ, None, True, [a], marks):
        yield


def tables():
    import numpy as np
    f4 = np.float32
    i = np.arange(P)
    sq = np.stack([np.eye(P), np.ones((P, P))]).astype(f4)
    low = np.where(i[None, :] >= i[:, None], 0.0, -1e30)
    high = np.where(i[None, :] <= i[:, None], 0.0, -1e30)
    mask = np.stack([low, high]).astype(f4)
    tri = (i[:, None] > i[None, :]).astype(f4)
    past = (i[:, None] < i[None, :]).astype(f4)
    sb = np.stack([tri, past, np.where(past > 0, 0.0, -1e30)]).astype(f4)

    def rope(ang):
        c, s = np.cos(ang).T, np.sin(ang).T
        return np.stack([np.concatenate([c, c]), np.concatenate([s, -s])]).astype(f4)

    t = np.arange(SEQ)
    inv = (10000.0 ** (-np.arange(32) / 32.0)).astype(f4)
    ang = np.concatenate([(t // 64).astype(f4)[:, None] * inv, (t % 64).astype(f4)[:, None] * inv], axis=1)
    inv2 = (10000.0 ** (-np.arange(64) / 64.0)).astype(f4)
    ang2 = t.astype(f4)[:, None] * inv2
    rc = np.stack([1.0 / (np.clip(t + w // 2, 0, SEQ) - np.clip(t - w // 2, 0, SEQ)) for w in (2, 4, 8, 16)])
    rc = np.ascontiguousarray(np.broadcast_to(rc[:, None, :], (4, P, SEQ))).astype(f4)
    g = np.log1p(-np.exp2(-5.0 - np.arange(8)))
    rel = t[None, :] - i[:, None]
    dec = np.where(rel[None] >= 0, np.exp(np.maximum(rel, 0)[None] * g[:, None, None]), 0.0) * SCALE
    r4 = np.array([[1, 0], [0, 1], [1, 0], [0, 1]], f4)
    return {"t_r4": r4, "t_sq": sq, "t_mask": mask, "t_sb": sb, "t_rope_a": rope(ang.astype(np.float64)),
            "t_rope_b": rope(ang2.astype(np.float64)), "t_rcnt": rc, "t_decay": dec.astype(f4)}


def kernel(**inputs):
    import numpy as np
    import concourse.bacc as bacc
    from concourse.bass_utils import run_bass_kernel_spmd as run

    nc = bacc.Bacc("TRN2", target_bir_lowering=False, num_devices=1)
    arrays, T = {}, {}
    const = tables()
    for name in INPUTS + TABLES:
        a = np.ascontiguousarray(const[name] if name in const else inputs[name])
        arrays[f"in_{name}"] = a
        T[name] = nc.dram_tensor(f"in_{name}", a.shape, F32, kind="ExternalInput").ap()
    out = nc.dram_tensor("out_x", (1, SEQ, D), F32, kind="ExternalOutput").ap()
    program(nc, T, out)
    r = run(nc, [arrays], core_ids=[0])
    return r.results[0]["out_x"]
```

```python
from contextlib import ExitStack

import concourse.bass as bass
from concourse import mybir

F32 = mybir.dt.float32
F32R = mybir.dt.float32r
ALU = mybir.AluOpType
ACT = mybir.ActivationFunctionType
AX_X = mybir.AxisListType.X

P = 128
D = 2048
KT = 16
SEQ = 512
CTX = 256
EPS = 1e-6
SCALE = 128.0 ** -0.5
NAT_LOG_EXP = 6

INPUTS = [
    "x", "c", "ctx", "c_ctx", "ev_mod_w", "ev_mod_b", "ev_pre_g", "ev_post_g", "ev_w_in", "ev_q_norm",
    "ev_k_norm", "ev_sink", "ev_w_out", "od_mod_w", "od_mod_b", "od_pre_g", "od_post_g", "od_w_in",
    "od_pool_w", "od_pool_scale", "od_w_out", "c_2", "w_ada_2", "b_ada_2", "norm_gain_2", "w_in_2",
    "sb_q_gain_2", "sb_k_gain_2", "ret_norm_gain_2", "w_out_2",
]
TABLES = ["t_sq", "t_mask", "t_sb", "t_r4", "t_rope_a", "t_rope_b", "t_rcnt", "t_decay"]


class Line:

    def __init__(self, sem):
        self.sem, self.n, self.ops = sem, 0, []

    def do(self, fn, after=(), sig=True):
        if sig:
            self.n += 1
        self.ops.append((fn, [m for m in after if m is not None], self.sem if sig else None, 1))
        return (self.sem, self.n) if sig else None

    def dma(self, out, in_, slot, after=()):
        slot.n += 16
        self.ops.append((lambda e: e.dma_start(out, in_), [m for m in after if m is not None], slot.sem, 16))
        return (slot.sem, slot.n)

    def emit(self, eng):
        seen = {}
        for fn, after, sem, by in self.ops:
            for s, v in after:
                if seen.get(s.name, 0) < v:
                    eng.wait_ge(s, v)
                    seen[s.name] = v
            ins = fn(eng)
            if sem is not None:
                ins.then_inc(sem, by)


class Slot:

    def __init__(self, sem):
        self.sem, self.n = sem, 0


def program(nc, T, out):
    with ExitStack() as ctx:
        build(nc, ctx, T, out)


def build(nc, ctx, T, out):
    base = nc.sbuf_base
    end = nc.sbuf_usable_end
    arena = ctx.enter_context(nc.sbuf_tensor("arena", [P, (end - base) // 4 - 64], F32))
    del arena
    top = [(base + 63) // 64 * 64]

    def place(name, shape, dt, at=None):
        size = 4
        for s in shape[1:]:
            size *= s
        if at is None:
            at = top[0]
            top[0] += (size + 31) // 32 * 32
            assert top[0] <= end - 32, (name, top[0], end)
        return nc.alloc_sbuf_tensor_at(name, list(shape), dt, offset=at), at

    def sem(name):
        return ctx.enter_context(nc.semaphore(name))

    def slot(name):
        return Slot(sem(name))

    HHI, _ = place("HHI", [P, KT, SEQ], F32R)
    HLO, _ = place("HLO", [P, KT, SEQ], F32R)
    Y, y0 = place("Y", [P, KT, SEQ], F32)
    CLO, _ = place("CLO", [P, KT, CTX], F32R, y0)
    NR, NS = 3, 3
    RAW = [place(f"RAW{i}", [P, 4, 256], F32)[0] for i in range(NR)]
    WHI = [place(f"WHI{i}", [P, 4, 256], F32R)[0] for i in range(NS)]
    WLO = [place(f"WLO{i}", [P, 4, 256], F32R)[0] for i in range(NS)]
    MRAW = [place(f"MRAW{i}", [P, 4, 256], F32)[0] for i in range(2)]
    MACC = [place(f"MACC{i}", [P, 256], F32)[0] for i in range(2)]
    SQ2 = [place(f"SQ{i}", [P, SEQ], F32)[0] for i in range(2)]
    TM, _ = place("TM", [P, SEQ], F32)
    TY, _ = place("TY", [P, SEQ], F32)
    TT_, _ = place("TT", [P, SEQ], F32)
    IDN, _ = place("IDN", [P, P], F32)
    ONE, _ = place("ONE", [P, P], F32)
    CS, _ = place("CS", [P, SEQ], F32)
    SN, _ = place("SN", [P, SEQ], F32)
    MK, _ = place("MK", [P, 3, P], F32)
    COL, _ = place("COL", [P, 304], F32)
    MOD, _ = place("MOD", [P, 3, 48], F32)
    MODX, _ = place("MODX", [P, 32], F32)
    SC, _ = place("SC", [P, 48], F32)
    SM, _ = place("SM", [P, 64], F32)
    s0 = top[0]
    room = end - 32 - s0

    def scratch(name, shape, dt, off):
        size = 4
        for s in shape[1:]:
            size *= s
        assert off + size <= room, (name, off, size, room)
        return place(name, shape, dt, s0 + off)[0]

    K1 = 1024
    PR = [scratch(f"PR{i}", [P, P], F32, 46 * K1 - 1536 + i * 512) for i in range(3)]
    XN = [scratch(f"XN{i}", [P, D], F32, 16 * K1 + i * 8 * K1) for i in range(3)]
    CT = scratch("CT", [P, KT, CTX], F32, 0)
    KTA = scratch("KTA", [P, 4, 768], F32, 0)
    VV = scratch("VV", [P, 6, 512], F32, 12 * K1)
    PB = [scratch(f"PB{i}", [P, 768], F32, 24 * K1 + i * 3 * K1) for i in range(2)]
    PT = scratch("PT", [P, 6, SEQ], F32, 30 * K1)
    CHI = scratch("CHI", [P, KT, CTX], F32R, 24 * K1)
    ROW = [scratch(f"ROW{i}", [4, 256], F32, 40 * K1 + i * K1) for i in range(2)]
    SCR = scratch("SCR", [P, KT, 4], F32R, 42 * K1)
    SC4 = scratch("SC4", [P, KT, 4], F32, 42 * K1 + 256)
    SACC = scratch("SACC", [P, SEQ], F32, 44 * K1)
    XR = scratch("XR", [P, KT, SEQ], F32, 0)
    UP = [scratch(f"UP{i}", [P, 4, 544], F32, i * 8704) for i in range(3)]
    PHI = scratch("PHI", [P, 4, SEQ], F32R, 26112)
    PLO = scratch("PLO", [P, 4, SEQ], F32R, 26112 + 8192)
    RC = scratch("RC", [P, SEQ], F32, 26112 + 16384)
    Q2 = [scratch(f"Q2{i}", [P, 2, SEQ], F32, i * 4 * K1) for i in range(2)]
    K2 = [scratch(f"K2{i}", [P, 2, SEQ], F32, 8 * K1 + i * 4 * K1) for i in range(2)]
    V2 = [scratch(f"V2{i}", [P, 4, 256], F32, 16 * K1 + i * 4 * K1) for i in range(2)]
    SPH = scratch("SPH", [P, 1280], F32R, 24 * K1)
    SPL = scratch("SPL", [P, 1280], F32R, 29 * K1)
    DK = scratch("DK", [P, SEQ], F32, 24 * K1)
    LS = scratch("LS", [P, SEQ], F32, 34 * K1)
    LSB = scratch("LSB", [P, SEQ], F32, 36 * K1)
    WB = [scratch(f"WB{i}", [P, SEQ], F32, 38 * K1 + i * 2 * K1) for i in range(2)]
    TA = [scratch(f"TA{i}", [P, SEQ], F32, 42 * K1 + i * 2 * K1) for i in range(2)]
    TRIR = scratch("TRIR", [P, P], F32R, 46 * K1)
    ONER = scratch("ONER", [P, P], F32R, 46 * K1 + 512)

    def bank(name, n=512):
        return ctx.enter_context(nc.psum_tensor(name, [P, n], F32))

    G = [[bank("G0"), bank("G1")], [bank("G2"), bank("G3")]]
    S = bank("S", 1024)
    TB = bank("TB")
    OB = bank("OB")

    pe, act, dve, pool, sp = (Line(sem(n)) for n in ("s_pe", "s_act", "s_dve", "s_pool", "s_sp"))
    s_raw = [slot(f"s_raw{i}") for i in range(NR)]
    s_mraw = [slot(f"s_mraw{i}") for i in range(2)]
    s_par = slot("s_par")
    s_cst = slot("s_cst")
    s_xn = [slot(f"s_xn{i}") for i in range(3)]
    s_rope = slot("s_rope")
    s_tri = slot("s_tri")
    s_spill = slot("s_spill")
    s_back = [slot(f"s_back{i}") for i in range(4)]
    s_rc = slot("s_rc")
    s_dk = slot("s_dk")
    s_out = [slot(f"s_out{i}") for i in range(4)]
    XS = nc.dram_tensor("x_spill", [P, KT, SEQ], F32)

    XO = [scratch(f"XO{i}", [P, SEQ], F32, 32 * K1 + i * 2 * K1) for i in range(4)]
    ofree = [None] * 4

    def write_out(q, x_free):
        cnt = 0
        for i in range(4):
            bank_, key = ((TB, "tb"), (OB, "ob"))[i % 2]
            for j in range(4):
                k = 4 * q + j
                m = tr(bank_[:, j * P:(j + 1) * P], Y[:, k, i * P:(i + 1) * P], [y_marks[k], tmp[key]], sig=j == 3)
            tmp[key] = (vcopy if i % 2 else acopy)(XO[i][:, :], bank_[:, :], [m, ofree[i]] + x_free)
            ofree[i] = pool.dma(out[0, i * P:(i + 1) * P, 512 * q:512 * q + 512], XO[i][:, :], s_out[i],
                                [tmp[key]])
            yield

    def emit_all():
        with nc.Block() as block:
            @block.sync
            def _(eng):
                sp.emit(eng)

            @block.gpsimd
            def _(eng):
                pool.emit(eng)
                for s in s_out + s_raw + s_mraw:
                    eng.wait_ge(s.sem, s.n)
                eng.wait_ge(s_spill.sem, s_spill.n)

            @block.scalar
            def _(eng):
                act.emit(eng)

            @block.vector
            def _(eng):
                dve.emit(eng)

            @block.tensor
            def _(eng):
                pe.emit(eng)

    def mm(o, l, r, start, stop, after=(), sig=False):
        return pe.do(lambda e: e.matmul(o, l, r, start=start, stop=stop, skip_group_check=True), after, sig)

    def tr(o, i, after=(), sig=False):
        return pe.do(lambda e: e.transpose(o, i, IDN[:, :]), after, sig)

    def af(o, i, f, after=(), bias=0.0, scale=1.0, acc=None):
        if acc is None:
            return act.do(lambda e: e.activation(o, i, f, bias=bias, scale=scale), after)
        return act.do(lambda e: e.activation(o, i, f, bias=bias, scale=scale, accum_out=acc), after)

    def acopy(o, i, after=(), scale=1.0):
        return act.do(lambda e: e.activation(o, i, ACT.Copy, scale=scale), after)

    def tt(o, a, b, op, after=()):
        return dve.do(lambda e: e.tensor_tensor(o, a, b, op), after)

    def ts(o, a, s1, s2, op0, op1, after=()):
        if op1 is None:
            return dve.do(lambda e: e.tensor_scalar(o, a, s1, None, op0), after)
        return dve.do(lambda e: e.tensor_scalar(o, a, s1, s2, op0, op1), after)

    def stt(o, a, s, b, op0, op1, after=()):
        return dve.do(lambda e: e.scalar_tensor_tensor(out=o, in0=a, scalar=s, in1=b, op0=op0, op1=op1), after)

    def vcopy(o, i, after=()):
        return dve.do(lambda e: e.tensor_copy(o, i), after)

    def vset(o, v, after=()):
        return dve.do(lambda e: e.memset(o, v), after)

    def f(t):
        return t.bitcast(F32)

    MUL, ADD, SUB, MAX, MIN = ALU.mult, ALU.add, ALU.subtract, ALU.max, ALU.min

    def weight(w, n0, nk=KT, k0=0):
        return [w[(k0 + c) * P:(k0 + c + 4) * P, n0:n0 + 256].rearrange("(t p) n -> p t n", p=P)
                for c in range(0, nk, 4)]

    def out_units(w):
        a, b = weight(w, 0), weight(w, 256)
        return [a[:3] + b[:3] + a[3:] + b[3:]] + [weight(w, 256 * i) for i in range(2, 8)]

    ev_w = T["ev_w_in"][0]
    od_w = T["od_w_in"][0]
    w2 = T["w_in_2"][0]
    units = []
    units += [weight(ev_w, 2048 + 256 * i) for i in range(4)]
    for p in range(8):
        units += [weight(ev_w, 3072 + 256 * p), weight(ev_w, 256 * p)]
    units += out_units(T["ev_w_out"][0])
    for g in range(4):
        units += [weight(od_w, 512 * g), weight(od_w, 512 * g + 256)]
        units += [weight(od_w, 2048 + 512 * g), weight(od_w, 2048 + 512 * g + 256)]
        units += [weight(T["od_pool_w"][0, g], 0, 4), weight(T["od_pool_w"][0, g], 256, 4)]
    units += out_units(T["od_w_out"][0])
    for p in range(4):
        units += [weight(w2, 1024 * i + 256 * p) for i in range(4)]
    for p in range(4):
        units += [weight(w2, 4096 + 1024 * i + 256 * p) for i in range(4)]
    units += out_units(T["w_out_2"][0])
    chunks = [c for u in units for c in u]
    raw_free = [None] * NR
    split_free = [None] * NS
    loaded = {}
    split = {}
    at = {"load": 0, "split": 0, "use": 0, "unit": 0, "pair": 0}

    def load_next():
        i = at["load"]
        if i < len(chunks):
            loaded[i] = sp.dma(RAW[i % NR][:, :, :], chunks[i], s_raw[i % NR], [raw_free[i % NR]])
            at["load"] += 1

    def split_next():
        i = at["split"]
        if i < len(chunks):
            r, s = i % NR, i % NS
            a = acopy(WHI[s][:, :, :], RAW[r][:, :, :], [loaded[i], split_free[s]])
            b = tt(WLO[s][:, :, :], RAW[r][:, :, :], f(WHI[s][:, :, :]), SUB, [a])
            raw_free[r] = b
            split[i] = (a, b)
            at["split"] += 1
            load_next()

    background = []

    def step(gens):
        for g in list(gens):
            try:
                next(g)
            except StopIteration:
                if g in background:
                    background.remove(g)

    def finish(g):
        if g in background:
            for _ in g:
                pass
            background.remove(g)

    bank_free = [[None, None], [None, None]]
    gates = [[], []]

    def gated(pair):
        while gates[pair]:
            finish(gates[pair].pop())

    def unit(work):
        u = at["unit"]
        at["unit"] += 1
        nch = len(units[u])
        at["pair"] += nch // 8 + 1
        done = None
        for c in range(nch):
            i = at["use"]
            at["use"] += 1
            while at["split"] < min(i + NS, len(chunks)) and at["split"] <= i:
                split_next()
            s = i % NS
            after = list(split[i])
            done = work(4 * c, WHI[s], WLO[s], c == 0, c == nch - 1, after)
            split_free[s] = done
            while at["split"] < min(i + NS, len(chunks)):
                split_next()
            step([mods])
        return done

    def gemm(hi, lo, ready, extra=None):
        pair = at["pair"] % 2
        gated(pair)
        banks, free = G[pair], bank_free[pair]

        def work(k0, wh, wl, first, last, after):
            done = None
            for nt in range(2):
                cols = slice(nt * P, nt * P + P)
                for j in range(4):
                    k = k0 + j
                    w = after + [m for m in ready[k]]
                    if first and j == 0:
                        w = w + [free[nt]]
                    o = banks[nt][:, :]
                    a, b = wh[:, j, cols], wl[:, j, cols]
                    end = last and j == 3
                    fin = nt == 1 and j == 3
                    mm(o, a, hi[:, k, :], first and j == 0, False, w)
                    mm(o, a, lo[:, k, :], False, False)
                    done = mm(o, b, hi[:, k, :], False, end, sig=(fin or end) and extra is None)
                    if extra is not None:
                        eo, ehi, elo, eready, efree = extra
                        w = [m for m in eready[k]]
                        if first and j == 0 and nt == 0:
                            w = w + [efree]
                        mm(eo(nt), a, ehi[:, k, :], first and j == 0 and nt == 0, False, w)
                        mm(eo(nt), a, elo[:, k, :], False, False)
                        done = mm(eo(nt), b, ehi[:, k, :], False, end, sig=fin or end)
                    if end and nt == 0:
                        half.append(done)
                    if j % 2:
                        step(background)
            return done

        half = []
        done = unit(work)
        return pair, banks, [half[0], done]

    def gemm_two(hi, lo, ready, tail):
        first_pair = at["pair"] % 2
        gated(first_pair)
        seq = [(0, 0), (0, 4), (0, 8), (1, 0), (1, 4), (1, 8), (0, 12), (1, 12)]
        ends = [[], []]

        def work(at4, wh, wl, first, last, after):
            u, k0 = seq[at4 // 4]
            pair = (first_pair + u) % 2
            if at4 == 12:
                gated(pair)
            if at4 == 24:
                tail()
            for nt in range(2):
                cols = slice(nt * P, nt * P + P)
                for j in range(4):
                    k = k0 + j
                    w = after + [m for m in ready[k]]
                    if k == 0:
                        w = w + [bank_free[pair][nt]]
                    o = G[pair][nt][:, :]
                    end = k == 15
                    mm(o, wh[:, j, cols], hi[:, k, :], k == 0, False, w)
                    mm(o, wh[:, j, cols], lo[:, k, :], False, False)
                    done = mm(o, wl[:, j, cols], hi[:, k, :], False, end, sig=end or (nt == 1 and j == 3))
                    if end:
                        ends[u].append(done)
                    if j % 2:
                        step(background)
            return done

        unit(work)
        return [((first_pair + u) % 2, G[(first_pair + u) % 2], ends[u]) for u in range(2)]

    def gemm_tok(tiles, outs, frees):
        def work(k0, wh, wl, first, last, after):
            done = None
            for i, (hi, lo, ready) in enumerate(tiles):
                for j in range(4):
                    k = k0 + j
                    w = after + [m for m in ready[k]]
                    begin = first and j == 0 and i % 2 == 0
                    if begin:
                        w = w + [frees[i // 2]]
                    mm(outs(i), hi(k), wh[:, j, :], begin, False, w)
                    mm(outs(i), lo(k), wh[:, j, :], False, False)
                    done = mm(outs(i), hi(k), wl[:, j, :], False, last and j == 3,
                              sig=i == len(tiles) - 1 and j == 3)
                step(background)
            return done

        return unit(work)

    sp.dma(IDN[:, :], T["t_sq"][0], s_cst)
    m_cst = sp.dma(ONE[:, :], T["t_sq"][1], s_cst)
    m_eps = vset(SM[:, 50:51], EPS)
    z0 = vset(PR[1][:, :], 0.0)
    z1 = vset(PR[2][:, :], 0.0)

    def params(pr, r, src, n, after=()):
        return (sp if pr else act).dma(PR[pr][r:r + n, :], src.rearrange("(t p) -> t p", p=P), s_par, after)

    params(0, 0, T["c"][0], 16)
    params(0, 16, T["c_ctx"], 16)
    params(0, 32, T["c_2"][0], 16)
    params(0, 48, T["ev_pre_g"][0], 16)
    params(0, 64, T["ev_post_g"][0], 16)
    params(0, 80, T["od_pre_g"][0], 16)
    params(0, 96, T["od_post_g"][0], 16)
    params(0, 112, T["norm_gain_2"][0], 16)
    params(1, 0, T["od_pool_scale"][0], 16, [z0, z1])
    params(1, 16, T["ret_norm_gain_2"][0], 8)
    params(1, 24, T["ev_q_norm"][0], 1)
    params(1, 25, T["ev_k_norm"][0], 1)
    params(1, 26, T["sb_q_gain_2"][0], 1)
    params(1, 27, T["sb_k_gain_2"][0], 1)
    params(1, 32, T["ev_mod_b"][0], 48)
    params(1, 80, T["od_mod_b"][0], 48)
    params(2, 0, T["b_ada_2"][0], 48)
    sp.dma(SM[0:4, 40:42], T["t_r4"], s_par)
    m_par = act.dma(SM[0:1, 0:8], T["ev_sink"], s_par)
    m_xn = [pool.dma(XN[i][:, :], T["ctx"][0, i * P:(i + 1) * P, :], s_xn[i]) for i in range(2)]
    m_xn.append(pool.dma(XN[2][:, :], T["x"][0, 0:P, :], s_xn[2]))
    m_rope = pool.dma(CS[:, :], T["t_rope_a"][0], s_rope)
    m_rope = pool.dma(SN[:, :], T["t_rope_a"][1], s_rope)
    m_mk = pool.dma(MK[:, 0:2, :], T["t_mask"].rearrange("a p n -> p a n"), s_tri)

    act.do(lambda e: e.add_instruction(mybir.InstLoadActFuncSet(
        act_func_set_id=NAT_LOG_EXP, name=nc.get_next_instruction_name(),
        engine=mybir.EngineType.Activation, ins=[], outs=[])), (), False)

    tr(TB[:, 0:P], PR[0][:, :], [m_cst, m_par])
    tr(TB[:, P:2 * P], PR[1][:, :])
    tr(TB[:, 2 * P:3 * P], PR[2][:, :])
    m_t = mm(TB[:, 384:392], ONE[0:1, :], SM[0:1, 0:8], True, True, sig=True)
    m_col = vcopy(COL[:, :], TB[:, 0:304], [m_t])
    m_snk = ts(SM[:, 8:16], TB[:, 384:392], -1.0, None, MUL, None, [m_t])
    m_snk = ts(SM[:, 16:24], TB[:, 384:392], 1.0, None, MUL, None, [m_snk])

    a1 = af(SC[:, :], COL[:, 0:48], ACT.Abs, [m_col])
    a1 = af(SC[:, :], SC[:, :], ACT.Exp, [a1], scale=-1.0)
    a1 = af(SC[:, :], SC[:, :], ACT.Ln, [a1], bias=1.0)
    d1 = stt(SC[:, :], COL[:, 0:48], 0.0, SC[:, :], MIN, SUB, [a1])
    a1 = af(SC[:, :], SC[:, :], ACT.Exp, [d1])
    m_sc = tt(SC[:, :], COL[:, 0:48], SC[:, :], MUL, [a1])
    scv = SC[:, :].rearrange("p (v k) -> p k v", k=KT)[:, :, 0:2]
    z2 = vset(SC4[:, :, :], 0.0, [m_col])
    z2 = vcopy(SC4[:, :, 0:2], scv, [z2, m_sc])
    a1 = acopy(SCR[:, :, 0:2], scv, [m_sc])
    m_scr4 = tt(SCR[:, :, 2:4], scv, f(SCR[:, :, 0:2]), SUB, [a1, z2])

    tmp = {"sq": [None, None], "chain": None, "tb": m_snk, "ob": None}


    def rstd(n, bank_ap, m_stat, count, extra=()):
        a = act.do(lambda e: e.activation(TY[:, 0:n], bank_ap, ACT.Ln, bias=SM[:, 50:51], scale=1.0 / count),
                   [m_stat, tmp["chain"], m_eps] + list(extra))
        a2 = af(TY[:, 0:n], TY[:, 0:n], ACT.Exp, [a], scale=-0.5)
        m = ts(TM[:, 0:n], bank_ap, 1.0 / count, EPS, MUL, ADD, [a])
        b = tt(TT_[:, 0:n], TY[:, 0:n], TY[:, 0:n], MUL, [a2])
        b = stt(TT_[:, 0:n], TT_[:, 0:n], -0.5, TM[:, 0:n], MUL, MUL, [b])
        b = stt(TY[:, 0:n], TT_[:, 0:n], 1.5, TY[:, 0:n], ADD, MUL, [b])
        return m, b

    nat = [("c", 0), ("c", 1)] + [("x", i) for i in range(4)]
    xs = {}

    def x_prep():
        ring = [None] * 3
        bank2, key = [TB, OB], ["tb", "ob"]
        cnt = 0
        for n, (what, i) in enumerate(nat):
            r = n % 3
            if n >= 3:
                m_xn.append(pool.dma(XN[r][:, :], T["x"][0, i * P:(i + 1) * P, :], s_xn[r], [ring[r]]))
            for q in range(4):
                b = cnt % 2
                for j in range(4):
                    k = 4 * q + j
                    m = tr(bank2[b][:, j * P:(j + 1) * P], XN[r][:, k * P:(k + 1) * P],
                           [m_xn[n], tmp[key[b]], m_cst], sig=j == 3)
                dst = (CT if what == "c" else Y)[:, 4 * q:4 * q + 4, i * P:(i + 1) * P]
                src = bank2[b][:, :].rearrange("p (j n) -> p j n", j=4)
                if b:
                    tmp["ob"] = vcopy(dst, src, [m])
                else:
                    tmp["tb"] = acopy(dst, src, [m])
                cnt += 1
                if q % 2:
                    yield
            ring[r] = m
        both = [tmp["tb"], tmp["ob"]]
        xs["in"] = [m]
        xs["spill"] = pool.dma(XS.ap(), Y[:, :, :], s_spill, both)
        for name, tiles, n, bank_, key_ in (("x", Y, SEQ, TB, "tb"), ("c", CT, CTX, OB, "ob")):
            m = None
            for k in range(KT):
                m = stat_tile(tiles, n, k, both, bank_, tmp[key_])
                if k % 2:
                    yield
            tmp[key_], y_ = rstd(n, bank_[:, 0:n], m, D)
            yield
            for k in range(KT):
                if name == "x":
                    d = tt(Y[:, k, :], Y[:, k, :], TY[:, 0:n], MUL, [y_, xs["spill"]])
                else:
                    d = tt(CT[:, k, :], CT[:, k, :], TY[:, 0:n], MUL, [y_])
                if k % 2:
                    yield
            tmp["chain"] = d
            xs[name] = d
        yield

    def stat_tile(tiles, n, k, ready, bank, free):
        s = k % 2
        a = af(SQ2[s][:, 0:n], tiles[:, k, 0:n], ACT.Square, list(ready) + [tmp["sq"][s]])
        m = mm(bank[:, 0:n], ONE[:, :], SQ2[s][:, 0:n], k == 0, k == KT - 1, [a, free], sig=True)
        tmp["sq"][s] = m
        return m

    h_ready, hc_ready = [None] * KT, [None] * KT

    def split_tile(k, src, n, gain, shift, hi, lo, after, ready):
        s = k % 2
        d = ts(SQ2[s][:, 0:n], src, gain, shift, MUL, ADD, [tmp["sq"][s]] + list(after))
        a = act.do(lambda e: e.activation(hi, src, ACT.Identity, bias=shift, scale=gain), list(after))
        d = tt(lo, SQ2[s][:, 0:n], f(hi), SUB, [d, a])
        tmp["sq"][s] = d
        ready[k] = [d]
        return d

    ev_mw = T["ev_mod_w"][0]
    rings, rsem, rfree = RAW + MRAW, s_raw + s_mraw, [None] * 5
    order = [nb for i in range(8) for nb in (i, 8 + i)]
    jobs0 = [(nb, c) for nb in order for c in range(4)]
    arrived, parts0, sfree0 = {}, {}, [None] * NS
    rows_free, cols_free, row_m = [None, None], [None, None], {}
    mfree = [None, None]

    def direct(i):
        return i % 4 != 9

    nsplit = [0]

    def mod_load(i):
        if i < len(jobs0):
            nb, c = jobs0[i]
            arrived[i] = sp.dma(rings[i % 5][:, :, :], weight(ev_mw, 256 * nb)[c], rsem[i % 5], [rfree[i % 5]])

    def mod_split(i):
        if i < len(jobs0) and not direct(i):
            r, q = i % 5, nsplit[0] % NS
            nsplit[0] += 1
            a = acopy(WHI[q][:, :, :], rings[r][:, :, :], [arrived[i], sfree0[q]])
            b = tt(WLO[q][:, :, :], rings[r][:, :, :], f(WHI[q][:, :, :]), SUB, [a])
            parts0[i] = (q, b)
            rfree[r] = b

    def mod_cols(n):
        nb, b, a = row_m.pop(n)
        o = G[1][b]
        for nt in range(2):
            m = mm(o[:, 2 * nt:2 * nt + 2], ROW[b][:, nt * P:(nt + 1) * P], SM[0:4, 40:42], nt == 0, nt == 1,
                   [a, cols_free[b], m_par], sig=nt == 1)
        rows_free[b] = m
        v = o[:, 0:4].rearrange("p (n v) -> p v n", v=2)
        d = tt(MOD[:, 0, 2 * nb:2 * nb + 2], v[:, 0, :], COL[:, 160 + 2 * nb:162 + 2 * nb], ADD, [m, m_col])
        d = tt(MODX[:, 2 * nb:2 * nb + 2], v[:, 1, :], COL[:, 160 + 2 * nb:162 + 2 * nb], ADD, [m, d])
        cols_free[b] = d
        if nb >= 8:
            k = 2 * nb - 16
            d = stt(MOD[:, 0, 16 + k:18 + k], MOD[:, 0, 16 + k:18 + k], 1.0, COL[:, 48 + k:50 + k], ADD, MUL, [d])
            d = stt(MODX[:, 16 + k:18 + k], MODX[:, 16 + k:18 + k], 1.0, COL[:, 48 + k:50 + k], ADD, MUL, [d])
            queue.extend([(k, d), (k + 1, d)])

    queue = []

    def h_tile():
        k, d = queue.pop(0)
        m = split_tile(k, Y[:, k, :], SEQ, MOD[:, 0, 16 + k:17 + k], MOD[:, 0, k:k + 1], HHI[:, k, :],
                       HLO[:, k, :], [d, xs["x"]], h_ready)
        split_tile(k, CT[:, k, :], CTX, MODX[:, 16 + k:17 + k], MODX[:, k:k + 1], CHI[:, k, :], CLO[:, k, :],
                   [d, xs["c"], m] + xs["in"], hc_ready)

    prep = x_prep()
    for i in range(5):
        mod_load(i)
    for i in range(2):
        mod_split(i)
    last_q = None
    for i, (nb, c) in enumerate(jobs0):
        n, r = i // 4, i % 5
        b = n % 2
        mod_split(i + 2)
        row = G[0][b][0:4, 0:256]
        for j in range(4):
            first, end = c == 0 and j == 0, c == 3 and j == 3
            if direct(i):
                m = mm(row, SC4[:, 4 * c + j, :], rings[r][:, j, :], first, end,
                       [arrived[i], m_scr4, mfree[b]], sig=j == 3)
            else:
                q, w = parts0[i]
                mm(row, SCR[:, 4 * c + j, :], WHI[q][:, j, :], first, False, [w, m_scr4, mfree[b]])
                m = mm(row, SCR[:, 4 * c + j, :], WLO[q][:, j, :], False, end, sig=j == 3)
        if direct(i):
            rfree[r] = m
        else:
            sfree0[q] = m
        mod_load(i + 5)
        if c == 3:
            a = acopy(ROW[b][:, :], row, [m, rows_free[b]])
            mfree[b] = a
            row_m[n] = (nb, b, a)
        if c == 1 and n > 0:
            mod_cols(n - 1)
        for _ in range(2):
            next(prep, None)
        if "c" in xs and queue:
            h_tile()
    for _ in prep:
        pass
    mod_cols(len(order) - 1)
    while queue:
        h_tile()
    for q in range(NS):
        split_free[q] = sfree0[q]
    for r in range(NR):
        raw_free[r] = rfree[r]
    mraw_free = [rfree[3], rfree[4]]
    bank_free[0] = [mfree[0], mfree[1]]
    bank_free[1] = [cols_free[0], cols_free[1]]
    m_spill = xs["spill"]

    mod_jobs = [("ev", T["ev_mod_w"][0], 0, 0, 16, 24, 160), ("od", T["od_mod_w"][0], 1, 0, 0, 24, 208),
                ("w2", T["w_ada_2"][0], 2, 32, 0, 24, 256)]
    mod_done = {}

    def mod_stream():
        n = 0
        free = [None, None]
        last = None
        turn = 0
        for name, w, layer, c0, nb0, nb1, bias in mod_jobs:
            for nb in range(nb0, nb1):
                d = None
                acc = MACC[turn % 2]
                for c in range(4):
                    r = n % 2
                    n += 1
                    m_l = sp.dma(MRAW[r][:, :, :], weight(w, 256 * nb)[c], s_mraw[r], [mraw_free[r]])
                    yield
                    if c == 2 and last is not None:
                        free[(turn + 1) % 2] = mod_reduce(*last)
                        last = None
                    for j in range(4):
                        col = SC[:, c0 + 4 * c + j:c0 + 4 * c + j + 1]
                        if c == 0 and j == 0:
                            d = ts(acc[:, :], MRAW[r][:, j, :], col, None, MUL, None, [m_l, m_sc, free[turn % 2]])
                        else:
                            d = stt(acc[:, :], MRAW[r][:, j, :], col, acc[:, :], MUL, ADD, [m_l, d])
                    mraw_free[r] = d
                last = (name, nb, layer, bias, acc, d)
                turn += 1
        yield
        yield
        mod_reduce(*last)
        yield

    def mod_reduce(name, nb, layer, bias, acc, d):
        mm(TB[:, 0:1], acc[:, 0:P], ONE[:, 0:1], True, True, [d, tmp["tb"]])
        m = mm(TB[:, 1:2], acc[:, P:2 * P], ONE[:, 0:1], True, True, sig=True)
        v = tt(MOD[:, layer, 2 * nb:2 * nb + 2], TB[:, 0:2], COL[:, bias + 2 * nb:bias + 2 * nb + 2], ADD, [m])
        tmp["tb"] = v
        mod_done[(name, nb)] = v
        return m

    load_next()
    load_next()
    load_next()
    mods = mod_stream()
    m_hc = hc_ready[KT - 1][0]

    def norm_rope(src, dst, n, gcol, rope, after, fin):
        a = af(SQ2[1][:, 0:n], src, ACT.Square, list(after) + [tmp["sq"][1]])
        yield
        if gcol is not None:
            yield
            m = mm(TB[:, 0:n], ONE[:, :], SQ2[1][:, 0:n], True, True, [a, tmp["tb"]], sig=True)
            tmp["sq"][1] = m
            mm_, y = rstd(n, TB[:, 0:n], m, 128)
            tmp["tb"] = mm_
            yield
            d = stt(TM[:, 0:n], src, gcol, TY[:, 0:n], MUL, MUL, [y])
            cur = TM[:, 0:n]
            tmp["chain"] = d
        else:
            tmp["sq"][1] = a
            cur, d = src, a
        if rope:
            h = 64
            cl = cur
            d1 = tt(TT_[h:P, 0:n], cl[0:h, :], SN[0:h, 0:n], MUL, [d, m_rp[0], tmp["chain"]] + list(after))
            d2 = tt(TT_[0:h, 0:n], cl[h:P, :], SN[h:P, 0:n], MUL, [d1])
            d3 = tt(dst, cur, CS[:, 0:n], MUL, [d2])
            d4 = tt(dst, dst, TT_[:, 0:n], ADD, [d3])
        else:
            d4 = vcopy(dst, cur, [d])
        tmp["chain"] = d4
        fin.append(d4)
        yield

    def run(g):
        for _ in g:
            pass

    m_rp = [m_rope]

    ctx_place = lambda nt: OB[:, nt * CTX:(nt + 1) * CTX]
    kv_marks = []
    scr_free = [m_hc]
    x_tiles = [(lambda k, i=i: HHI[:, k, i * P:(i + 1) * P], lambda k, i=i: HLO[:, k, i * P:(i + 1) * P], h_ready)
               for i in range(4)]
    c_tiles = [(lambda k, i=i: CHI[:, k, i * P:(i + 1) * P], lambda k, i=i: CLO[:, k, i * P:(i + 1) * P], hc_ready)
               for i in range(2)]
    for side in range(2):
        pair, banks, done = gemm(HHI, HLO, h_ready, (ctx_place, CHI, CLO, hc_ready, tmp["ob"]))
        ev = []
        for nt in range(2):
            kh = 2 * side + nt
            a = acopy(KTA[:, kh, 0:SEQ], banks[nt][:, :], [done[1]] + scr_free)
            bank_free[pair][nt] = a
            a2 = acopy(KTA[:, kh, SEQ:768], ctx_place(nt), [done[1]])
            tmp["ob"] = a2
            ev.append((kh, a, a2))
        parts = []
        for kh, a, a2 in ev:
            if side == 0:
                parts.append(chain([
                    norm_rope(KTA[:, kh, 0:SEQ], KTA[:, kh, 0:SEQ], SEQ, COL[:, 153:154], True, [a], kv_marks),
                    norm_rope(KTA[:, kh, SEQ:768], KTA[:, kh, SEQ:768], CTX, COL[:, 153:154], False, [a2],
                              kv_marks)]))
            else:
                parts.append(norm_rope_copy(norm_rope, KTA, kh, SQ2, tmp, a, kv_marks, vcopy))
        task = chain(parts)
        background.append(task)
        pair = at["pair"] % 2
        outs = [G[pair][0][:, 0:256], G[pair][0][:, 256:512], G[pair][1][:, 0:256], G[pair][1][:, 256:512],
                OB[:, 0:256], OB[:, 256:512]]
        done = gemm_tok(x_tiles + c_tiles, lambda i: outs[i],
                        [bank_free[pair][0], bank_free[pair][1], tmp["ob"]])
        for i, b in enumerate([G[pair][0], G[pair][1], OB]):
            a = acopy(VV[:, 2 * i:2 * i + 2, side * 256:side * 256 + 256],
                      b[:, :].rearrange("p (t n) -> p t n", t=2), [done] + scr_free)
            if i < 2:
                bank_free[pair][i] = a
            else:
                tmp["ob"] = a
            kv_marks.append(a)
        finish(task)
    m_ctx_read = done

    buf = {"qt": None, "pb": [None, None], "pt": None, "s": None, "nm": 0}

    def score_rows(h, q, qt, ready):
        band = h >= 8
        kv = (h // 4) if not band else 2 + (h - 8) // 4
        kt_ = KTA[:, kv, :]
        b = buf["nm"] % 2
        lq = QR[:, q, qt * P:(qt + 1) * P]
        need = [buf["s"]] + ready + kv_marks
        if not band:
            mm(S[:, 0:512], lq, kt_[:, 0:512], True, True, need)
            m = mm(S[:, 512:768], lq, kt_[:, 512:768], True, True, sig=True)
            lo_ = 0
            jobs = [(j, j * P) for j in range(6)]
        else:
            t0, t1 = max(0, qt - 1), min(3, qt + 1)
            nb = t1 - t0 + 1
            lo_ = 512 - nb * P
            mm(S[:, lo_:512], lq, kt_[:, t0 * P:(t1 + 1) * P], True, True, need)
            m = mm(S[:, 512:768], lq, kt_[:, 512:768], True, True, sig=True)
            if qt > 0:
                m = tt(S[:, lo_:lo_ + P], S[:, lo_:lo_ + P], MK[:, 0, :], ADD, [m, m_mk])
            if qt < 3:
                m = tt(S[:, 384:512], S[:, 384:512], MK[:, 1, :], ADD, [m, m_mk])
            jobs = [(t0 + j, lo_ + j * P) for j in range(nb)] + [(4, 512), (5, 640)]
        m_q = (pe.sem, pe.n)
        i = 24 + 4 * (buf["nm"] % 4)
        buf["nm"] += 1
        nm, rs = SM[:, i:i + 1], SM[:, i + 1:i + 2]
        src = S[:, lo_:768]
        d = dve.do(lambda e: e.tensor_reduce(nm, src, AX_X, MAX, negate=True), [m])
        if band:
            d = ts(nm, nm, SM[:, h:h + 1], None, MIN, None, [d, m_snk])
        a = af(PB[b][:, lo_:768], src, ACT.Exp, [d, buf["pb"][b], m_ctx_read], bias=nm, acc=rs)
        buf["s"] = a
        if band:
            es = SM[:, i + 2:i + 3]
            a2 = af(es, SM[:, 8 + h:9 + h], ACT.Exp, [a], bias=nm)
            d = tt(rs, rs, es, ADD, [a2])
        else:
            d = a
        d = dve.do(lambda e: e.reciprocal(rs, rs), [d])
        m_p = ts(PB[b][:, lo_:768], PB[b][:, lo_:768], rs, None, MUL, None, [d])
        return (qt, b, jobs, m_p), m_q

    def spread(qt, b, part, m_p, final, bank, key):
        for x_, (j, c0) in enumerate(part):
            mt = tr(bank[:, x_ * P:(x_ + 1) * P], PB[b][:, c0:c0 + P], [m_p, tmp[key]], sig=x_ == len(part) - 1)
        if final:
            buf["pb"][b] = mt
        runs = []
        for x2, (j, c0) in enumerate(part):
            if runs and runs[-1][1] + runs[-1][2] == j:
                runs[-1][2] += 1
            else:
                runs.append([x2, j, 1])
        for x2, j, n in runs:
            dst = PT[:, j:j + n, qt * P:(qt + 1) * P]
            src = bank[:, x2 * P:(x2 + n) * P].rearrange("p (j n) -> p j n", j=n)
            tmp[key] = acopy(dst, src, [mt, buf["pt"], tmp[key]])
        return tmp[key]

    def values(h, last):
        band = h >= 8
        kv = (h // 4) if not band else 2 + (h - 8) // 4
        vcol = slice(kv * P, kv * P + P)
        for n, j in enumerate([4, 5, 0, 1, 2, 3]):
            c = slice(0, 512) if j > 3 or not band else slice(max(0, j - 1) * P, min(4, j + 2) * P)
            m = mm(OB[:, c], VV[:, j, vcol], PT[:, j, c], n == 0, n == 5, last, sig=n == 5)
        buf["pt"] = m
        return m

    def silu_pair(k0, pair, banks, done, after, col=None):
        t = SQ2[0][:, :]
        for nt in range(2):
            k, z, dst = k0 + nt, banks[nt][:, :], Y[:, k0 + nt, :]
            a = af(t, z, ACT.Abs, [done[nt], tmp["sq"][0]])
            a = af(t, t, ACT.Exp, [a], scale=-1.0)
            a = af(t, t, ACT.Ln, [a], bias=1.0)
            d = stt(t, z, 0.0, t, MIN, SUB, [a])
            yield
            yield
            a = af(t, t, ACT.Exp, [d])
            if col is None:
                d = tt(dst, z, t, MUL, [a] + after)
            else:
                d = stt(dst, z, col(k), t, MUL, MUL, [a] + after)
            tmp["sq"][0] = d
            z_marks[k] = bank_free[pair][nt] = d
            if nt == 0:
                yield
                yield

    def silu(*args):
        g = silu_pair(*args)
        gates[args[1]].append(g)
        background.append(g)

    QR = scratch("QR", [P, 2, SEQ], F32, 42 * K1)
    y_marks = [None] * KT
    qr_free = [None, None]
    task_rows = []
    z_marks = [None] * KT

    def pair_task(p, qm):
        gens, ready = [], []
        for i in range(2):
            fin = []
            src = QR[:, i, :]
            gens.append(norm_rope(src, src, SEQ, COL[:, 152:153] if p < 4 else None, True, [qm[i], qm[2]], fin))
            ready.append(fin)
        for g in gens:
            for _ in g:
                yield
        yield
        yield
        events = {}

        def plan(t, fn):
            events.setdefault(t, []).append(fn)

        def rows(t, n):
            i, qt = divmod(n, 4)
            task_rows.append(n)
            (qt, b, jobs, m_p), qr_free[i] = score_rows(2 * p + i, i, qt, ready[i])
            two = len(jobs) > 4
            plan(t + 4, lambda: spread(qt, b, jobs[:4], m_p, not two, TB, "tb"))
            if two:
                plan(t + 5, lambda: spread(qt, b, jobs[4:], m_p, True, OB, "ob"))
            if qt == 3:
                plan(t + 6, lambda: pv(t + 6, 2 * p + i))

        def pv(t, h):
            m = values(h, [tmp["tb"], tmp["ob"]])
            plan(t + 1, lambda: gate_y(h, m))

        def gate_y(h, m):
            tmp["ob"] = tt(Y[:, h, :], OB[:, :], Y[:, h, :], MUL, [m, z_marks[h]])
            y_marks[h] = tmp["ob"]

        for n in range(8):
            plan(3 * n, lambda n=n: rows(3 * n, n))
        t = 0
        while events:
            for fn in reversed(events.pop(t, [])):
                fn()
            t += 1
            yield

    m_qs = ts(COL[:, 152:153], COL[:, 152:153], SCALE, None, MUL, None, [m_col])
    task = None
    for p in range(8):
        pair, banks, done = gemm(HHI, HLO, h_ready)
        silu(2 * p, pair, banks, done, [m_ctx_read])
        pair, banks, done = gemm(HHI, HLO, h_ready)
        while task is not None and task in background and len(task_rows) < 8 * p:
            step(background)
        qm = []
        for nt in range(2):
            a = acopy(QR[:, nt, :], banks[nt][:, :], [done[nt], qr_free[nt], m_ctx_read], scale=SCALE if p >= 4 else 1.0)
            bank_free[pair][nt] = a
            qm.append(a)
        task = pair_task(p, qm + [m_qs])
        background.append(task)
    m_h_read = done[1]

    back_marks = []

    def project_out(post, gate, m_gate, x_free):
        ready = [None] * KT
        back_marks.clear()
        back = back_marks

        def split_y(k):
            a = acopy(HHI[:, k, :], Y[:, k, :], [y_marks[k], m_h_read_[0]])
            d = tt(HLO[:, k, :], Y[:, k, :], f(HHI[:, k, :]), SUB, [a])
            ready[k] = [d]

        def tail():
            for g in list(background):
                finish(g)
            for k in range(12, KT):
                split_y(k)
            free = x_free()
            for q in range(4):
                back.append(pool.dma(XR[:, 4 * q:4 * q + 4, :], XS.ap()[:, 4 * q:4 * q + 4, :], s_back[q], free))

        def evacuate(u, pair, banks, done):
            all_split = ready[-1][0]
            for nt in range(2):
                k = 2 * u + nt
                if post:
                    a2 = af(SQ2[nt][:, :], banks[nt][:, :], ACT.Square, [done[nt], tmp["sq"][nt], *(acc[-1:] if u == 1 else ())])
                    a = act.do(lambda e, k=k, b=banks[nt]: e.activation(Y[:, k, :], b[:, :], ACT.Copy,
                                                                        scale=gate(k)),
                               [done[nt], all_split, m_gate()])
                    bank_free[pair][nt] = a
                    y_marks[k] = a
                    if u < 7:
                        if k == 0:
                            p_ = pool.do(lambda e: e.tensor_copy(SACC[:, :], SQ2[0][:, :]), [a2] + x_free())
                        else:
                            p_ = pool.do(lambda e, nt=nt: e.tensor_tensor(SACC[:, :], SACC[:, :], SQ2[nt][:, :],
                                                                          ADD), [a2, acc[-1]])
                        acc.append(p_)
                        tmp["sq"][nt] = p_
                    else:
                        if nt == 0:
                            mm(OB[:, :], ONE[:, :], SACC[:, :], True, False, [acc[-1], tmp["ob"]])
                        stat.append(mm(OB[:, :], ONE[:, :], SQ2[nt][:, :], False, nt == 1, [a2], sig=True))
                        tmp["sq"][nt] = stat[-1]
                else:
                    d = stt(Y[:, k, :], banks[nt][:, :], gate(k), XR[:, k, :], MUL, ADD,
                            [done[nt], m_gate(), all_split, back_marks[k // 4]])
                    bank_free[pair][nt] = d
                    y_marks[k] = d

        acc, stat = [], []
        for k in range(12):
            split_y(k)
        two = gemm_two(HHI, HLO, ready, tail)
        for u in range(2):
            evacuate(u, *two[u])
        for u in range(2, 8):
            if not post and u % 2 == 0:
                background.append(write_out(u // 2 - 1, x_free()))
            pair, banks, done = gemm(HHI, HLO, ready)
            evacuate(u, pair, banks, done)
        m_h_read_[0] = done[1]
        if post:
            m1, y_ = rstd(SEQ, OB[:, :], stat[-1], D)
            tmp["ob"] = m1
            update.append(y_)

    update = []

    def update_x(k0):
            y_ = update[-1]
            for k in (k0, k0 + 1):
                d = tt(Y[:, k, :], Y[:, k, :], TY[:, :], MUL, [y_, y_marks[k]])
                if (k % 8 in (0, 2, 4, 6, 7) or k % 4 == 1) and k < 14:
                    y_marks[k] = pool.do(lambda e, k=k: e.tensor_tensor(Y[:, k, :], Y[:, k, :], XR[:, k, :], ADD),
                                         [d, back_marks[k // 4]])
                else:
                    y_marks[k] = tt(Y[:, k, :], Y[:, k, :], XR[:, k, :], ADD, [d, back_marks[k // 4]])
            tmp["chain"] = d




    m_h_read_ = [m_h_read]
    gcol = {}

    def need_mods(name, nb):
        while (name, nb) not in mod_done:
            next(mods)
        return mod_done[(name, nb)]

    m = need_mods("ev", 23)
    m_gate0 = tt(MOD[:, 0, 32:48], MOD[:, 0, 32:48], COL[:, 64:80], MUL, [m])
    project_out(True, lambda k: MOD[:, 0, 32 + k:33 + k], lambda: m_gate0, lambda: [buf["pt"]])

    def next_layer(layer, gain, after_x):
        pairs = [SQ2, [TM, TT_]]
        free = [list(tmp["sq"]), [tmp["chain"], tmp["chain"]]]
        for k in range(0, KT, 2):
            s = k // 2 % 2
            a, b = pairs[s]
            for later in ([0, 2] if k == 0 else [k + 2] if k + 2 < KT else []):
                update_x(later)
            marks = y_marks
            a1 = af(a[:, :], Y[:, k, :], ACT.Square, [marks[k], free[s][0]])
            a2 = af(b[:, :], Y[:, k + 1, :], ACT.Square, [marks[k + 1], free[s][1]])
            d = tt(a[:, :], a[:, :], b[:, :], ADD, [a2])
            m_s = mm(OB[:, :], ONE[:, :], a[:, :], k == 0, k == KT - 2, [d, tmp["ob"]], sig=True)
            free[s] = [m_s, m_s]
        tmp["sq"] = [m_s, m_s]
        tmp["chain"] = m_s
        sp_ = pool.dma(XS.ap(), Y[:, :, :], s_spill, y_marks + [(b.sem, b.n) for b in s_back])
        m1, y_ = rstd(SEQ, OB[:, :], m_s, D)
        tmp["ob"] = m1
        g = stt(MOD[:, layer, 16:32], MOD[:, layer, 16:32], 1.0, gain, ADD, MUL, [after_x])
        ready = [None] * KT
        last = []

        def tile(k):
            if k < KT:
                s = k % 2
                d = scaled[k] = stt(SQ2[s][:, :], Y[:, k, :], MOD[:, layer, 16 + k:17 + k], TY[:, :], MUL, MUL,
                                    [y_, g, tmp["sq"][s]])
                rounded[k] = act.do(lambda e: e.activation(HHI[:, k, :], SQ2[s][:, :], ACT.Identity,
                                                           bias=MOD[:, layer, k:k + 1]), [d, m_h_read_[0]])
            if k > 0:
                j = k - 1
                d = stt(HLO[:, j, :], SQ2[j % 2][:, :], MOD[:, layer, j:j + 1], f(HHI[:, j, :]), ADD, SUB,
                        [rounded[j]])
                tmp["sq"][j % 2] = d
                ready[j] = [d]
                m_h[0] = tmp["chain"] = d

        scaled, rounded = {}, {}

        def rest():
            for k in range(5, KT + 1):
                tile(k)
                yield

        for k in range(5):
            tile(k)
        background.append(rest())
        return sp_, ready

    m_h = [None]

    m = need_mods("od", 15)
    m_spill, h_ready = next_layer(1, COL[:, 80:96], m)

    pad = [pool.do(lambda e, i=i: e.memset(UP[i][:, :, :], 0.0), y_marks) for i in range(3)]
    up_free = [None]
    ph_free = [None]
    pooled = [None]
    m_scr = y_marks[KT - 1]
    n_rc = [None]

    def pool_group(g, ev):
        rc = pool.dma(RC[:, :], T["t_rcnt"][g], s_rc, [n_rc[0], m_scr])
        cur = 0
        lo_, hi_ = 1, 544
        d = tt(UP[1][:, :, 1:544], UP[0][:, :, 0:543], UP[0][:, :, 1:544], ADD, ev + [up_free[0]])
        cur = 1
        yield
        yield
        sh = 1
        for lv in range(g):
            nxt = 2 if cur == 1 else 1
            a, b = lo_ + sh, hi_ - sh
            d = pool.do(lambda e, n_=nxt, c_=cur, a=a, b=b, sh=sh: e.tensor_tensor(
                UP[n_][:, :, a:b], UP[c_][:, :, a - sh:b - sh], UP[c_][:, :, a + sh:b + sh], ADD), [d])
            lo_, hi_ = a, b
            sh *= 2
            cur = nxt
            for _ in range(4):
                yield
        o = 2 if cur == 1 else 1
        dst = UP[o][:, :, 16:528]
        for j in range(4):
            d = tt(dst[:, j, :], UP[cur][:, j, 16:528], RC[:, :], MUL, [d, rc])
        n_rc[0] = d
        d = tt(dst, dst, UP[0][:, :, 16:528], SUB, [d])
        for _ in range(5):
            yield
        for j in range(4):
            a = acopy(PHI[:, j, :], dst[:, j, :], [d, ph_free[0]])
            b = tt(PLO[:, j, :], dst[:, j, :], f(PHI[:, j, :]), SUB, [a])
            if j % 2:
                yield
        d = b
        up_free[0] = d
        pooled[0] = d
        yield

    for g in range(4):
        ev = []
        for u in range(2):
            pair, banks, done = gemm(HHI, HLO, h_ready)
            for nt in range(2):
                a = acopy(UP[0][:, 2 * u + nt, 16:528], banks[nt][:, :], [done[nt], pad[2], up_free[0]])
                bank_free[pair][nt] = a
                ev.append(a)
        task = pool_group(g, [ev[-1]])
        background.append(task)
        for u in range(2):
            pair, banks, done = gemm(HHI, HLO, h_ready)
            silu(4 * g + 2 * u, pair, banks, done, [m_spill, m_h[0]], lambda k: COL[:, 128 + k:129 + k])
        m_h_read_[0] = done[1]
        finish(task)
        for u in range(2):
            pair, banks, done = gemm(PHI, PLO, [[pooled[0]]] * 4)
            for nt in range(2):
                k = 4 * g + 2 * u + nt
                gated(0)
                gated(1)
                d = tt(Y[:, k, :], banks[nt][:, :], Y[:, k, :], MUL, [done[nt], z_marks[k]])
                bank_free[pair][nt] = d
                y_marks[k] = d
        ph_free[0] = done[1]

    m = need_mods("od", 23)
    m_gate1 = tt(MOD[:, 1, 32:48], MOD[:, 1, 32:48], COL[:, 96:112], MUL, [m])
    project_out(True, lambda k: MOD[:, 1, 32 + k:33 + k], lambda: m_gate1, lambda: [ph_free[0], up_free[0]])
    m = need_mods("w2", 15)
    m_spill, h_ready = next_layer(2, COL[:, 112:128], m)

    m_rope = pool.dma(CS[:, :], T["t_rope_b"][0], s_rope, [y_marks[0]])
    m_rope = pool.dma(SN[:, :], T["t_rope_b"][1], s_rope)
    m_rp[0] = m_rope
    m_tri = pool.dma(MK[:, :, :], T["t_sb"].rearrange("a p n -> p a n"), s_tri, [y_marks[0]])
    m_scr = y_marks[KT - 1]
    m_sg = ts(COL[:, 154:155], COL[:, 154:155], SCALE, None, MUL, None, [m_col])
    bf = {"q": [m_scr, m_scr], "k": [m_scr, m_scr], "v": [m_scr, m_scr], "ls": [None, None],
          "sp": None, "w": [None, None], "dk": None, "ta": [None, None], "s": [buf["s"], buf["s"]],
          "n": 0, "wn": 0, "sn": 0}
    LS2 = [LS, LSB]
    OFF = {3: 0, 2: 128, 1: 384, 0: 768}
    m_tri = acopy(TRIR[:, :], MK[:, 0, :], [m_tri])
    m_oner = acopy(ONER[:, :], ONE[:, :], [m_scr])

    def stick_z(h, b, i, kt, vm):
        q, k_ = Q2[b][:, i, :], K2[b][:, i, :]
        c0 = kt * P
        n = SEQ - c0
        sb_ = kt % 2
        Z = S[:, sb_ * 512 + c0:sb_ * 512 + 512]
        m = mm(Z, k_[:, c0:c0 + P], q[:, c0:SEQ], True, True, [bf["s"][sb_]] + vm, sig=True)
        ls, spt, ta = LS2[sb_][:, c0:SEQ], TA[1][:, c0:SEQ], TA[0][:, c0:SEQ]
        hi, lo = SPH[:, OFF[kt]:OFF[kt] + n], SPL[:, OFF[kt]:OFF[kt] + n]
        a = af(ta, Z, ACT.Abs, [m, bf["ta"][0], m_scr])
        a = af(ta, ta, ACT.Exp, [a], scale=-1.0)
        a = af(ta, ta, ACT.Ln, [a], bias=1.0)
        d2 = stt(spt, Z, 0.0, ta, MAX, ADD, [a, bf["ta"][1], m_zero])
        d3 = tt(TA[1][:, c0:c0 + P], TA[1][:, c0:c0 + P], MK[:, 1, :], MUL, [d2, m_tri])
        ah = acopy(hi, spt, [d3, bf["sp"]])
        d = stt(ls, Z, 0.0, ta, MIN, SUB, [a, bf["ls"][sb_]])
        bf["s"][sb_] = d
        bf["ta"][0] = d
        d4 = tt(LS2[sb_][:, c0:c0 + P], LS2[sb_][:, c0:c0 + P], MK[:, 2, :], ADD, [d])
        d3 = tt(lo, spt, f(hi), SUB, [ah])
        bf["ta"][1] = d3
        stick[kt] = (d3, d4)

    def stick_w(h, b, i, kt):
        d3, d4 = stick[kt]
        c0 = kt * P
        n = SEQ - c0
        sb_ = kt % 2
        ls = LS2[sb_][:, c0:SEQ]
        C = TB[:, c0:SEQ]
        mm(C, TRIR[:, :], SPH[:, OFF[kt]:OFF[kt] + n], True, False, [d3, tmp["tb"], m_oner])
        mc = mm(C, TRIR[:, :], SPL[:, OFF[kt]:OFF[kt] + n], False, kt == 3, sig=True)
        for k2 in range(kt + 1, 4):
            w = SEQ - k2 * P
            mm(TB[:, k2 * P:SEQ], ONER[:, :], SPH[:, OFF[k2]:OFF[k2] + w], False, False)
            mc = mm(TB[:, k2 * P:SEQ], ONER[:, :], SPL[:, OFF[k2]:OFF[k2] + w], False, k2 == 3, sig=True)
        if kt == 0:
            bf["sp"] = mc
        d = tt(ls, ls, C, SUB, [mc, d4])
        tmp["tb"] = d
        wi = sb_
        if kt == 3:
            z = vset(WB[wi][:, 0:c0], 0.0, [bf["w"][wi], m_scr])
        else:
            z = None
        a = af(WB[wi][:, c0:SEQ], ls, ACT.Exp, [d, bf["w"][wi], z, m_scr])
        bf["ls"][sb_] = a
        stick[kt] = a

    def stick_v(h, b, i, kt, vmk):
        c0 = 0 if kt == 3 else kt * P
        v = V2[b]
        mo = mm(OB[:, c0:SEQ], v[:, kt, i * P:(i + 1) * P], WB[kt % 2][:, c0:SEQ], kt == 3, kt == 0,
                [stick[kt], tmp["ob"], vmk], sig=True)
        bf["w"][kt % 2] = mo
        if kt == 0:
            readers.append(mo)
            tmp["ob"] = tt(Y[:, h, :], OB[:, :], Y[:, h, :], MUL, [mo, z_marks[h]])
            y_marks[h] = tmp["ob"]

    stick = {}

    readers = []
    m_zero = m_scr

    def sb_task(p, b, qm, km, vmk, fin):
        f1 = []
        for i in range(2):
            for _ in norm_rope_plain(Q2[b][:, i, :], COL[:, 154:155], [qm[i]], f1):
                yield
            for _ in norm_rope_plain(K2[b][:, i, :], COL[:, 155:156], [km[i]], f1):
                yield

        def first(plan):
            t = 0
            for i in range(2):
                for kt in (3, 2, 1, 0):
                    plan(t + 6, lambda i=i, kt=kt: stick_v(2 * p + i, b, i, kt, vmk))
                    plan(t + 4, lambda i=i, kt=kt: stick_w(2 * p + i, b, i, kt))
                    t += 4
            t = 0
            for i in range(2):
                for kt in (3, 2, 1, 0):
                    plan(t, lambda i=i, kt=kt: stick_z(2 * p + i, b, i, kt, f1))
                    t += 4

        yield
        for _ in timed_fwd(first):
            yield
        bf["q"][b] = bf["k"][b] = bf["v"][b] = readers[-1]

    def timed_fwd(first):
        events = {}
        first(lambda t, fn: events.setdefault(t, []).append(fn))
        t = 0
        while events:
            for fn in events.pop(t, []):
                fn()
            t += 1
            yield

    def norm_rope_plain(t, gcol_, after, fin):
        a = af(SQ2[1][:, :], t, ACT.Square, list(after) + [tmp["sq"][1]])
        yield
        yield
        m = mm(TB[:, :], ONE[:, :], SQ2[1][:, :], True, True, [a, tmp["tb"]], sig=True)
        tmp["sq"][1] = m
        m_, y = rstd(SEQ, TB[:, :], m, 128)
        tmp["tb"] = m_
        yield
        d = stt(t, t, gcol_, TY[:, :], MUL, MUL, [y])
        tmp["chain"] = d
        fin.append(d)
        yield

    def rope_only(t, after, fin):
        h = 64
        d1 = tt(TT_[h:P, :], t[0:h, :], SN[0:h, :], MUL, [tmp["chain"], m_rp[0]] + list(after))
        d2 = tt(TT_[0:h, :], t[h:P, :], SN[h:P, :], MUL, [d1])
        yield
        d3 = tt(t, t, CS[:, :], MUL, [d2])
        d4 = tt(t, t, TT_[:, :], ADD, [d3])
        tmp["chain"] = d4
        fin.append(d4)
        yield
        yield

    def ret_z(h, b, i, kt, vm, dk):
        c0 = kt * P
        sb_ = kt % 2
        Z = S[:, sb_ * 512 + c0:sb_ * 512 + 512]
        m = mm(Z, K2[b][:, i, c0:c0 + P], Q2[b][:, i, c0:SEQ], True, True, [bf["s"][sb_]] + vm, sig=True)
        d = tt(WB[sb_][:, c0:SEQ], Z, DK[:, 0:SEQ - c0], MUL, [m, dk, bf["w"][sb_]])
        bf["s"][sb_] = d
        stick[kt] = d
        if kt == 3:
            bf["dk"] = d

    def ret_v(h, b, i, kt, vmk):
        c0 = kt * P
        mo = mm(OB[:, c0:SEQ], V2[b][:, kt, i * P:(i + 1) * P], WB[kt % 2][:, c0:SEQ], kt == 0, kt == 3,
                [stick[kt], tmp["ob"], vmk], sig=True)
        bf["w"][kt % 2] = mo
        if kt == 3:
            readers.append(mo)
            stick["o"] = acopy(LS[:, :], OB[:, :], [mo, bf["ls"][0]])
            tmp["ob"] = stick["o"]

    def ret_mean():
        m = mm(TB[:, :], ONE[:, :], LS[:, :], True, True, [stick["o"], tmp["tb"]], sig=True)
        d = stt(LS[:, :], TB[:, :], -1.0 / 128, LS[:, :], MUL, ADD, [m])
        tmp["tb"] = d
        stick["c"] = af(SQ2[1][:, :], LS[:, :], ACT.Square, [d, tmp["sq"][1]])

    def ret_norm(h):
        m = mm(TB[:, :], ONE[:, :], SQ2[1][:, :], True, True, [stick["c"], tmp["tb"]], sig=True)
        tmp["sq"][1] = m
        m_, y = rstd(SEQ, TB[:, :], m, 128)
        tmp["tb"] = m_
        d = stt(LS[:, :], LS[:, :], COL[:, 144 + h:145 + h], TY[:, :], MUL, MUL, [y])
        tmp["chain"] = d
        d = tt(Y[:, 8 + h, :], LS[:, :], Y[:, 8 + h, :], MUL, [d, z_marks[8 + h]])
        bf["ls"][0] = d
        y_marks[8 + h] = d

    def ret_task(p, b, qm, km, vmk):
        f1 = []
        dks = {}

        def load(h):
            dks[h] = pool.dma(DK[:, :], T["t_decay"][h], s_dk, [bf["dk"] or readers[-1]])

        load(2 * p)
        for i in range(2):
            for _ in rope_only(Q2[b][:, i, :], [qm[i]], f1):
                yield
            for _ in rope_only(K2[b][:, i, :], [km[i]], f1):
                yield
        yield
        yield

        def first(plan):
            for i in range(2):
                h, t = 2 * p + i, 20 * i
                for kt in range(4):
                    plan(t + 2 * kt + 3, lambda h=h, i=i, kt=kt: ret_v(h, b, i, kt, vmk))
                for kt in range(4):
                    plan(t + 2 * kt, lambda h=h, i=i, kt=kt: ret_z(h, b, i, kt, f1, dks[h]))
                if i == 0:
                    plan(t + 7, lambda h=h: load(h + 1))
                plan(t + 12, ret_mean)
                plan(t + 15, lambda h=h: ret_norm(h))

        for _ in timed_fwd(first):
            yield
        bf["q"][b] = bf["k"][b] = bf["v"][b] = readers[-1]

    x_tiles = [(lambda k, i=i: HHI[:, k, i * P:(i + 1) * P], lambda k, i=i: HLO[:, k, i * P:(i + 1) * P], h_ready)
               for i in range(4)]
    task = None
    for n in range(8):
        b = n % 2
        sides = []
        for what, dst in (("q", Q2[b]), ("k", K2[b])):
            pair, banks, done = gemm(HHI, HLO, h_ready)
            ms = []
            for nt in range(2):
                a = acopy(dst[:, nt, :], banks[nt][:, :], [done[nt], bf[what][b]])
                bank_free[pair][nt] = a
                ms.append(a)
            sides.append(ms)
        pair = at["pair"] % 2
        gated(pair)
        outs2 = [G[pair][i // 2][:, (i % 2) * 256:(i % 2) * 256 + 256] for i in range(4)]
        done = gemm_tok(x_tiles, lambda i, outs2=outs2: outs2[i], [bank_free[pair][0], bank_free[pair][1]])
        for i in range(2):
            a = acopy(V2[b][:, 2 * i:2 * i + 2, :], G[pair][i][:, :].rearrange("p (t n) -> p t n", t=2),
                      [done, bf["v"][b]])
            bank_free[pair][i] = a
        vmk = a
        pair, banks, done = gemm(HHI, HLO, h_ready)
        silu(2 * n, pair, banks, done, [m_spill, m_h[0]])
        if task is not None:
            finish(task)
        if n < 4:
            task = sb_task(n, b, sides[0], sides[1], vmk, None)
        else:
            task = ret_task(n - 4, b, sides[0], sides[1], vmk)
        background.append(task)
    m_h_read_[0] = done[1]
    m = need_mods("w2", 23)
    project_out(False, lambda k: MOD[:, 2, 32 + k:33 + k], lambda: m, lambda: [readers[-1], y_marks[KT - 1]])

    run(write_out(3, []))
    emit_all()


def chain(gens):
    for g in gens:
        for _ in g:
            yield


def norm_rope_copy(norm_rope, KTA, kh, SQ2, tmp, a, marks, vcopy):
    for _ in norm_rope(KTA[:, kh, 0:SEQ], KTA[:, kh, 0:SEQ], SEQ, None, True, [a], marks):
        yield


def tables():
    import numpy as np
    f4 = np.float32
    i = np.arange(P)
    sq = np.stack([np.eye(P), np.ones((P, P))]).astype(f4)
    low = np.where(i[None, :] >= i[:, None], 0.0, -1e30)
    high = np.where(i[None, :] <= i[:, None], 0.0, -1e30)
    mask = np.stack([low, high]).astype(f4)
    tri = (i[:, None] > i[None, :]).astype(f4)
    past = (i[:, None] < i[None, :]).astype(f4)
    sb = np.stack([tri, past, np.where(past > 0, 0.0, -1e30)]).astype(f4)

    def rope(ang):
        c, s = np.cos(ang).T, np.sin(ang).T
        return np.stack([np.concatenate([c, c]), np.concatenate([s, -s])]).astype(f4)

    t = np.arange(SEQ)
    inv = (10000.0 ** (-np.arange(32) / 32.0)).astype(f4)
    ang = np.concatenate([(t // 64).astype(f4)[:, None] * inv, (t % 64).astype(f4)[:, None] * inv], axis=1)
    inv2 = (10000.0 ** (-np.arange(64) / 64.0)).astype(f4)
    ang2 = t.astype(f4)[:, None] * inv2
    rc = np.stack([1.0 / (np.clip(t + w // 2, 0, SEQ) - np.clip(t - w // 2, 0, SEQ)) for w in (2, 4, 8, 16)])
    rc = np.ascontiguousarray(np.broadcast_to(rc[:, None, :], (4, P, SEQ))).astype(f4)
    g = np.log1p(-np.exp2(-5.0 - np.arange(8)))
    rel = t[None, :] - i[:, None]
    dec = np.where(rel[None] >= 0, np.exp(np.maximum(rel, 0)[None] * g[:, None, None]), 0.0) * SCALE
    r4 = np.array([[1, 0], [0, 1], [1, 0], [0, 1]], f4)
    return {"t_r4": r4, "t_sq": sq, "t_mask": mask, "t_sb": sb, "t_rope_a": rope(ang.astype(np.float64)),
            "t_rope_b": rope(ang2.astype(np.float64)), "t_rcnt": rc, "t_decay": dec.astype(f4)}


def kernel(**inputs):
    import numpy as np
    import concourse.bacc as bacc
    from concourse.bass_utils import run_bass_kernel_spmd as run

    nc = bacc.Bacc("TRN2", target_bir_lowering=False, num_devices=1)
    arrays, T = {}, {}
    const = tables()
    for name in INPUTS + TABLES:
        a = np.ascontiguousarray(const[name] if name in const else inputs[name])
        arrays[f"in_{name}"] = a
        T[name] = nc.dram_tensor(f"in_{name}", a.shape, F32, kind="ExternalInput").ap()
    out = nc.dram_tensor("out_x", (1, SEQ, D), F32, kind="ExternalOutput").ap()
    program(nc, T, out)
    r = run(nc, [arrays], core_ids=[0])
    return r.results[0]["out_x"]
```
